# Optimizing a Trainium2 kernel written in Bass

```python
import jax, jax.numpy as jnp
from jax import lax
import numpy as np

D_MODEL = 1024
BATCH = 1
SEQ = 512
DEPTH = 1
DEC_BATCH = 1
DEC_SEQ = 512
PAST_LEN = 128

GRID_W = 64
HA = 4
DK_A = 128
DV_A = 128
CONV_K = 5
CHUNK = 64
HB = 8
DH_B = 64
WIN_ROWS = 8
WIN_COLS = 16
N_EXPERTS = 16
EC_FACTOR = 2
D_EXPERT = 2048
RMS_EPS = 1e-6
N_MOD = 6

A_QKV_W = HA * DK_A * 2 + HA * DV_A
A_Z_W = HA * DV_A
A_W = HA * DV_A
B_W = HB * DH_B
IN_WIDTHS = (A_QKV_W, A_Z_W, 2 * HA, 2 * HA, B_W, B_W, B_W, D_MODEL, D_MODEL)
IN_WIDTH = sum(IN_WIDTHS)

kernel_name = "hybrid_deltanet_natten_ec_moe_encoder"

def _rmsnorm(x, g):
    xf = x.astype(jnp.float32)
    y = xf * lax.rsqrt(jnp.mean(xf * xf, axis=-1, keepdims=True) + RMS_EPS)
    return (y * g.astype(jnp.float32)).astype(x.dtype)

def _l2norm(x):
    xf = x.astype(jnp.float32)
    return xf * lax.rsqrt(jnp.sum(xf * xf, axis=-1, keepdims=True) + 1e-6)

def _centred_dwconv(x, w):
    C = x.shape[-1]
    return lax.conv_general_dilated(
        x, w[:, None, :].astype(x.dtype), window_strides=(1,),
        padding=[(CONV_K // 2, CONV_K // 2)],
        dimension_numbers=("NWC", "WIO", "NWC"), feature_group_count=C)

def _gated_delta_chunked(q, k, v, g, beta):
    Bx, L, H, DK = q.shape
    DV = v.shape[-1]
    n = L // CHUNK

    def chunks(t):
        return t.reshape(Bx, n, CHUNK, H, t.shape[-1]).transpose(1, 0, 3, 2, 4)

    qc, kc, vc = chunks(q), chunks(k), chunks(v)
    gc = jnp.cumsum(g.reshape(Bx, n, CHUNK, H).transpose(1, 0, 3, 2), axis=-1)
    bc = beta.reshape(Bx, n, CHUNK, H).transpose(1, 0, 3, 2)
    incl = jnp.tril(jnp.ones((CHUNK, CHUNK), dtype=bool))
    strict = jnp.tril(jnp.ones((CHUNK, CHUNK), dtype=bool), -1)
    diff = gc[..., :, None] - gc[..., None, :]
    decay = jnp.where(incl, jnp.exp(jnp.where(incl, diff, 0.0)), 0.0)
    kk = jnp.einsum("nbhid,nbhjd->nbhij", kc, kc)
    lower = jnp.where(strict, bc[..., :, None] * kk * decay, 0.0)
    rhs = jnp.concatenate([vc * bc[..., None], kc * (bc * jnp.exp(gc))[..., None]], axis=-1)
    sol = lax.linalg.triangular_solve(lower + jnp.eye(CHUNK, dtype=lower.dtype), rhs,
                                      left_side=True, lower=True, unit_diagonal=True)
    u, w = sol[..., :DV], sol[..., DV:]
    qk = jnp.einsum("nbhid,nbhjd->nbhij", qc, kc) * decay

    def step(S, xs):
        q_i, k_i, u_i, w_i, qk_i, g_i = xs
        v_new = u_i - jnp.einsum("bhck,bhkv->bhcv", w_i, S)
        o = (jnp.einsum("bhck,bhkv->bhcv", q_i * jnp.exp(g_i)[..., None], S)
             + jnp.einsum("bhij,bhjv->bhiv", qk_i, v_new))
        g_last = g_i[..., -1:]
        S = (S * jnp.exp(g_last)[..., None]
             + jnp.einsum("bhck,bhcv->bhkv", k_i * jnp.exp(g_last - g_i)[..., None], v_new))
        return S, o

    S0 = jnp.zeros((Bx, H, DK, DV), jnp.float32)
    _, o = lax.scan(step, S0, (qc, kc, u, w, qk, gc))
    return o.transpose(1, 0, 3, 2, 4).reshape(Bx, L, H, DV)

def _deltanet_branch(qkv, z, beta_logit, alpha, a_log, dt_bias, conv_w, gn_w):
    Bx, L, _ = qkv.shape
    qkv = jax.nn.silu(_centred_dwconv(qkv, conv_w))
    q, k, v = jnp.split(qkv, [HA * DK_A, 2 * HA * DK_A], axis=-1)
    q = _l2norm(q.reshape(Bx, L, HA, DK_A)) * (DK_A ** -0.5)
    k = _l2norm(k.reshape(Bx, L, HA, DK_A))
    v = v.reshape(Bx, L, HA, DV_A).astype(jnp.float32)
    beta = jax.nn.sigmoid(beta_logit.astype(jnp.float32)).reshape(Bx, L, 2, HA)
    g = -jnp.exp(a_log.astype(jnp.float32)) * jax.nn.softplus(
        alpha.astype(jnp.float32).reshape(Bx, L, 2, HA) + dt_bias.astype(jnp.float32))
    flip = lambda t: jnp.flip(t, axis=1)
    o_f = _gated_delta_chunked(q, k, v, g[:, :, 0], beta[:, :, 0])
    o_b = flip(_gated_delta_chunked(flip(q), flip(k), flip(v), flip(g[:, :, 1]), flip(beta[:, :, 1])))
    o = o_f + o_b
    o = (o * lax.rsqrt(jnp.mean(o * o, axis=-1, keepdims=True) + RMS_EPS) * gn_w.astype(jnp.float32)
         * jax.nn.silu(z.astype(jnp.float32).reshape(Bx, L, HA, DV_A)))
    return o.reshape(Bx, L, A_W).astype(qkv.dtype)

def _neighbourhood_attention(q, k, v, rpb):
    Bx, L, _ = q.shape
    rows = L // GRID_W
    wr = min(WIN_ROWS, rows)
    shp = (Bx, rows, GRID_W, HB, DH_B)
    qg = q.reshape(shp) * (DH_B ** -0.5)
    kg = k.reshape(shp)
    vg = v.reshape(shp)
    cols = jnp.arange(GRID_W)
    col_idx = jnp.clip(cols - WIN_COLS // 2, 0, GRID_W - WIN_COLS)[:, None] + jnp.arange(WIN_COLS)
    col_off = col_idx - cols[:, None] + (WIN_COLS - 1)

    def row_block(i):
        r0 = jnp.clip(i - wr // 2, 0, rows - wr)
        kb = lax.dynamic_slice_in_dim(kg, r0, wr, axis=1)[:, :, col_idx]
        vb = lax.dynamic_slice_in_dim(vg, r0, wr, axis=1)[:, :, col_idx]
        qi = lax.dynamic_index_in_dim(qg, i, axis=1, keepdims=False)
        s = jnp.einsum("bjhd,brjchd->bhjrc", qi, kb).astype(jnp.float32)
        row_off = r0 + jnp.arange(wr) - i + (WIN_ROWS - 1)
        bias = rpb[:, row_off][:, :, col_off]
        s = s + jnp.transpose(bias, (0, 2, 1, 3)).astype(jnp.float32)[None]
        p = jax.nn.softmax(s.reshape(Bx, HB, GRID_W, wr * WIN_COLS), axis=-1).reshape(s.shape)
        return jnp.einsum("bhjrc,brjchd->bjhd", p.astype(vb.dtype), vb)

    o = lax.map(row_block, jnp.arange(rows))
    return jnp.transpose(o, (1, 0, 2, 3, 4)).reshape(Bx, L, B_W)

def _mixer(h, w_in, conv_w, a_log, dt_bias, gn_w, rpb, w_oa, w_ob, w_out):
    proj = h @ w_in
    split_points = np.cumsum(IN_WIDTHS)[:-1].tolist()
    qkv_a, z_a, beta_a, alpha_a, q_b, k_b, v_b, gate_a, gate_b = jnp.split(proj, split_points, axis=-1)
    o_a = _deltanet_branch(qkv_a, z_a, beta_a, alpha_a, a_log, dt_bias, conv_w, gn_w)
    o_b = _neighbourhood_attention(q_b, k_b, v_b, rpb)
    merged = jax.nn.sigmoid(gate_a) * (o_a @ w_oa) + jax.nn.sigmoid(gate_b) * (o_b @ w_ob)
    return merged @ w_out

def _expert_choice_moe(h, w_router, w_gate, w_up, w_down):
    Bx, L, D = h.shape
    T = Bx * L
    cap = EC_FACTOR * T // N_EXPERTS
    ht = h.reshape(T, D)
    probs = jax.nn.softmax((ht @ w_router).astype(jnp.float32), axis=-1)
    gates, idx = lax.top_k(probs.T, cap)

    def expert(args):
        idx_e, gate_e, wg, wu, wd = args
        xe = ht[idx_e]
        he = jax.nn.silu(xe @ wg) * (xe @ wu)
        return (he @ wd) * gate_e[:, None].astype(xe.dtype)

    ye = lax.map(expert, (idx, gates, w_gate, w_up, w_down))
    y = jnp.zeros_like(ht).at[idx.reshape(-1)].add(ye.reshape(-1, D))
    return y.reshape(Bx, L, D)

def _layer(x, c, w_ada, b_ada, norm1_g, w_in, conv_w, a_log, dt_bias, gn_w, rpb,
           w_oa, w_ob, w_out, norm2_g, w_router, w_gate, w_up, w_down):
    mod = (jax.nn.silu(c) @ w_ada + b_ada)[:, None, :]
    shift1, scale1, gate1, shift2, scale2, gate2 = jnp.split(mod, N_MOD, axis=-1)
    h = _rmsnorm(x, norm1_g) * (1 + scale1) + shift1
    x = x + gate1 * _mixer(h, w_in, conv_w, a_log, dt_bias, gn_w, rpb, w_oa, w_ob, w_out)
    h = _rmsnorm(x, norm2_g) * (1 + scale2) + shift2
    x = x + gate2 * _expert_choice_moe(h, w_router, w_gate, w_up, w_down)
    return x

def setup_inputs(seed: int = 0) -> dict:
    key = jax.random.key(seed)
    ks = jax.random.split(key, 24)
    nrm = lambda k, shp, s: jax.random.normal(k, shp, jnp.float32) * s
    dt = jnp.exp(jax.random.uniform(ks[10], (DEPTH, 2, HA), jnp.float32,
                                    minval=float(np.log(1e-3)), maxval=float(np.log(1e-1))))
    return {
        "x_prompt": nrm(ks[0], (BATCH, SEQ, D_MODEL), 1.0),
        "x_sample": nrm(ks[1], (DEC_BATCH, DEC_SEQ, D_MODEL), 1.0),
        "c_prompt": nrm(ks[2], (BATCH, D_MODEL), 1.0),
        "c_sample": nrm(ks[3], (DEC_BATCH, D_MODEL), 1.0),
        "w_ada": nrm(ks[4], (DEPTH, D_MODEL, N_MOD * D_MODEL), D_MODEL ** -0.5),
        "b_ada": nrm(ks[5], (DEPTH, N_MOD * D_MODEL), 0.02),
        "norm1_g": 1.0 + nrm(ks[6], (DEPTH, D_MODEL), 0.02),
        "w_in": nrm(ks[7], (DEPTH, D_MODEL, IN_WIDTH), D_MODEL ** -0.5),
        "conv_w": nrm(ks[8], (DEPTH, CONV_K, A_QKV_W), CONV_K ** -0.5),
        "a_log": jnp.log(jax.random.uniform(ks[9], (DEPTH, 2, HA), jnp.float32, minval=1.0, maxval=16.0)),
        "dt_bias": dt + jnp.log(-jnp.expm1(-dt)),
        "gn_w": 1.0 + nrm(ks[11], (DEPTH, DV_A), 0.02),
        "rpb": nrm(ks[12], (DEPTH, HB, 2 * WIN_ROWS - 1, 2 * WIN_COLS - 1), 0.02),
        "w_oa": nrm(ks[13], (DEPTH, A_W, D_MODEL), A_W ** -0.5),
        "w_ob": nrm(ks[14], (DEPTH, B_W, D_MODEL), B_W ** -0.5),
        "w_out": nrm(ks[15], (DEPTH, D_MODEL, D_MODEL), D_MODEL ** -0.5),
        "norm2_g": 1.0 + nrm(ks[16], (DEPTH, D_MODEL), 0.02),
        "w_router": nrm(ks[17], (DEPTH, D_MODEL, N_EXPERTS), D_MODEL ** -0.5),
        "w_gate": nrm(ks[18], (DEPTH, N_EXPERTS, D_MODEL, D_EXPERT), D_MODEL ** -0.5),
        "w_up": nrm(ks[19], (DEPTH, N_EXPERTS, D_MODEL, D_EXPERT), D_MODEL ** -0.5),
        "w_down": nrm(ks[20], (DEPTH, N_EXPERTS, D_EXPERT, D_MODEL), D_EXPERT ** -0.5),
        "final_g": 1.0 + nrm(ks[21], (D_MODEL,), 0.02),
    }

def reference(x_prompt, x_sample, c_prompt, c_sample, w_ada, b_ada, norm1_g, w_in, conv_w, a_log,
              dt_bias, gn_w, rpb, w_oa, w_ob, w_out, norm2_g, w_router, w_gate, w_up, w_down, final_g):
    def trunk(x, c):
        for l in range(DEPTH):
            x = _layer(x, c, w_ada[l], b_ada[l], norm1_g[l], w_in[l], conv_w[l], a_log[l], dt_bias[l],
                       gn_w[l], rpb[l], w_oa[l], w_ob[l], w_out[l], norm2_g[l], w_router[l],
                       w_gate[l], w_up[l], w_down[l])
        return _rmsnorm(x, final_g)

    y_prompt = trunk(x_prompt, c_prompt)
    y_sample = trunk(x_sample, c_sample)
    return (y_prompt, y_sample)


_drawn_inputs = setup_inputs


def setup_inputs(seed=0):
    import zlib

    import numpy as np

    out = dict(_drawn_inputs(seed))
    spreads = {}
    factors = {'norm1_g': 3.298, 'gn_w': 4.468, 'rpb': 7.283, 'norm2_g': 2.814, 'final_g': 2.756}
    for name, (base, spread) in spreads.items():
        noise = np.random.default_rng([zlib.crc32(name.encode()), seed]).standard_normal(out[name].shape)
        drawn = base * np.exp(spread * noise) if base else spread * noise
        out[name] = __import__('jax').numpy.asarray(drawn.astype(out[name].dtype))
    for name, factor in factors.items():
        out[name] = (out[name] * factor).astype(out[name].dtype)
    return out
```

```python
from contextlib import ExitStack

import concourse.bass as bass
from concourse import mybir

F32 = mybir.dt.float32
U32 = mybir.dt.uint32
ALU = mybir.AluOpType
ACT = mybir.ActivationFunctionType
AX_X = mybir.AxisListType.X

P = 128
D_MODEL = 1024
SEQ = 512
GROUPS = 2
TOK = GROUPS * SEQ
KD = D_MODEL // P
TPG = SEQ // P
NT = TOK // P
GRID_W = 64
ROWS = SEQ // GRID_W
HA = 4
DK = 128
CONV_K = 5
CHUNK = 64
NCHUNK = SEQ // CHUNK
HB = 8
DH = 64
PAIRS = HB * DH // P
WIN_ROWS = 8
WIN_COLS = 16
NE = 16
CAP = 2 * SEQ // NE
D_EXPERT = 2048
EPS = 1e-6
BIG = 1e30
A_W = HA * DK
OFF_Z = 3 * A_W
OFF_SMALL = 4 * A_W
OFF_QB = OFF_SMALL + 4 * HA
OFF_GA = OFF_QB + 3 * HB * DH
OFF_GB = OFF_GA + D_MODEL
ADA_BLOCK = 512
ADA_FIRST = 2 * D_MODEL // ADA_BLOCK
ADA_TILES = ADA_BLOCK // P
BETA, CUM, ECUM, BECUM, EREST, LOGD, ETOT = range(7)
NQ = 8
VB, VN1, VN2, VC = 0, 48, 56, 64
VROWS = 80
CROWS = 12 * CONV_K + 1
LEVELS = 6
WCOLS = 48
RPB_C = 2 * WIN_COLS - 1
RPB_R = 2 * WIN_ROWS - 1
RPB_FRONT = 15 * RPB_R + 7 + 8
RPB_RUN = WCOLS * RPB_R
RPB_LEN = RPB_FRONT + RPB_RUN
KEY_TILES = [(0, 2), (0, 3), (1, 4), (2, 4)]


class Steps:

    def __init__(self, eng, sem, before=0):
        self.eng, self.sem, self.before, self.n = eng, sem, before, 0

    def did(self, ins):
        ins.then_inc(self.sem, 1)
        self.n += 1

    def settle(self):
        self.eng.wait_ge(self.sem, self.before + self.n)

    def do(self, ins):
        self.did(ins)
        self.settle()


def bcast(ap, axis, n):
    ap = ap.unsqueeze(axis)
    shape = list(ap.shape)
    shape[axis] = n
    return ap.to_broadcast(shape)


def shared_buffers(nc, ctx):
    def sb(name, shape, dt=F32):
        return ctx.enter_context(nc.sbuf_tensor(name, shape, dt))

    m = {}
    m["ones"] = sb("ones", [P, P])
    m["upto"] = sb("upto", [P, 2, P])
    m["vecT"] = sb("vecT", [P, VROWS])
    m["convT"] = sb("convT", [P, CROWS])
    m["modT"] = sb("modT", [P, 48, GROUPS])
    m["sc"] = sb("sc", [P, KD, GROUPS])
    m["hT"] = sb("hT", [P, KD, TOK])
    m["oaT"] = sb("oaT", [P, HA, TOK])
    m["obT"] = sb("obT", [P, PAIRS, TOK])
    m["tab"] = sb("tab", [P, NQ, NT, 2 * HA])
    return m


def phase_prepare(nc, a, m, ps):
    with ExitStack() as ctx:
        def sb(name, shape, dt=F32):
            return ctx.enter_context(nc.sbuf_tensor(name, shape, dt))

        def sem(name):
            return ctx.enter_context(nc.semaphore(name))

        rows = sb("rows", [VROWS, P])
        crows = sb("crows", [CROWS, P])
        ada = sb("ada", [P, ADA_FIRST, KD, ADA_BLOCK])
        xt = sb("xt", [P, NT, D_MODEL])
        junk = sb("junk", [P, D_MODEL])
        wsm = sb("wsm", [P, KD, 4 * HA])
        alog = sb("alog", [P, 2 * HA])
        dtb = sb("dtb", [P, 2 * HA])
        ealog = sb("ealog", [P, 2 * HA])
        ssq = sb("ssq", [P, NT])
        ms = sb("ms", [P, NT])
        rinv = sb("rinv", [P, NT])
        mul1 = sb("mul1", [P, KD, GROUPS])
        al = sb("al", [P, NT, 2 * HA])
        nal = sb("nal", [P, NT, 2 * HA])
        sp1 = sb("sp1", [P, NT, 2 * HA])
        eb = sb("eb", [P, NT, 2 * HA])
        rest = sb("rest", [P, NT, 2 * HA])
        same = sb("same", [P, P])
        half = sb("half", [P, 2, P])
        tab = m["tab"]

        vec_in = sem("vec_in")
        ada_in = [sem(f"ada_in{i}") for i in range(ADA_FIRST)]
        x_in = [sem(f"x_in{g}") for g in range(GROUPS)]
        small_in = sem("small_in")
        pool_step = sem("pool_step_a")
        dve_step = sem("dve_step_a")
        consts = sem("consts")
        vec_ps = sem("vec_ps")
        vec_sb = sem("vec_sb")
        mod_ps = sem("mod_ps")
        mul_ready = sem("mul_ready")
        ssq_done = sem("ssq_done")
        ms_done = sem("ms_done")
        rinv_done = sem("rinv_done")
        xn_done = sem("xn_done")
        xT_ps = sem("xT_ps")
        hT_act = sem("hT_act")
        hT_dve = sem("hT_dve")
        small_ps = sem("small_ps")
        al_done = sem("al_done")
        nal_done = sem("nal_done")
        act_step = sem("act_step_a")
        logd_done = sem("logd_done")
        cum_ps = sem("cum_ps")
        cum_sb = sem("cum_sb")

        with nc.Block() as block:

            @block.sync
            def _(sp):
                for dst, src in (
                    (rows[VB:VB + 48, :], a["b_ada"].rearrange("a (r c) -> (a r) c", c=P)),
                    (rows[VN1:VN1 + 8, :], a["norm1_g"].rearrange("a (r c) -> (a r) c", c=P)),
                    (rows[VN2:VN2 + 8, :], a["norm2_g"].rearrange("a (r c) -> (a r) c", c=P)),
                    (rows[VC:VC + 16, :], a["c"].rearrange("a (r c) -> (a r) c", c=P)),
                    (crows[0:60, :], a["conv_w"].rearrange("a t (r c) -> (a t r) c", c=P)),
                    (crows[60:61, :], a["gn_w"]),
                ):
                    sp.dma_start(dst, src).then_inc(vec_in, 16)
                x_v = a["x"].rearrange("(t p) c -> p t c", p=P)
                w_ada = a["w_ada"].rearrange("a (k p) n -> p (a k) n", p=P)
                for g in range(GROUPS):
                    sp.dma_start(xt[:, g * TPG:(g + 1) * TPG, :], x_v[:, g * TPG:(g + 1) * TPG, :]).then_inc(x_in[g], 16)
                    for b in (2 * g, 2 * g + 1):
                        sp.dma_start(ada[:, b, :, :], w_ada[:, :, b * ADA_BLOCK:(b + 1) * ADA_BLOCK]).then_inc(ada_in[b], 16)
                w_in = a["w_in"].rearrange("a (k p) n -> p (a k) n", p=P)
                sp.dma_start(wsm[:, :, :], w_in[:, :, OFF_SMALL:OFF_SMALL + 4 * HA]).then_inc(small_in, 16)
                sp.dma_start(alog[:, :], bass.AP(a["a_log"].tensor, 0, [[0, P], [1, 2 * HA]])).then_inc(small_in, 16)
                sp.dma_start(dtb[:, :], bass.AP(a["dt_bias"].tensor, 0, [[0, P], [1, 2 * HA]])).then_inc(small_in, 16)

            @block.gpsimd
            def _(pool):
                st = Steps(pool, pool_step)
                st.did(pool.memset(m["ident"][:, :], 0.0))
                st.did(pool.memset(m["ones"][:, :], 1.0))
                st.did(pool.memset(m["neghalf"][:, :], -0.5))
                st.did(pool.memset(m["upto"][:, :, :], 1.0))
                st.did(pool.memset(same[:, :], 0.0))
                st.did(pool.memset(half[:, :, :], 0.0))
                st.settle()
                pool.affine_select(out=m["ident"][:, :], in_=m["ident"][:, :], compare_op=ALU.not_equal, fill=1.0,
                                   base=0, pattern=[[-1, P]], channel_multiplier=1).then_inc(consts, 1)
                for d, sign in ((0, 1), (1, -1)):
                    st.did(pool.affine_select(out=m["upto"][:, d, :], in_=m["upto"][:, d, :], compare_op=ALU.is_ge,
                                              fill=0.0, base=0, pattern=[[sign, P]], channel_multiplier=-sign))
                st.settle()
                st.did(pool.memset(m["upto"][0:CHUNK, 0, CHUNK:P], 0.0))
                st.did(pool.memset(m["upto"][CHUNK:P, 1, 0:CHUNK], 0.0))
                for c in range(2):
                    own = slice(c * CHUNK, (c + 1) * CHUNK)
                    st.did(pool.memset(same[own, own], 1.0))
                    st.did(pool.memset(half[own, c, :], 1.0))
                st.settle()
                pool.sem_inc(consts, 1)
                pool.wait_ge(ms_done, 1)
                pool.tensor_tensor(rinv[:, :], ms[:, :], m["neghalf"][:, 0:NT], ALU.pow).then_inc(rinv_done, 1)

            @block.tensor
            def _(pe):
                pe.wait_ge(vec_in, 96)
                pe.wait_ge(consts, 1)
                pe.transpose(ps[:, 0, 0:VROWS], rows[:, :], m["ident"][0:VROWS, 0:VROWS])
                pe.transpose(ps[:, 0, P:P + CROWS], crows[:, :], m["ident"][0:CROWS, 0:CROWS]).then_inc(vec_ps, 1)
                pe.wait_ge(vec_sb, 3)
                for b in range(ADA_FIRST):
                    pe.wait_ge(ada_in[b], 16)
                    for j in range(ADA_TILES):
                        c = 2 * (b * ADA_TILES + j)
                        for k in range(KD):
                            mm = pe.matmul(ps[:, 1, c:c + 2], ada[:, b, k, j * P:(j + 1) * P], m["sc"][:, k, :],
                                           start=(k == 0), stop=(k == KD - 1))
                mm.then_inc(mod_ps, 1)
                for n in range(GROUPS * KD):
                    g, k = divmod(n, KD)
                    if k == 0:
                        pe.wait_ge(xn_done, TPG * (g + 1))
                    if n >= 6:
                        pe.wait_ge(hT_dve if n % 2 == 0 else hT_act, (n - 6) // 2 + 1)
                    for t in range(TPG):
                        mm = pe.transpose(ps[:, 2 + n % 6, t * P:(t + 1) * P], xt[:, g * TPG + t, k * P:(k + 1) * P],
                                          m["ident"][:, :])
                    mm.then_inc(xT_ps, 1)
                pe.wait_ge(hT_dve, KD)
                pe.wait_ge(hT_act, KD)
                pe.wait_ge(small_in, 48)
                for t in range(NT):
                    for k in range(KD):
                        mm = pe.matmul(ps[:, 0, t * 16:(t + 1) * 16], m["hT"][:, k, t * P:(t + 1) * P], wsm[:, k, :],
                                       start=(k == 0), stop=(k == KD - 1))
                mm.then_inc(small_ps, 1)
                pe.wait_ge(logd_done, 1)
                pe.wait_ge(consts, 2)
                logd = tab[:, LOGD, :, :]
                for d in range(2):
                    pe.matmul(ps[:, 1, 32 * d:32 * d + 32], m["upto"][:, d, :], logd[:, :, d * HA:(d + 1) * HA],
                              start=True, stop=True)
                pe.matmul(ps[:, 1, 64:128], same[:, :], logd, start=True, stop=True)
                for c in range(2):
                    mm = pe.matmul(ps[:, 1, 128 + 64 * c:192 + 64 * c], half[:, c, :], logd, start=True, stop=True)
                mm.then_inc(cum_ps, 1)

            @block.scalar
            def _(act):
                st = Steps(act, act_step)
                act.wait_ge(vec_ps, 1)
                act.activation(m["vecT"][:, :], ps[:, 0, 0:VROWS], ACT.Copy).then_inc(vec_sb, 1)
                act.activation(m["convT"][:, :], ps[:, 0, P:P + CROWS], ACT.Copy).then_inc(vec_sb, 1)
                act.activation(m["sc"][:, :, :], ps[:, 0, VC:VC + 16].rearrange("p (g k) -> p k g", g=GROUPS),
                               ACT.Silu).then_inc(vec_sb, 1)
                for t in range(NT):
                    if t % TPG == 0:
                        act.wait_ge(x_in[t // TPG], 16)
                    if t:
                        act.wait_ge(ssq_done, t)
                    act.activation(junk[:, :], xt[:, t, :], ACT.Square, accum_out=ssq[:, t:t + 1]).then_inc(ssq_done, 1)
                act.wait_ge(mul_ready, 2)
                for n in range(1, GROUPS * KD, 2):
                    g, k = divmod(n, KD)
                    act.wait_ge(xT_ps, n + 1)
                    act.activation(m["hT"][:, k, g * SEQ:(g + 1) * SEQ], ps[:, 2 + n % 6, :], ACT.Identity,
                                   bias=m["modT"][:, k, g:g + 1], scale=mul1[:, k, g:g + 1]).then_inc(hT_act, 1)
                act.wait_ge(small_in, 48)
                st.did(act.activation(ealog[:, :], alog[:, :], ACT.Exp))
                small = ps[:, 0, 0:P].rearrange("p (t c) -> p t c", t=NT)
                act.wait_ge(al_done, 1)
                st.did(act.activation(eb[:, :, :], small[:, :, 0:2 * HA], ACT.Exp, scale=-1.0))
                act.activation(nal[:, :, :], nal[:, :, :], ACT.Exp).then_inc(nal_done, 1)
                act.wait_ge(al_done, 2)
                act.activation(sp1[:, :, :], sp1[:, :, :], ACT.Ln).then_inc(nal_done, 1)
                act.wait_ge(cum_sb, 1)
                for d in range(2):
                    act.activation(tab[:, ECUM, :, d * HA:(d + 1) * HA],
                                   ps[:, 1, 32 * d:32 * d + 32].rearrange("p (t h) -> p t h", t=NT),
                                   ACT.Exp).then_inc(act_step, 1)
                act.activation(tab[:, ETOT:ETOT + 2, :, :],
                               ps[:, 1, 128:256].rearrange("p (c t h) -> p c t h", c=2, t=NT), ACT.Exp).then_inc(act_step, 1)
                act.activation(tab[:, EREST, :, :], rest[:, :, :], ACT.Exp).then_inc(act_step, 1)

            @block.vector
            def _(dve):
                st = Steps(dve, dve_step)
                dve.wait_ge(ssq_done, NT)
                dve.tensor_scalar(ms[:, :], ssq[:, :], 1.0 / D_MODEL, EPS, ALU.mult, ALU.add).then_inc(ms_done, 1)
                dve.wait_ge(rinv_done, 1)
                for t in range(NT):
                    dve.tensor_scalar(xt[:, t, :], xt[:, t, :], rinv[:, t:t + 1], None, ALU.mult).then_inc(xn_done, 1)
                dve.wait_ge(mod_ps, 1)
                dve.wait_ge(vec_sb, 2)
                n1 = 2 * KD
                dve.tensor_tensor(m["modT"][:, 0:n1, :], ps[:, 1, 0:2 * n1].rearrange("p (j g) -> p j g", g=GROUPS),
                                  bcast(m["vecT"][:, VB:VB + n1], 2, GROUPS), ALU.add).then_inc(mul_ready, 1)
                dve.wait_ge(mul_ready, 1)
                dve.scalar_tensor_tensor(out=mul1[:, :, :], in0=m["modT"][:, KD:n1, :], scalar=1.0,
                                         in1=bcast(m["vecT"][:, VN1:VN1 + 8], 2, GROUPS),
                                         op0=ALU.add, op1=ALU.mult).then_inc(mul_ready, 1)
                dve.wait_ge(mul_ready, 2)
                for n in range(0, GROUPS * KD, 2):
                    g, k = divmod(n, KD)
                    dve.wait_ge(xT_ps, n + 1)
                    dve.tensor_scalar(m["hT"][:, k, g * SEQ:(g + 1) * SEQ], ps[:, 2 + n % 6, :],
                                      mul1[:, k, g:g + 1], m["modT"][:, k, g:g + 1], ALU.mult, ALU.add).then_inc(hT_dve, 1)
                dve.wait_ge(small_ps, 1)
                dve.wait_ge(small_in, 48)
                small = ps[:, 0, 0:P].rearrange("p (t c) -> p t c", t=NT)
                st.do(dve.tensor_tensor(al[:, :, :], small[:, :, 2 * HA:4 * HA], bcast(dtb[:, :], 1, NT), ALU.add))
                dve.scalar_tensor_tensor(out=nal[:, :, :], in0=al[:, :, :], scalar=-1.0, in1=al[:, :, :],
                                         op0=ALU.mult, op1=ALU.min).then_inc(al_done, 1)
                dve.wait_ge(nal_done, 1)
                dve.tensor_scalar(sp1[:, :, :], nal[:, :, :], 1.0, None, ALU.add).then_inc(al_done, 1)
                dve.wait_ge(nal_done, 2)
                st.do(dve.scalar_tensor_tensor(out=al[:, :, :], in0=al[:, :, :], scalar=0.0, in1=sp1[:, :, :],
                                               op0=ALU.max, op1=ALU.add))
                dve.wait_ge(act_step, 2)
                dve.scalar_tensor_tensor(out=tab[:, LOGD, :, :], in0=al[:, :, :], scalar=-1.0,
                                         in1=bcast(ealog[:, :], 1, NT), op0=ALU.mult, op1=ALU.mult).then_inc(logd_done, 1)
                st.do(dve.tensor_scalar(eb[:, :, :], eb[:, :, :], 1.0, None, ALU.add))
                st.do(dve.reciprocal(tab[:, BETA, :, :], eb[:, :, :]))
                dve.wait_ge(cum_ps, 1)
                for d in range(2):
                    st.did(dve.tensor_copy(tab[:, CUM, :, d * HA:(d + 1) * HA],
                                           ps[:, 1, 32 * d:32 * d + 32].rearrange("p (t h) -> p t h", t=NT)))
                st.settle()
                dve.tensor_tensor(rest[:, :, :], ps[:, 1, 64:128].rearrange("p (t h) -> p t h", t=NT),
                                  tab[:, CUM, :, :], ALU.subtract).then_inc(cum_sb, 1)
                dve.wait_ge(act_step, 5)
                st.do(dve.tensor_tensor(tab[:, BECUM, :, :], tab[:, BETA, :, :], tab[:, ECUM, :, :], ALU.mult))


def phase_deltanet(nc, a, m, ps):
    NPROJ = 4 * GROUPS
    with ExitStack() as ctx:
        def sb(name, shape, dt=F32):
            return ctx.enter_context(nc.sbuf_tensor(name, shape, dt))

        sems = []

        def sem(name):
            sems.append(nc.alloc_semaphore(name))
            return sems[-1]

        w4 = sb("w4", [P, 4, KD, P])
        ada = sb("ada_d", [P, KD, ADA_BLOCK])
        posmask = sb("posmask", [P, 2, P])
        levelmask = sb("levelmask", [P, 2, LEVELS, P])
        pre = sb("pre", [P, 2, SEQ + CONV_K - 1])
        conv = sb("conv", [P, 3, GROUPS, SEQ])
        zT = sb("zT", [P, GROUPS, SEQ])
        cw = sb("cw", [P, CONV_K * 3])
        hd = sb("hd", [P, NQ, NT, 2])
        junk = sb("junk_d", [P, P])
        ssqk = sb("ssqk", [P, 2 * TPG])
        msqk = sb("msqk", [P, 2 * TPG])
        rqk = sb("rqk", [P, 2 * TPG])
        qn = sb("qn", [P, TPG, P])
        kn = sb("kn", [P, TPG, P])
        qnT = sb("qnT", [P, TPG, P])
        knT = sb("knT", [P, TPG, P])
        vb = [sb(f"vb{d}", [P, TPG, P]) for d in range(2)]
        kbe = [sb(f"kbe{d}", [P, TPG, P]) for d in range(2)]
        kd = [sb(f"kd{d}", [P, TPG, P]) for d in range(2)]
        qe = [sb(f"qe{d}", [P, TPG, P]) for d in range(2)]
        qeT = [sb(f"qeT{d}", [P, TPG, P]) for d in range(2)]
        gsum = [sb(f"gsum{d}", [P, TPG, P]) for d in range(2)]
        dec = [sb(f"dec{d}", [P, TPG, P]) for d in range(2)]
        xb = [sb(f"xb{d}", [P, TPG, P]) for d in range(2)]
        xbT = [sb(f"xbT{d}", [P, TPG, P]) for d in range(2)]
        qkT = [sb(f"qkT{d}", [P, TPG, P]) for d in range(2)]
        inv = [sb(f"inv{d}", [P, 2, TPG, P]) for d in range(2)]
        vnew = [sb(f"vnew{d}", [P, TPG, P]) for d in range(2)]
        state = [sb(f"state{d}", [P, NCHUNK, P]) for d in range(2)]
        ssqo = sb("ssqo", [P, TPG])
        mso = sb("mso", [P, TPG])
        ro = sb("ro", [P, TPG])
        on = sb("on", [P, TPG, P])

        w_in_ready = sem("w_in_ready")
        ada_in = sem("ada_in_d")
        masks = sem("masks_d")
        posmask_done = sem("posmask_done")
        pool_step = sem("pool_step_d")
        dve_step = sem("dve_step_d")
        hd_ready = sem("hd_ready")
        proj_ps = sem("proj_ps")
        proj_read = sem("proj_read")
        conv_done = sem("conv_done")
        silu_done = sem("silu_done")
        mod_ps = sem("mod_ps_d")
        mod_done = sem("mod_done_d")
        tok_ps = sem("tok_ps")
        sq_done = sem("sq_done")
        ms_done = sem("ms_done_d")
        rqk_done = sem("rqk_done")
        qn_done = sem("qn_done")
        kn_done = sem("kn_done")
        vb_done = sem("vb_done")
        chn_ps = sem("chn_ps")
        chn_sb = sem("chn_sb")
        gsum_done = sem("gsum_done")
        row_ps = [sem(f"row_ps{d}") for d in range(2)]
        diff_done = [sem(f"diff_done{d}") for d in range(2)]
        dec_done = [sem(f"dec_done{d}") for d in range(2)]
        qe_done = sem("qe_done")
        qeT_ps = sem("qeT_ps")
        qeT_sb = sem("qeT_sb")
        gram_ps = sem("gram_ps")
        x_done = [sem(f"x_done{d}") for d in range(2)]
        xT_ps = [sem(f"xT_ps_d{d}") for d in range(2)]
        xT_sb = [sem(f"xT_sb_d{d}") for d in range(2)]
        kbe_done = sem("kbe_done")
        inv0_done = [sem(f"inv0_done{d}") for d in range(2)]
        y_ps = [sem(f"y_ps{d}") for d in range(2)]
        y_sb = [sem(f"y_sb{d}") for d in range(2)]
        upd_ps = [sem(f"upd_ps{d}") for d in range(2)]
        inv_done = [sem(f"inv_done{d}") for d in range(2)]
        uw_ps = [sem(f"uw_ps{d}") for d in range(2)]
        uw_sb = [sem(f"uw_sb{d}") for d in range(2)]
        ws_ps = [sem(f"ws_ps{d}") for d in range(2)]
        vnew_done = [sem(f"vnew_done{d}") for d in range(2)]
        kv_ps = [sem(f"kv_ps{d}") for d in range(2)]
        state_done = [sem(f"state_done{d}") for d in range(2)]
        o_ps = sem("o_ps")
        osq_done = sem("osq_done")
        mso_done = sem("mso_done")
        ro_done = sem("ro_done")
        on_done = sem("on_done")
        oT_ps = sem("oT_ps")
        oa_done = sem("oa_done")

        LV = LEVELS - 1
        NC1 = NCHUNK - 1
        D_STEPS = 1 + 3 * GROUPS * (CONV_K - 1)

        def chunks(d):
            return range(NCHUNK) if d == 0 else range(NCHUNK - 1, -1, -1)

        def place(c):
            return c // 2, slice(CHUNK * (c % 2), CHUNK * (c % 2) + CHUNK)

        with nc.Block() as block:

            @block.sync
            def _(sp):
                w_in = a["w_in"].rearrange("a (k p) n -> p (a k) n", p=P)
                w_ada = a["w_ada"].rearrange("a (k p) n -> p (a k) n", p=P)
                with sp.Fori(0, HA) as h:
                    sp.wait_ge(proj_ps, h * NPROJ)
                    for b in range(4):
                        sp.dma_start(w4[:, b, :, :], w_in[:, :, bass.ds(h * P + b * A_W, P)]).then_inc(w_in_ready, 16)
                    for b in range(2):
                        sp.wait_ge(mod_ps, 2 * h + b)
                        sp.dma_start(ada[:, :, :], w_ada[:, :, bass.ds(h * (2 * ADA_BLOCK) + (ADA_FIRST + b) * ADA_BLOCK,
                                                                       ADA_BLOCK)]).then_inc(ada_in, 16)

            @block.gpsimd
            def _(pool):
                st = Steps(pool, pool_step)
                st.did(pool.memset(levelmask[:, :, :, :], 0.0))
                st.settle()
                for d in range(2):
                    for lv in range(LEVELS):
                        s = 2 ** lv
                        part = levelmask[:, d, lv, :].rearrange("p (b u s) -> p b u s", u=2, s=s)[:, :, d, :]
                        st.do(pool.memset(part, 1.0))
                        lo = s if d == 0 else 0
                        pat = [[-2 * s, P // (2 * s)], [0, s]]
                        st.do(pool.affine_select(out=part, in_=part, compare_op=ALU.is_ge, fill=0.0, base=-lo,
                                                 pattern=pat, channel_multiplier=1))
                        st.do(pool.affine_select(out=part, in_=part, compare_op=ALU.is_ge, fill=0.0, base=lo + s - 1,
                                                 pattern=[[2 * s, P // (2 * s)], [0, s]], channel_multiplier=-1))
                st.did(pool.memset(pre[:, :, 0:2], 0.0))
                st.did(pool.memset(pre[:, :, SEQ + 2:SEQ + 4], 0.0))
                st.settle()
                pool.sem_inc(masks, 1)

                with pool.Fori(0, HA) as h:
                    for g in range(GROUPS):
                        n = h * GROUPS + g
                        tiles = slice(g * TPG, (g + 1) * TPG)
                        if g == 0:
                            pool.wait_ge(hd_ready, h + 1)
                        for d in range(2):
                            if g == 1:
                                pool.wait_ge(row_ps[d], n)
                            pool.tensor_tensor(gsum[d][:, :, :], bcast(m["upto"][:, d, :], 1, TPG),
                                               bcast(hd[:, LOGD, tiles, d], 2, P), ALU.mult).then_inc(gsum_done, 1)
                        pool.wait_ge(ms_done, n + 1)
                        pool.tensor_tensor(rqk[:, :], msqk[:, :], m["neghalf"][:, 0:2 * TPG], ALU.pow).then_inc(rqk_done, 1)
                        pool.wait_ge(qn_done, n + 1)
                        for d in range(2):
                            pool.tensor_tensor(qe[d][:, :, :], qn[:, :, :], bcast(hd[:, ECUM, tiles, d], 2, P),
                                               ALU.mult).then_inc(qe_done, 1)
                        pool.wait_ge(kn_done, n + 1)
                        for d in range(2):
                            pool.tensor_tensor(kbe[d][:, :, :], kn[:, :, :], bcast(hd[:, BECUM, tiles, d], 2, P),
                                               ALU.mult).then_inc(kbe_done, 1)
                            pool.tensor_tensor(kd[d][:, :, :], kn[:, :, :], bcast(hd[:, EREST, tiles, d], 2, P),
                                               ALU.mult).then_inc(kbe_done, 1)
                        for d in range(2):
                            pool.wait_ge(x_done[d], 2 * n + 2)
                            pool.wait_ge(xT_sb[d], 2 * n + 1)
                            for side, src in enumerate((xb[d], xbT[d])):
                                pool.tensor_tensor(inv[d][:, side, :, :], src[:, :, :],
                                                   bcast(levelmask[:, (d + side) % 2, 0, :], 1, TPG),
                                                   ALU.mult).then_inc(inv0_done[d], 1)
                            pool.wait_ge(inv0_done[d], 4 * n + 2)
                            for side in range(2):
                                pool.tensor_tensor(inv[d][:, side, :, :], bcast(m["ident"][:, :], 1, TPG),
                                                   inv[d][:, side, :, :], ALU.subtract).then_inc(inv0_done[d], 1)
                        pool.wait_ge(mso_done, n + 1)
                        pool.tensor_tensor(ro[:, :], mso[:, :], m["neghalf"][:, 0:TPG], ALU.pow).then_inc(ro_done, 1)

            @block.tensor
            def _(pe):
                ident = m["ident"][:, :]
                with pe.Fori(0, HA) as h:
                    pe.wait_ge(w_in_ready, (h + 1) * 64)
                    for u in range(NPROJ):
                        b, g = divmod(u, GROUPS)
                        if u < 2:
                            pe.wait_ge(proj_read, h * NPROJ)
                            pe.wait_ge(oa_done, h * GROUPS)
                            pe.wait_ge(uw_sb[1], h * 2 * GROUPS)
                        else:
                            pe.wait_ge(proj_read, h * NPROJ + (u - 1))
                        for k in range(KD):
                            mm = pe.matmul(ps[:, u % 2, :], w4[:, b, k, :], m["hT"][:, k, g * SEQ:(g + 1) * SEQ],
                                           start=(k == 0), stop=(k == KD - 1))
                        mm.then_inc(proj_ps, 1)
                    for b in range(2):
                        pe.wait_ge(ada_in, (2 * h + b + 1) * 16)
                        pe.wait_ge(mod_done, 2 * h + b)
                        for j in range(ADA_TILES):
                            for k in range(KD):
                                mm = pe.matmul(ps[:, 2, 2 * j:2 * j + 2], ada[:, k, j * P:(j + 1) * P], m["sc"][:, k, :],
                                               start=(k == 0), stop=(k == KD - 1))
                        mm.then_inc(mod_ps, 1)
                    for g in range(GROUPS):
                        n = h * GROUPS + g
                        pe.wait_ge(on_done, n)
                        for i in range(3):
                            pe.wait_ge(silu_done, h * 6 + (2 * i + g + 1))
                            for t in range(TPG):
                                mm = pe.transpose(ps[:, 3 + i, t * P:(t + 1) * P], conv[:, i, g, t * P:(t + 1) * P], ident)
                            mm.then_inc(tok_ps, 1)
                        pe.wait_ge(gsum_done, 2 * n + 2)
                        pe.wait_ge(proj_read, h * NPROJ + NPROJ)
                        pe.wait_ge(oa_done, n)
                        for d in range(2):
                            pe.matmul(ps[:, d, :], m["ones"][:, :], gsum[d][:, :, :], start=True,
                                      stop=True).then_inc(row_ps[d], 1)
                        for i, (src, ready) in enumerate(((kn, kn_done), (qn, qn_done))):
                            pe.wait_ge(ready, n + 1)
                            for t in range(TPG):
                                mm = pe.transpose(ps[:, 6 + i, t * P:(t + 1) * P], src[:, t, :], ident)
                            mm.then_inc(chn_ps, 1)
                        pe.wait_ge(chn_sb, 2 * n + 2)
                        for i, lhs in enumerate((knT, qnT)):
                            for t in range(TPG):
                                mm = pe.matmul(ps[:, 3 + i, t * P:(t + 1) * P], lhs[:, t, :], knT[:, t, :],
                                               start=True, stop=True)
                        mm.then_inc(gram_ps, 1)
                        pe.wait_ge(vb_done, n + 1)
                        for d in range(2):
                            pe.wait_ge(qe_done, 2 * n + d + 1)
                            for t in range(TPG):
                                mm = pe.transpose(ps[:, 5 + d, t * P:(t + 1) * P], qe[d][:, t, :], ident)
                            mm.then_inc(qeT_ps, 1)
                        for d in range(2):
                            pe.wait_ge(x_done[d], 2 * n + 2)
                            for t in range(TPG):
                                mm = pe.transpose(ps[:, d, t * P:(t + 1) * P], xb[d][:, t, :], ident)
                            mm.then_inc(xT_ps[d], 1)
                            pe.wait_ge(qeT_sb, 2 * n + 2)
                            for t in range(TPG):
                                mm = pe.transpose(ps[:, 5 + 2 * d, t * P:(t + 1) * P], dec[d][:, t, :], ident)
                            mm.then_inc(xT_ps[d], 1)
                        for lv in range(LV):
                            for d in range(2):
                                if lv == 0:
                                    pe.wait_ge(x_done[1 - d], 2 * n + 2)
                                    pe.wait_ge(xT_sb[d], 2 * n + 2)
                                    pe.wait_ge(inv0_done[d], 4 * n + 4)
                                else:
                                    pe.wait_ge(inv_done[d], n * LV + lv)
                                for t in range(TPG):
                                    mm = pe.matmul(ps[:, d, t * P:(t + 1) * P], xbT[d][:, t, :], inv[d][:, 0, t, :],
                                                   start=True, stop=True)
                                mm.then_inc(y_ps[d], 1)
                            for d in range(2):
                                pe.wait_ge(y_sb[d], n * LV + lv + 1)
                                if lv < LV - 1:
                                    for t in range(TPG):
                                        pe.matmul(ps[:, 4 + 2 * d, t * P:(t + 1) * P], inv[d][:, 1, t, :], xb[d][:, t, :],
                                                  start=True, stop=True)
                                for t in range(TPG):
                                    mm = pe.matmul(ps[:, 5 + 2 * d, t * P:(t + 1) * P], xb[d][:, t, :], inv[d][:, 1, t, :],
                                                   start=True, stop=True)
                                mm.then_inc(upd_ps[d], 1)
                        for d in range(2):
                            pe.wait_ge(inv_done[d], n * LV + LV)
                            pe.wait_ge(kbe_done, 4 * n + 2 * d + 1)
                            for t in range(TPG):
                                pe.matmul(ps[:, d, t * P:(t + 1) * P], inv[d][:, 1, t, :], vb[d][:, t, :],
                                          start=True, stop=True)
                            for t in range(TPG):
                                mm = pe.matmul(ps[:, 4 + 2 * d, t * P:(t + 1) * P], kbe[d][:, t, :], inv[d][:, 1, t, :],
                                               start=True, stop=True)
                            mm.then_inc(uw_ps[d], 1)
                        pe.wait_ge(kbe_done, 4 * n + 4)
                        for i in range(NCHUNK):
                            for d in range(2):
                                t, rows = place(chunks(d)[i])
                                if i == 0:
                                    pe.wait_ge(uw_sb[d], 2 * n + 2)
                                else:
                                    pe.wait_ge(state_done[d], n * NC1 + i)
                                    pe.matmul(ps[rows, 5 + 2 * d, 0:P], xbT[d][:, t, rows],
                                              state[d][:, i, :], start=True, stop=True).then_inc(ws_ps[d], 1)
                            for d in range(2):
                                t, rows = place(chunks(d)[i])
                                if i > 0:
                                    pe.wait_ge(vnew_done[d], n * NC1 + i)
                                if i < NC1:
                                    pe.matmul(ps[:, 5 + 2 * d, P:2 * P], kd[d][rows, t, :], vnew[d][rows, t, :],
                                              start=True, stop=True).then_inc(kv_ps[d], 1)
                        for t in range(TPG):
                            out = ps[:, 3, t * P:(t + 1) * P]
                            pe.matmul(out, qkT[0][:, t, :], vnew[0][:, t, :], start=True, stop=False)
                            terms = [(d, c) for d in range(2) for c in (2 * t, 2 * t + 1) if chunks(d)[0] != c]
                            for d, c in terms:
                                rows = place(c)[1]
                                pe.matmul(ps[rows, 3, t * P:(t + 1) * P], qeT[d][:, t, rows],
                                          state[d][:, chunks(d).index(c), :], start=False, stop=False)
                            mm = pe.matmul(out, qkT[1][:, t, :], vnew[1][:, t, :], start=False, stop=True)
                        mm.then_inc(o_ps, 1)
                        pe.wait_ge(on_done, n + 1)
                        for t in range(TPG):
                            mm = pe.transpose(ps[:, 0, t * P:(t + 1) * P], on[:, t, :], ident)
                        mm.then_inc(oT_ps, 1)

            @block.scalar
            def _(act):
                act.wait_ge(masks, 1)
                with act.Fori(0, HA) as h:
                    def silu(u):
                        b, g = divmod(u, GROUPS)
                        act.wait_ge(conv_done, h * 6 + (u + 1))
                        act.activation(conv[:, b, g, :], conv[:, b, g, :], ACT.Silu).then_inc(silu_done, 1)

                    for u in range(NPROJ):
                        b, g = divmod(u, GROUPS)
                        act.wait_ge(proj_ps, h * NPROJ + (u + 1))
                        if b < 3:
                            act.activation(pre[:, u % 2, 2:SEQ + 2], ps[:, u % 2, :], ACT.Copy).then_inc(proj_read, 1)
                        else:
                            act.activation(zT[:, g, :], ps[:, u % 2, :], ACT.Silu).then_inc(proj_read, 1)
                        if 1 <= u <= 6:
                            silu(u - 1)
                    for g in range(GROUPS):
                        n = h * GROUPS + g
                        for i in range(2):
                            act.wait_ge(tok_ps, 3 * n + i + 1)
                            for t in range(TPG):
                                c = i * TPG + t
                                act.wait_ge(sq_done, n * 2 * TPG + c)
                                act.activation(junk[:, :], ps[:, 3 + i, t * P:(t + 1) * P], ACT.Square,
                                               accum_out=ssqk[:, c:c + 1]).then_inc(sq_done, 1)
                        for i, dst in enumerate((knT, qnT)):
                            act.wait_ge(chn_ps, 2 * n + i + 1)
                            act.activation(dst[:, :, :], ps[:, 6 + i, :], ACT.Copy).then_inc(chn_sb, 1)
                        for d in range(2):
                            act.wait_ge(diff_done[d], TPG * n + TPG)
                            act.activation(dec[d][:, :, :], dec[d][:, :, :], ACT.Exp, scale=-1.0).then_inc(dec_done[d], 1)
                        for d in range(2):
                            act.wait_ge(qeT_ps, 2 * n + d + 1)
                            act.activation(qeT[d][:, :, :], ps[:, 5 + d, :], ACT.Copy).then_inc(qeT_sb, 1)
                        for d in range(2):
                            act.wait_ge(xT_ps[d], 2 * n + 1)
                            act.activation(xbT[d][:, :, :], ps[:, d, :], ACT.Copy).then_inc(xT_sb[d], 1)
                            act.wait_ge(xT_ps[d], 2 * n + 2)
                            act.activation(qkT[d][:, :, :], ps[:, 5 + 2 * d, :], ACT.Copy).then_inc(xT_sb[d], 1)
                        for d in range(2):
                            act.wait_ge(uw_ps[d], n + 1)
                            act.activation(vnew[d][:, :, :], ps[:, d, :], ACT.Copy).then_inc(uw_sb[d], 1)
                            act.activation(xbT[d][:, :, :], ps[:, 4 + 2 * d, :], ACT.Copy).then_inc(uw_sb[d], 1)
                        act.wait_ge(o_ps, n + 1)
                        for t in range(TPG):
                            act.wait_ge(osq_done, n * TPG + t)
                            act.activation(junk[:, :], ps[:, 3, t * P:(t + 1) * P], ACT.Square,
                                           accum_out=ssqo[:, t:t + 1]).then_inc(osq_done, 1)

            @block.vector
            def _(dve):
                for d in range(2):
                    dve.tensor_scalar(posmask[:, d, :], m["upto"][:, 1 - d, :], -BIG, BIG, ALU.mult, ALU.add).then_inc(posmask_done, 1)
                dve.wait_ge(posmask_done, 2)
                dve.wait_ge(masks, 1)
                with dve.Fori(0, HA) as h:
                    st = Steps(dve, dve_step, before=h * D_STEPS)
                    dve.tensor_copy(hd[:, :, :, :], m["tab"][:, :, :, :].rearrange("p q t (d h) -> p (q t d) h", d=2)
                                    [:, :, bass.ds(h, 1)]).then_inc(hd_ready, 1)
                    st.do(dve.tensor_copy(cw[:, :], m["convT"][:, 0:60].rearrange("p (r h) -> p r h", h=HA)
                                          [:, :, bass.ds(h, 1)]))
                    for u in range(6):
                        b, g = divmod(u, GROUPS)
                        dve.wait_ge(proj_read, h * NPROJ + (u + 1))
                        acc = conv[:, b, g, :]
                        st.do(dve.tensor_scalar(acc, pre[:, u % 2, 0:SEQ], cw[:, b:b + 1], None, ALU.mult))
                        for tap in range(1, CONV_K):
                            ins = dve.scalar_tensor_tensor(out=acc, in0=pre[:, u % 2, tap:tap + SEQ],
                                                           scalar=cw[:, 3 * tap + b:3 * tap + b + 1], in1=acc,
                                                           op0=ALU.mult, op1=ALU.add)
                            if tap < CONV_K - 1:
                                st.do(ins)
                            else:
                                ins.then_inc(conv_done, 1)
                    for b in range(2):
                        dve.wait_ge(mod_ps, 2 * h + b + 1)
                        first = 16 + b * ADA_TILES
                        dve.tensor_tensor(m["modT"][:, :, :].rearrange("p j g -> p (j g)")[:, bass.ds(h * 16 + 2 * first, 8)]
                                          .rearrange("p (j g) -> p j g", g=2),
                                          ps[:, 2, 0:8].rearrange("p (j g) -> p j g", g=2),
                                          bcast(m["vecT"][:, bass.ds(h * 8 + first, 4)], 2, GROUPS), ALU.add).then_inc(mod_done, 1)
                    for g in range(GROUPS):
                        n = h * GROUPS + g
                        tiles = slice(g * TPG, (g + 1) * TPG)
                        dve.wait_ge(sq_done, (n + 1) * 2 * TPG)
                        dve.tensor_scalar(msqk[:, 0:TPG], ssqk[:, 0:TPG], EPS, float(DK), ALU.add, ALU.mult)
                        dve.tensor_scalar(msqk[:, TPG:], ssqk[:, TPG:], EPS, None, ALU.add).then_inc(ms_done, 1)
                        dve.wait_ge(tok_ps, 3 * n + 3)
                        for d in range(2):
                            ins = dve.tensor_tensor(vb[d][:, :, :], ps[:, 5, :].rearrange("p (t c) -> p t c", t=TPG),
                                                    bcast(hd[:, BETA, tiles, d], 2, P), ALU.mult)
                        ins.then_inc(vb_done, 1)
                        dve.wait_ge(rqk_done, n + 1)
                        dve.tensor_tensor(kn[:, :, :], ps[:, 4, :].rearrange("p (t c) -> p t c", t=TPG),
                                          bcast(rqk[:, TPG:], 2, P), ALU.mult).then_inc(kn_done, 1)
                        dve.tensor_tensor(qn[:, :, :], ps[:, 3, :].rearrange("p (t c) -> p t c", t=TPG),
                                          bcast(rqk[:, 0:TPG], 2, P), ALU.mult).then_inc(qn_done, 1)
                        for d in range(2):
                            dve.wait_ge(row_ps[d], n + 1)
                            for t in range(TPG):
                                dve.scalar_tensor_tensor(out=dec[d][:, t, :], in0=ps[:, d, t * P:(t + 1) * P],
                                                         scalar=hd[:, CUM, g * TPG + t, d:d + 1], in1=posmask[:, d, :],
                                                         op0=ALU.subtract, op1=ALU.add).then_inc(diff_done[d], 1)
                        dve.wait_ge(gram_ps, n + 1)
                        for d in range(2):
                            dve.wait_ge(dec_done[d], n + 1)
                            for t in range(TPG):
                                ins = dve.scalar_tensor_tensor(out=xb[d][:, t, :], in0=ps[:, 3, t * P:(t + 1) * P],
                                                               scalar=hd[:, BETA, g * TPG + t, d:d + 1],
                                                               in1=dec[d][:, t, :], op0=ALU.mult, op1=ALU.mult)
                            ins.then_inc(x_done[d], 1)
                            dve.wait_ge(x_done[d], 2 * n + 1)
                            dve.tensor_tensor(dec[d][:, :, :], ps[:, 4, :], dec[d][:, :, :].rearrange("p t c -> p (t c)"),
                                              ALU.mult).then_inc(x_done[d], 1)
                        for lv in range(LV):
                            for d in range(2):
                                dve.wait_ge(y_ps[d], n * LV + lv + 1)
                                if lv == 0:
                                    dve.wait_ge(inv0_done[d], 4 * n + 4)
                                dve.tensor_tensor(xb[d][:, :, :], ps[:, d, :].rearrange("p (t c) -> p t c", t=TPG),
                                                  bcast(levelmask[:, d, lv + 1, :], 1, TPG), ALU.mult).then_inc(y_sb[d], 1)
                            for d in range(2):
                                dve.wait_ge(upd_ps[d], n * LV + lv + 1)
                                lo = 0 if lv < LV - 1 else 1
                                dve.tensor_tensor(inv[d][:, lo:2, :, :].rearrange("p s t c -> p s (t c)"),
                                                  inv[d][:, lo:2, :, :].rearrange("p s t c -> p s (t c)"),
                                                  ps[:, 4 + 2 * d + lo:6 + 2 * d, :], ALU.subtract).then_inc(inv_done[d], 1)
                        for i in range(NCHUNK):
                            for d in range(2):
                                t, rows = place(chunks(d)[i])
                                if i > 0:
                                    dve.wait_ge(ws_ps[d], n * NC1 + i)
                                    dve.tensor_tensor(vnew[d][rows, t, :], vnew[d][rows, t, :], ps[rows, 5 + 2 * d, 0:P],
                                                      ALU.subtract).then_inc(vnew_done[d], 1)
                            for d in range(2):
                                c = chunks(d)[i]
                                if i < NC1:
                                    dve.wait_ge(kv_ps[d], n * NC1 + i + 1)
                                    kv = ps[:, 5 + 2 * d, P:2 * P]
                                    if i == 0:
                                        dve.tensor_copy(state[d][:, 1, :], kv).then_inc(state_done[d], 1)
                                    else:
                                        dve.scalar_tensor_tensor(out=state[d][:, i + 1, :], in0=state[d][:, i, :],
                                                                 scalar=hd[:, ETOT + c % 2, g * TPG + c // 2, d:d + 1], in1=kv,
                                                                 op0=ALU.mult, op1=ALU.add).then_inc(state_done[d], 1)
                        dve.wait_ge(osq_done, (n + 1) * TPG)
                        dve.tensor_scalar(mso[:, :], ssqo[:, :], 1.0 / DK, EPS, ALU.mult, ALU.add).then_inc(mso_done, 1)
                        dve.wait_ge(ro_done, n + 1)
                        dve.tensor_tensor(on[:, :, :], ps[:, 3, :].rearrange("p (t c) -> p t c", t=TPG),
                                          bcast(ro[:, :], 2, P), ALU.mult).then_inc(on_done, 1)
                        dve.wait_ge(oT_ps, n + 1)
                        dve.scalar_tensor_tensor(out=m["oaT"][:, :, :].rearrange("p h t -> p (h t)")
                                                 [:, bass.ds(h * TOK + g * SEQ, SEQ)],
                                                 in0=ps[:, 0, :], scalar=m["convT"][:, 60:61], in1=zT[:, g, :],
                                                 op0=ALU.mult, op1=ALU.mult).then_inc(oa_done, 1)
                    assert st.n == D_STEPS
        nc.clear_and_free_semaphores(sems)
        nc.all_engine_barrier()


def phase_attention(nc, a, m, ps):
    NPROJ = 3 * GROUPS
    NU = GROUPS * 2 * TPG
    KINDS = [(16, 48), (0, 48), (0, 32)]
    KIND_OF = [0, 1, 1, 2]
    KIND_AT = [0, 256, 640]
    BIAS_W = 896
    with ExitStack() as ctx:
        def sb(name, shape, dt=F32):
            return ctx.enter_context(nc.sbuf_tensor(name, shape, dt))

        def sem(name):
            return ctx.enter_context(nc.semaphore(name))

        w3 = sb("w3", [P, 3, KD, P])
        rel = sb("rel", [P, HB, RPB_RUN])
        outside = sb("outside", [P, BIAS_W])
        bias = sb("bias", [P, 2, BIAS_W])
        qT = sb("qT", [P, GROUPS, SEQ])
        kT = sb("kT", [P, GROUPS, SEQ])
        vT = sb("vT", [P, GROUPS, SEQ])
        vtok = sb("vtok", [P, GROUPS, TPG, P])
        sc = sb("scores", [P, 2, 3 * P])
        low = sb("low", [P, 2])
        pr = sb("pr", [P, 2, 3 * P])
        den = sb("den", [P, 2])
        rden = sb("rden", [P, 2])
        pT = sb("pT", [P, 2, 3 * P])
        otok = sb("otok", [P, GROUPS, TPG, P])

        w_ready = sem("w3_ready")
        rel_in = sem("rel_in")
        outside_done = sem("outside_done")
        bias_done = sem("bias_done")
        proj_ps = sem("projb_ps")
        proj_read = sem("projb_read")
        vt_ps = sem("vt_ps")
        vtok_sb = sem("vtok_sb")
        s_ps = sem("s_ps")
        sc_done = sem("sc_done")
        low_done = sem("low_done")
        exp_done = sem("exp_done")
        pT_ps = sem("pT_ps")
        pT_sb = sem("pT_sb")
        pv_ps = sem("pv_ps")
        rden_done = sem("rden_done")
        otok_done = sem("otok_done")
        obT_ps = sem("obT_ps")
        ob_done = sem("ob_done")

        def unit(w):
            g, r = divmod(w, 2 * TPG)
            hp, t = divmod(r, TPG)
            return g, hp, t

        def width(t):
            return (KEY_TILES[t][1] - KEY_TILES[t][0]) * P

        def before(w, lag):
            return max(w - lag + 1, 0)

        with nc.Block() as block:

            @block.sync
            def _(sp):
                rpb = a["rpb"]
                for c in range(16):
                    src = bass.AP(rpb.tensor, RPB_FRONT - 15 * c - 8, [[HB * RPB_LEN, ROWS], [RPB_LEN, HB], [1, RPB_RUN]])
                    sp.dma_start(rel[8 * c:8 * c + 8, :, :], src).then_inc(rel_in, 16)
                w_in = a["w_in"].rearrange("a (k p) n -> p (a k) n", p=P)
                with sp.Fori(0, PAIRS) as h:
                    sp.wait_ge(proj_ps, h * NPROJ)
                    for b in range(3):
                        sp.dma_start(w3[:, b, :, :], w_in[:, :, bass.ds(h * P + (OFF_QB + b * HB * DH), P)]).then_inc(w_ready, 16)

            @block.gpsimd
            def _(pool):
                pool.memset(outside[:, :], 0.0).then_inc(outside_done, 1)
                n = 1

                def keep(kind, x0, x1, base, step, cm):
                    nonlocal n
                    pool.wait_ge(outside_done, n)
                    lo = KINDS[kind][0]
                    part = outside[:, KIND_AT[kind] + (x0 - lo) * 8:KIND_AT[kind] + (x1 - lo) * 8]
                    pool.affine_select(out=part, in_=part, compare_op=ALU.is_ge, fill=BIG, base=base + step * x0,
                                       pattern=[[step, x1 - x0], [0, 8]], channel_multiplier=cm).then_inc(outside_done, 1)
                    n += 1

                keep(0, 16, 48, 7 - 64, 8, -1)
                keep(0, 32, 48, 184, -8, 1)
                keep(1, 0, 48, 7 - 64, 8, -1)
                keep(1, 0, 48, 184, -8, 1)
                keep(2, 0, 16, 7 - 64, 8, -1)
                keep(2, 0, 32, 184, -8, 1)
                pool.wait_ge(outside_done, n)
                pool.wait_ge(rel_in, 16 * 16)
                rel_flat = rel[:, :, :].rearrange("p h x -> p (h x)")
                with pool.Fori(0, PAIRS) as h:
                    pool.wait_ge(sc_done, h * NU)
                    for hp in range(2):
                        for kind, (x0, x1) in enumerate(KINDS):
                            nx = x1 - x0
                            src = rel_flat[:, bass.ds(h * (2 * RPB_RUN) + (hp * RPB_RUN + x0 * RPB_R), nx * RPB_R)]
                            at = slice(KIND_AT[kind], KIND_AT[kind] + nx * 8)
                            pool.tensor_tensor(bias[:, hp, at].rearrange("p (x r) -> p x r", r=8),
                                               src.rearrange("p (x r) -> p x r", r=RPB_R)[:, :, 0:8],
                                               outside[:, at].rearrange("p (x r) -> p x r", r=8),
                                               ALU.subtract).then_inc(bias_done, 1)

            @block.tensor
            def _(pe):
                ident = m["ident"][:, :]
                with pe.Fori(0, PAIRS) as h:
                    pe.wait_ge(w_ready, (h + 1) * 48)
                    for u in range(NPROJ):
                        b, g = divmod(u, GROUPS)
                        if u < 2:
                            pe.wait_ge(proj_read, h * NPROJ)
                            pe.wait_ge(ob_done, h * GROUPS)
                        else:
                            pe.wait_ge(proj_read, h * NPROJ + (u - 1))
                        for k in range(KD):
                            mm = pe.matmul(ps[:, u % 2, :], w3[:, b, k, :], m["hT"][:, k, g * SEQ:(g + 1) * SEQ],
                                           start=(k == 0), stop=(k == KD - 1))
                        mm.then_inc(proj_ps, 1)
                    for g in range(GROUPS):
                        pe.wait_ge(proj_read, h * NPROJ + (5 + g))
                        pe.wait_ge(sc_done, h * NU)
                        for t in range(TPG):
                            mm = pe.transpose(ps[:, 2 + g, t * P:(t + 1) * P], vT[:, g, t * P:(t + 1) * P], ident)
                        mm.then_inc(vt_ps, 1)

                    def scores(w):
                        g, hp, t = unit(w)
                        k0, k1 = KEY_TILES[t]
                        if w < 2:
                            pe.wait_ge(vtok_sb, h * GROUPS + GROUPS)
                        pe.wait_ge(sc_done, h * NU + before(w, 2))
                        rows = slice(hp * DH, (hp + 1) * DH)
                        pe.matmul(ps[:, 2 + w % 2, 0:width(t)], qT[rows, g, t * P:(t + 1) * P],
                                  kT[rows, g, k0 * P:k1 * P], start=True, stop=True).then_inc(s_ps, 1)

                    def turn(w):
                        g, hp, t = unit(w)
                        pe.wait_ge(exp_done, h * NU + (w + 1))
                        pe.wait_ge(pT_sb, h * NU + before(w, 2))
                        for i in range(width(t) // P):
                            mm = pe.transpose(ps[:, 4 + w % 2, i * P:(i + 1) * P], pr[:, w % 2, i * P:(i + 1) * P], ident)
                        mm.then_inc(pT_ps, 1)

                    def values(w):
                        g, hp, t = unit(w)
                        k0, k1 = KEY_TILES[t]
                        pe.wait_ge(pT_sb, h * NU + (w + 1))
                        pe.wait_ge(otok_done, h * NU + before(w, 2))
                        for i in range(k1 - k0):
                            mm = pe.matmul(ps[:, 6 + w % 2, 0:DH], pT[:, w % 2, i * P:(i + 1) * P],
                                           vtok[:, g, k0 + i, hp * DH:(hp + 1) * DH], start=(i == 0), stop=(i == k1 - k0 - 1))
                        mm.then_inc(pv_ps, 1)

                    for w in range(NU + 3):
                        if w < NU:
                            scores(w)
                        if 2 <= w < NU + 2:
                            turn(w - 2)
                        if w >= 3:
                            values(w - 3)
                    for g in range(GROUPS):
                        pe.wait_ge(otok_done, h * NU + (g + 1) * 2 * TPG)
                        for t in range(TPG):
                            mm = pe.transpose(ps[:, g, t * P:(t + 1) * P], otok[:, g, t, :], ident)
                        mm.then_inc(obT_ps, 1)

            @block.scalar
            def _(act):
                with act.Fori(0, PAIRS) as h:
                    for u in range(NPROJ):
                        b, g = divmod(u, GROUPS)
                        act.wait_ge(proj_ps, h * NPROJ + (u + 1))
                        dst = (qT, kT, vT)[b][:, g, :].rearrange("p (c r) -> p r c", r=ROWS)
                        act.activation(dst, ps[:, u % 2, :].rearrange("p (r c) -> p r c", r=ROWS), ACT.Copy,
                                       scale=(-DH ** -0.5 if b == 0 else 1.0)).then_inc(proj_read, 1)
                    for g in range(GROUPS):
                        act.wait_ge(vt_ps, h * GROUPS + (g + 1))
                        act.activation(vtok[:, g, :, :], ps[:, 2 + g, :], ACT.Copy).then_inc(vtok_sb, 1)
                    for w in range(NU + 1):
                        if w < NU:
                            g, hp, t = unit(w)
                            act.wait_ge(low_done, h * NU + (w + 1))
                            act.wait_ge(pT_ps, h * NU + before(w, 2))
                            act.wait_ge(rden_done, h * NU + before(w, 2))
                            act.activation(pr[:, w % 2, 0:width(t)], sc[:, w % 2, 0:width(t)], ACT.Exp, scale=-1.0,
                                           bias=low[:, w % 2:w % 2 + 1],
                                           accum_out=den[:, w % 2:w % 2 + 1]).then_inc(exp_done, 1)
                        if w >= 1:
                            v = w - 1
                            g, hp, t = unit(v)
                            act.wait_ge(pT_ps, h * NU + (v + 1))
                            act.wait_ge(pv_ps, h * NU + before(v, 2))
                            act.activation(pT[:, v % 2, 0:width(t)], ps[:, 4 + v % 2, 0:width(t)], ACT.Copy).then_inc(pT_sb, 1)

            @block.vector
            def _(dve):
                with dve.Fori(0, PAIRS) as h:
                    dve.wait_ge(bias_done, (h + 1) * 6)
                    for w in range(NU + 3):
                        if w < NU:
                            g, hp, t = unit(w)
                            n = width(t)
                            dve.wait_ge(s_ps, h * NU + (w + 1))
                            dve.wait_ge(exp_done, h * NU + before(w, 2))
                            at = KIND_AT[KIND_OF[t]]
                            dve.tensor_tensor(sc[:, w % 2, 0:n], ps[:, 2 + w % 2, 0:n], bias[:, hp, at:at + n],
                                              ALU.subtract).then_inc(sc_done, 1)
                            dve.wait_ge(sc_done, h * NU + (w + 1))
                            dve.tensor_reduce(low[:, w % 2:w % 2 + 1], sc[:, w % 2, 0:n], AX_X, ALU.min).then_inc(low_done, 1)
                        if w >= 3:
                            v = w - 3
                            g, hp, t = unit(v)
                            dve.wait_ge(pv_ps, h * NU + (v + 1))
                            dve.wait_ge(rden_done, h * NU + (v + 1))
                            dve.tensor_scalar(otok[:, g, t, hp * DH:(hp + 1) * DH], ps[:, 6 + v % 2, 0:DH],
                                              rden[:, v % 2:v % 2 + 1], None, ALU.mult).then_inc(otok_done, 1)
                        if 2 <= w < NU + 2:
                            v = w - 2
                            dve.wait_ge(exp_done, h * NU + (v + 1))
                            dve.wait_ge(otok_done, h * NU + before(v, 2))
                            dve.reciprocal(rden[:, v % 2:v % 2 + 1], den[:, v % 2:v % 2 + 1]).then_inc(rden_done, 1)
                    for g in range(GROUPS):
                        dve.wait_ge(obT_ps, h * GROUPS + (g + 1))
                        dst = m["obT"][:, :, :].rearrange("p h t -> p (h t)")[:, bass.ds(h * TOK + g * SEQ, SEQ)]
                        dve.tensor_copy(dst.rearrange("p (r c) -> p r c", r=ROWS),
                                        ps[:, g, :].rearrange("p (c r) -> p r c", r=ROWS)).then_inc(ob_done, 1)


def late_buffers(nc, ctx):
    def sb(name, shape, dt=F32):
        return ctx.enter_context(nc.sbuf_tensor(name, shape, dt))

    late = {}
    late["mergedT"] = sb("mergedT", [P, KD, TOK])
    late["gate1"] = sb("gate1", [P, GROUPS, D_MODEL])
    late["mul2row"] = sb("mul2row", [P, GROUPS, D_MODEL])
    late["shift2"] = sb("shift2", [P, GROUPS, D_MODEL])
    late["wout"] = sb("wout", [P, KD, D_MODEL])
    late["wr"] = sb("wr", [P, KD, NE])
    late["route_in"] = ctx.enter_context(nc.semaphore("route_in"))
    return late


def phase_merge(nc, a, m, ps, late):
    JOBS = 2 * GROUPS
    ROWS_OF = 8
    with ExitStack() as ctx:
        def sb(name, shape, dt=F32):
            return ctx.enter_context(nc.sbuf_tensor(name, shape, dt))

        def sem(name):
            return ctx.enter_context(nc.semaphore(name))

        wj = [sb(f"wj{i}", [P, 3 * KD, P]) for i in range(2)]
        sig = sb("sig", [P, GROUPS, 2, SEQ])
        wide = sb("wide", [P, GROUPS, 2, SEQ])
        mul2 = sb("mul2", [P, KD, GROUPS])
        diag = sig[:, :, :, :].rearrange("p g b (k c) -> p g (b k) c", c=P)
        halfcols = sb("halfcols", [P, 2, P])

        halfcols_done = sem("halfcols_done")
        mul2_done = sem("mul2_done")
        diag_done = sem("diag_done")
        row_ps = sem("adarow_ps")
        row_sb = sem("adarow_sb")
        wj_in = [sem(f"wj_in{i}") for i in range(2)]
        gates_ps = sem("gates_ps")
        wide_ps = sem("wide_ps")
        sig_done = sem("sig_done")
        wide_done = sem("wide_done")
        merged_done = sem("merged_done")

        def row_jobs():
            mod = m["modT"]
            for g in range(GROUPS):
                yield late["gate1"][:, g, :], mod[:, 2 * KD:3 * KD, g], m["ones"][:, :], True, True
            for g in range(GROUPS):
                yield late["mul2row"][:, g, :], mul2[:, :, g], m["ones"][:, :], True, True
            for g in range(GROUPS):
                yield late["shift2"][:, g, :], mod[:, 3 * KD:4 * KD, g], m["ones"][:, :], True, True
            for g in range(GROUPS):
                yield m["gate2"][:, :], mod[:, 5 * KD:6 * KD, g], halfcols[:, g, :], g == 0, g == 1

        with nc.Block() as block:

            @block.sync
            def _(sp):
                w_in = a["w_in"].rearrange("a (k p) n -> p (a k) n", p=P)
                w_oa = a["w_oa"].rearrange("a (k p) n -> p (a k) n", p=P)
                w_ob = a["w_ob"].rearrange("a (k p) n -> p (a k) n", p=P)
                with sp.Fori(0, KD // 2) as jj:
                    for i in range(2):
                        sp.wait_ge(wide_ps, jj * JOBS if i == 0 else jj * JOBS)
                        col = jj * (2 * P) + i * P
                        sp.dma_start(wj[i][:, 0:KD, :], w_in[:, :, bass.ds(col + OFF_GA, P)]).then_inc(wj_in[i], 16)
                        sp.dma_start(wj[i][:, KD:2 * KD, :], w_in[:, :, bass.ds(col + OFF_GB, P)]).then_inc(wj_in[i], 16)
                        sp.dma_start(wj[i][:, 2 * KD:2 * KD + HA, :], w_oa[:, :, bass.ds(col, P)]).then_inc(wj_in[i], 16)
                        sp.dma_start(wj[i][:, 2 * KD + HA:3 * KD, :], w_ob[:, :, bass.ds(col, P)]).then_inc(wj_in[i], 16)
                sp.dma_start(late["wout"][:, :, :], a["w_out"].rearrange("a (k p) n -> p (a k) n", p=P)).then_inc(late["route_in"], 16)
                sp.dma_start(late["wr"][:, :, :], a["w_router"].rearrange("a (k p) n -> p (a k) n", p=P)).then_inc(late["route_in"], 16)

            @block.gpsimd
            def _(pool):
                pool.memset(halfcols[:, :, :], 0.0).then_inc(halfcols_done, 1)
                pool.wait_ge(halfcols_done, 1)
                for g in range(GROUPS):
                    pool.memset(halfcols[:, g, g * CAP:(g + 1) * CAP], 1.0).then_inc(halfcols_done, 1)
                with pool.Fori(0, KD // 2) as jj:
                    for r in range(JOBS):
                        i, g = divmod(r, GROUPS)
                        pool.wait_ge(wide_done, jj * 2 * JOBS + (2 * r + 2))
                        dst = late["mergedT"][:, :, :].rearrange("p k t -> p (k t)")[:, bass.ds(
                            jj * (2 * TOK) + (i * TOK + g * SEQ), SEQ)]
                        pool.tensor_tensor(dst, wide[:, g, 0, :], wide[:, g, 1, :], ALU.add).then_inc(merged_done, 1)

            @block.tensor
            def _(pe):
                pe.wait_ge(halfcols_done, 3)
                for r, (_, _, lhs, start, stop) in enumerate(row_jobs()):
                    pe.wait_ge(diag_done, r + 1)
                    if r >= 2:
                        pe.wait_ge(row_sb, r - 1)
                    bank = 2 * (r % 2) if r < 6 else 0
                    for c in range(2):
                        mm = pe.matmul(ps[:, bank + c, :], lhs, diag[:, r % 2, c * 4:(c + 1) * 4, :], start=start, stop=stop)
                    mm.then_inc(row_ps, 1)
                pe.wait_ge(row_sb, ROWS_OF - 1)
                with pe.Fori(0, KD // 2) as jj:
                    for r in range(JOBS):
                        i, g = divmod(r, GROUPS)
                        if g == 0:
                            pe.wait_ge(wj_in[i], (jj + 1) * 64)
                        pe.wait_ge(sig_done, jj * 2 * JOBS + 2 * max(r - 1, 0))
                        pe.wait_ge(wide_done, jj * 2 * JOBS + 2 * max(r - 1, 0))
                        cols = slice(g * SEQ, (g + 1) * SEQ)
                        for b in range(2):
                            for k in range(KD):
                                mm = pe.matmul(ps[:, 4 * g + b, :], wj[i][:, b * KD + k, :], m["hT"][:, k, cols],
                                               start=(k == 0), stop=(k == KD - 1))
                            mm.then_inc(gates_ps, 1)
                        for b, src in enumerate((m["oaT"], m["obT"])):
                            for k in range(HA):
                                mm = pe.matmul(ps[:, 4 * g + 2 + b, :], wj[i][:, 2 * KD + b * HA + k, :], src[:, k, cols],
                                               start=(k == 0), stop=(k == HA - 1))
                        mm.then_inc(wide_ps, 1)

            @block.scalar
            def _(act):
                with act.Fori(0, KD // 2) as jj:
                    for r in range(JOBS):
                        g = r % GROUPS
                        act.wait_ge(wide_done, jj * 2 * JOBS + 2 * max(r - 1, 0))
                        for b in range(2):
                            act.wait_ge(gates_ps, jj * 2 * JOBS + (2 * r + b + 1))
                            act.activation(sig[:, g, b, :], ps[:, 4 * g + b, :], ACT.Sigmoid).then_inc(sig_done, 1)

            @block.vector
            def _(dve):
                dve.scalar_tensor_tensor(out=mul2[:, :, :], in0=m["modT"][:, 4 * KD:5 * KD, :], scalar=1.0,
                                         in1=bcast(m["vecT"][:, VN2:VN2 + KD], 2, GROUPS),
                                         op0=ALU.add, op1=ALU.mult).then_inc(mul2_done, 1)
                dve.wait_ge(mul2_done, 1)
                jobs = list(row_jobs())
                for r in range(ROWS_OF + 1):
                    if r < ROWS_OF:
                        if r >= 2:
                            dve.wait_ge(row_ps, r - 1)
                        dve.tensor_tensor(diag[:, r % 2, :, :], bcast(m["ident"][:, :], 1, KD), bcast(jobs[r][1], 2, P),
                                          ALU.mult).then_inc(diag_done, 1)
                    if r >= 1:
                        v = r - 1
                        dve.wait_ge(row_ps, v + 1)
                        if v == 6:
                            continue
                        bank = 2 * (v % 2) if v < 6 else 0
                        dve.tensor_copy(jobs[v][0], ps[:, bank:bank + 2, :].rearrange("p b c -> p (b c)")).then_inc(row_sb, 1)
                with dve.Fori(0, KD // 2) as jj:
                    for r in range(JOBS):
                        g = r % GROUPS
                        dve.wait_ge(wide_ps, jj * JOBS + (r + 1))
                        dve.wait_ge(merged_done, jj * JOBS + max(r - 1, 0))
                        for b in range(2):
                            dve.wait_ge(sig_done, jj * 2 * JOBS + (2 * r + b + 1))
                            dve.tensor_tensor(wide[:, g, b, :], sig[:, g, b, :], ps[:, 4 * g + 2 + b, :],
                                              ALU.mult).then_inc(wide_done, 1)


def phase_route(nc, a, m, ps, late, x2_dram, h2_dram):
    NR = GROUPS * NE
    xt = m["hT"]
    with ExitStack() as ctx:
        def sb(name, shape, dt=F32):
            return ctx.enter_context(nc.sbuf_tensor(name, shape, dt))

        def sem(name):
            return ctx.enter_context(nc.semaphore(name))

        xm = sb("xm", [P, 2, D_MODEL])
        h2 = sb("h2", [P, 2, D_MODEL])
        junk = sb("junk_r", [P, D_MODEL])
        h2T = sb("h2T", [P, 2, KD, P])
        ssq = sb("ssq_r", [P, NT])
        ms = sb("ms_r", [P, NT])
        rinv = sb("rinv_r", [P, NT])
        negmax = sb("negmax", [P, NT])
        ex = sb("ex", [P, NT, NE])
        den = sb("den_r", [P, NT])
        rden = sb("rden_r", [P, NT])
        probs = sb("probs", [P, TPG, GROUPS, NE])
        work = sb("work", [NR, 2, SEQ])
        vals = sb("vals", [NR, CAP])
        idx = sb("idx", [NR, CAP], U32)
        idxf = sb("idxf", [NR, CAP])
        first = sb("first_token", [NR, 1])
        own = sb("own_half", [NR, GROUPS, CAP])
        pick = sb("pick", [NR, NE])
        spread = sb("spread", [NR, 2, GROUPS, CAP])

        xt_in = sem("xt_in")
        sel_const = sem("sel_const")
        out_ps = sem("out_ps")
        xm_done = sem("xm_done")
        x2_done = sem("x2_done")
        ssq_done = sem("ssq_done_r")
        ms_done = sem("ms_done_r")
        rinv_done = sem("rinv_done_r")
        hm_done = sem("hm_done")
        h2_done = sem("h2_done")
        x2_out = sem("x2_out")
        h2_out = [sem(f"h2_out{i}") for i in range(2)]
        h2T_ps = sem("h2T_ps")
        h2T_sb = sem("h2T_sb")
        logit_ps = sem("logit_ps")
        negmax_done = sem("negmax_done")
        ex_done = sem("ex_done")
        rden_done = sem("rden_done_r")
        probs_done = sem("probs_done")
        probsT_ps = sem("probsT_ps")
        top_step = sem("top_step")
        pick_ps = sem("pick_ps")

        with nc.Block() as block:

            @block.sync
            def _(sp):
                sp.dma_start(xt[:, :, :], a["x"].rearrange("(t p) c -> p t c", p=P)).then_inc(xt_in, 16)
                x2_v = x2_dram.rearrange("(t p) c -> t p c", p=P)
                h2_v = h2_dram.rearrange("(t p) c -> t p c", p=P)
                for t in range(NT):
                    sp.wait_ge(x2_done, t + 1)
                    sp.dma_start(x2_v[t], xt[:, t, :]).then_inc(x2_out, 16)
                    sp.wait_ge(h2_done, t + 1)
                    sp.dma_start(h2_v[t], h2[:, t % 2, :]).then_inc(h2_out[t % 2], 16)
                sp.wait_ge(x2_out, 16 * NT)
                for i in range(2):
                    sp.wait_ge(h2_out[i], 16 * NT // 2)

            @block.gpsimd
            def _(pool):
                st = Steps(pool, sel_const)
                st.did(pool.memset(first[:, :], float(SEQ)))
                st.did(pool.memset(own[:, :, :], 1.0))
                st.did(pool.memset(pick[:, :], 0.0))
                st.settle()
                st.did(pool.affine_select(out=first[:, :], in_=first[:, :], compare_op=ALU.is_ge, fill=0.0, base=-NE,
                                          pattern=[[1, 1]], channel_multiplier=1))
                st.did(pool.affine_select(out=own[:, 0, :], in_=own[:, 0, :], compare_op=ALU.is_ge, fill=0.0, base=NE - 1,
                                          pattern=[[0, CAP]], channel_multiplier=-1))
                st.did(pool.affine_select(out=own[:, 1, :], in_=own[:, 1, :], compare_op=ALU.is_ge, fill=0.0, base=-NE,
                                          pattern=[[0, CAP]], channel_multiplier=1))
                for g in range(GROUPS):
                    st.do(pool.affine_select(out=pick[:, :], in_=pick[:, :], compare_op=ALU.not_equal, fill=1.0,
                                             base=-g * NE, pattern=[[-1, NE]], channel_multiplier=1))
                pool.wait_ge(xt_in, 16)
                for t in range(NT):
                    g = t // TPG
                    pool.wait_ge(xm_done, t + 1)
                    pool.tensor_tensor(xt[:, t, :], xt[:, t, :], xm[:, t % 2, :], ALU.add).then_inc(x2_done, 1)
                    pool.wait_ge(ms_done, t + 1)
                    pool.tensor_tensor(rinv[:, t:t + 1], ms[:, t:t + 1], m["neghalf"][:, 0:1], ALU.pow).then_inc(rinv_done, 1)
                    pool.wait_ge(hm_done, t + 1)
                    pool.tensor_tensor(h2[:, t % 2, :], h2[:, t % 2, :], late["shift2"][:, g, :], ALU.add).then_inc(h2_done, 1)

            @block.tensor
            def _(pe):
                ident = m["ident"][:, :]
                pe.wait_ge(late["route_in"], 32)

                def project(t):
                    if t >= 2:
                        pe.wait_ge(xm_done, t - 1)
                    for c in range(2):
                        for k in range(KD):
                            mm = pe.matmul(ps[:, 2 * (t % 2) + c, :], late["mergedT"][:, k, t * P:(t + 1) * P],
                                           late["wout"][:, k, c * 512:(c + 1) * 512], start=(k == 0), stop=(k == KD - 1))
                    mm.then_inc(out_ps, 1)

                def route(t):
                    pe.wait_ge(h2_done, t + 1)
                    if t >= 1:
                        pe.wait_ge(h2T_sb, t)
                    for k in range(KD):
                        mm = pe.transpose(ps[:, 4 + k // 4, (k % 4) * P:(k % 4 + 1) * P],
                                          h2[:, t % 2, k * P:(k + 1) * P], ident)
                    mm.then_inc(h2T_ps, 1)

                def logits(t):
                    pe.wait_ge(h2T_sb, t + 1)
                    if t >= 2:
                        pe.wait_ge(ex_done, t - 1)
                    for k in range(KD):
                        mm = pe.matmul(ps[:, 6 + t % 2, 0:NE], h2T[:, t % 2, k, :], late["wr"][:, k, :],
                                       start=(k == 0), stop=(k == KD - 1))
                    mm.then_inc(logit_ps, 1)

                for t in range(NT + 2):
                    if t < NT:
                        project(t)
                    if 1 <= t <= NT:
                        route(t - 1)
                    if t >= 2:
                        logits(t - 2)
                for t in range(TPG):
                    pe.wait_ge(probs_done, TPG + t + 1)
                    mm = pe.transpose(ps[0:NR, 0, t * P:(t + 1) * P], probs[:, t, :, :].rearrange("p g e -> p (g e)"), ident)
                mm.then_inc(probsT_ps, 1)
                pe.wait_ge(top_step, 3 + 3 * (CAP // 8) + 1)
                for i in range(2):
                    mm = pe.matmul(ps[:, 1, i * NE:(i + 1) * NE], spread[:, i, :, :].rearrange("p g c -> p (g c)"), pick[:, :],
                                   start=True, stop=True)
                mm.then_inc(pick_ps, 1)

            @block.scalar
            def _(act):
                for t in range(NT + 1):
                    if t < NT:
                        act.wait_ge(x2_done, t + 1)
                        if t:
                            act.wait_ge(ssq_done, t)
                        act.activation(junk[:, :], xt[:, t, :], ACT.Square, accum_out=ssq[:, t:t + 1]).then_inc(ssq_done, 1)
                        act.wait_ge(h2T_ps, t + 1)
                        if t >= 2:
                            act.wait_ge(logit_ps, t - 1)
                        act.activation(h2T[:, t % 2, :, :], ps[:, 4:6, :].rearrange("p b (k c) -> p (b k) c", c=P),
                                       ACT.Copy).then_inc(h2T_sb, 1)
                    if t >= 1:
                        v = t - 1
                        act.wait_ge(negmax_done, v + 1)
                        act.activation(ex[:, v, :], ps[:, 6 + v % 2, 0:NE], ACT.Exp, bias=negmax[:, v:v + 1],
                                       accum_out=den[:, v:v + 1]).then_inc(ex_done, 1)

            @block.vector
            def _(dve):
                def softmax_tail(v):
                    dve.wait_ge(logit_ps, v + 1)
                    dve.tensor_reduce(negmax[:, v:v + 1], ps[:, 6 + v % 2, 0:NE], AX_X, ALU.max, negate=True).then_inc(negmax_done, 1)
                    dve.wait_ge(ex_done, v + 1)
                    dve.reciprocal(rden[:, v:v + 1], den[:, v:v + 1]).then_inc(rden_done, 1)
                    dve.wait_ge(rden_done, v + 1)
                    dve.tensor_scalar(probs[:, v % TPG, v // TPG, :], ex[:, v, :], rden[:, v:v + 1], None,
                                      ALU.mult).then_inc(probs_done, 1)

                for t in range(NT + 1):
                    if t < NT:
                        g = t // TPG
                        dve.wait_ge(out_ps, t + 1)
                        if t >= 2:
                            dve.wait_ge(x2_done, t - 1)
                        dve.tensor_tensor(xm[:, t % 2, :], ps[:, 2 * (t % 2):2 * (t % 2) + 2, :].rearrange("p b c -> p (b c)"),
                                          late["gate1"][:, g, :], ALU.mult).then_inc(xm_done, 1)
                        dve.wait_ge(ssq_done, t + 1)
                        dve.tensor_scalar(ms[:, t:t + 1], ssq[:, t:t + 1], 1.0 / D_MODEL, EPS, ALU.mult, ALU.add).then_inc(ms_done, 1)
                        dve.wait_ge(rinv_done, t + 1)
                        if t >= 2:
                            dve.wait_ge(h2_out[t % 2], 16 * (t // 2))
                            dve.wait_ge(h2T_ps, t - 1)
                        dve.scalar_tensor_tensor(out=h2[:, t % 2, :], in0=xt[:, t, :], scalar=rinv[:, t:t + 1],
                                                 in1=late["mul2row"][:, g, :], op0=ALU.mult, op1=ALU.mult).then_inc(hm_done, 1)
                    if t >= 1:
                        softmax_tail(t - 1)
                st = Steps(dve, top_step)
                dve.wait_ge(probsT_ps, 1)
                st.do(dve.tensor_copy(work[:, 0, :], ps[0:NR, 0, :]))
                for r in range(CAP // 8):
                    got = slice(8 * r, 8 * r + 8)
                    st.do(dve.max(vals[:, got], work[:, r % 2, :]))
                    st.did(dve.max_index(idx[:, got], vals[:, got], work[:, r % 2, :]))
                    st.do(dve.match_replace(work[:, 1 - r % 2, :], vals[:, got], work[:, r % 2, :], -1.0))
                dve.wait_ge(sel_const, 8)
                st.do(dve.tensor_scalar(idxf[:, :], idx[:, :], first[:, 0:1], None, ALU.add))
                st.did(dve.tensor_tensor(spread[:, 0, :, :], bcast(vals[:, :], 1, GROUPS), own[:, :, :], ALU.mult))
                st.do(dve.tensor_tensor(spread[:, 1, :, :], bcast(idxf[:, :], 1, GROUPS), own[:, :, :], ALU.mult))
                assert st.n == 3 + 3 * (CAP // 8) + 1
                dve.wait_ge(pick_ps, 1)
                st.did(dve.tensor_copy(m["gates"][:, :], ps[:, 1, 0:NE]))
                st.did(dve.tensor_copy(m["token"][:, 0:NE], ps[:, 1, NE:2 * NE]))
                st.did(dve.tensor_copy(m["token"][:, NE:NE + 1], ps[:, 1, NE:NE + 1]))
                st.settle()


def phase_experts(nc, a, m, ps, x2_dram, h2_dram):
    NQ4 = 4
    FW = D_EXPERT // NQ4
    FT = FW // P
    ORDER = [("g", 0), ("u", 0), ("g", 1), ("u", 1), ("d", 0), ("g", 2), ("u", 2), ("d", 1), ("g", 3), ("u", 3),
             ("d", 2), ("d", 3)]
    NP_ = len(ORDER)
    with ExitStack() as ctx:
        def sb(name, shape, dt=F32):
            return ctx.enter_context(nc.sbuf_tensor(name, shape, dt))

        def sem(name):
            return ctx.enter_context(nc.semaphore(name))

        wgt = {kind: [sb(f"w{kind}{i}", [P, KD * FW]) for i in range(2)] for kind in "gud"}
        tok_g = sb("tok_g", [P, 1], U32)
        tok_s = sb("tok_s", [P, 1], U32)
        gate = sb("gate_e", [P, 1])
        xe = sb("xe", [P, D_MODEL])
        xeT = sb("xeT", [P, KD, P])
        sg = sb("sg", [P, 2, FW])
        hid = sb("hid", [P, 2, FW])
        hidT = sb("hidT", [P, 2, FT, P])
        ye = sb("ye", [P, D_MODEL])

        w_in = {kind: [sem(f"w{kind}_in{i}") for i in range(2)] for kind in "gud"}
        piece_done = sem("piece_done")
        tok_ready = sem("tok_ready")
        xe_in = sem("xe_in")
        xeT_ps = sem("xeT_ps")
        xeT_sb = sem("xeT_sb")
        silu_done = sem("silu_done_e")
        hid_done = sem("hid_done")
        hidT_ps = sem("hidT_ps")
        hidT_sb = sem("hidT_sb")
        ye_done = sem("ye_done")
        gate_ready = sem("gate_ready")
        scattered = sem("scattered")
        gather_go = sem("gather_go")
        scatter_go = sem("scatter_go")
        pos = {piece: i for i, piece in enumerate(ORDER)}

        with nc.Block() as block:

            @block.sync
            def _(sp):
                wg = a["w_gate"].rearrange("a e (k p) n -> p (a e) k n", p=P)
                wu = a["w_up"].rearrange("a e (k p) n -> p (a e) k n", p=P)
                wd = a["w_down"].rearrange("a e (k p) n -> p (a e) k n", p=P)
                with sp.Fori(0, NE) as e:
                    for kind, n in ORDER:
                        if n >= 2:
                            sp.wait_ge(piece_done, e * NP_ + (NP_ + pos[kind, n - 2] + 1))
                        else:
                            sp.wait_ge(piece_done, e * NP_ + (pos[kind, n + 2] + 1))
                        if kind == "d":
                            src = wd[:, bass.ds(e, 1), n * FT:(n + 1) * FT, :].rearrange("p e k n -> p (e k) n")
                            dst = wgt[kind][n % 2][:, :].rearrange("p (k n) -> p k n", k=FT)
                        else:
                            src = (wg if kind == "g" else wu)[:, bass.ds(e, 1), :, n * FW:(n + 1) * FW].rearrange(
                                "p e k n -> p (e k) n")
                            dst = wgt[kind][n % 2][:, :].rearrange("p (k n) -> p k n", k=KD)
                        sp.dma_start(dst, src).then_inc(w_in[kind][n % 2], 16)

            @block.gpsimd
            def _(pool):
                def gather(e_tok, count):
                    pool.tensor_copy(tok_g[:, :], m["token"][:, e_tok]).then_inc(tok_ready, 1)
                    pool.wait_ge(tok_ready, count)
                    pool.sem_inc(gather_go, 1)
                    pool.indirect_dma_start(out=xe[:, :], out_offset=None, in_=h2_dram[:, :],
                                            in_offset=bass.IndirectOffsetOnAxis(ap=tok_g[:, 0:1], axis=0)).then_inc(xe_in, 16)

                gather(slice(0, 1), 1)
                with pool.Fori(0, NE) as e:
                    pool.wait_ge(xe_in, (e + 1) * 16)
                    pool.wait_ge(xeT_ps, e * 2 + 2)
                    gather(bass.ds(e + 1, 1), e * 2 + 2)
                    pool.wait_ge(scattered, e * 16)
                    pool.tensor_copy(gate[:, :], m["gates"][:, bass.ds(e, 1)]).then_inc(gate_ready, 1)
                    pool.tensor_copy(tok_s[:, :], m["token"][:, bass.ds(e, 1)]).then_inc(tok_ready, 1)
                    pool.wait_ge(tok_ready, e * 2 + 3)
                    pool.wait_ge(ye_done, e + 1)
                    pool.sem_inc(scatter_go, 1)
                    pool.indirect_dma_start(out=x2_dram[:, :], out_offset=bass.IndirectOffsetOnAxis(ap=tok_s[:, 0:1], axis=0),
                                            in_=ye[:, :], in_offset=None, compute_op=ALU.add).then_inc(scattered, 16)
                pool.wait_ge(scattered, NE * 16)
                pool.wait_ge(xe_in, (NE + 1) * 16)

            @block.tensor
            def _(pe):
                ident = m["ident"][:, :]
                pe.sem_inc(piece_done, NP_)

                def turn_tokens(half, count_in, count_sb):
                    pe.wait_ge(xe_in, count_in)
                    pe.wait_ge(xeT_sb, count_sb)
                    for k in range(4):
                        mm = pe.transpose(ps[:, 7, k * P:(k + 1) * P], xe[:, (4 * half + k) * P:(4 * half + k + 1) * P], ident)
                    mm.then_inc(xeT_ps, 1)

                turn_tokens(0, 16, 0)
                turn_tokens(1, 16, 1)
                with pe.Fori(0, NE) as e:
                    def arrived(kind, n):
                        pe.wait_ge(w_in[kind][n % 2], e * 32 + (n // 2 + 1) * 16)

                    for kind, n in ORDER:
                        arrived(kind, n)
                        if kind in "gu":
                            if kind == "g":
                                pe.wait_ge(xeT_sb, e * 2 + 2)
                            pe.wait_ge(silu_done if kind == "g" else hid_done, e * NQ4 + max(n - 1, 0))
                            w = wgt[kind][n % 2][:, :].rearrange("p (k n) -> p k n", k=KD)
                            for k in range(KD):
                                mm = pe.matmul(ps[:, 2 * (n % 2) + (kind == "u"), :], xeT[:, k, :], w[:, k, :],
                                               start=(k == 0), stop=(k == KD - 1))
                            mm.then_inc(piece_done, 1)
                        else:
                            pe.wait_ge(hid_done, e * NQ4 + n + 1)
                            pe.wait_ge(hidT_sb, e * NQ4 + n)
                            for f in range(FT):
                                mm = pe.transpose(ps[:, 4, f * P:(f + 1) * P], hid[:, n % 2, f * P:(f + 1) * P], ident)
                            mm.then_inc(hidT_ps, 1)
                            if n == 0:
                                pe.wait_ge(ye_done, e)
                            if n == 2:
                                turn_tokens(0, e * 16 + 32, e * 2 + 2)
                            if n == 3:
                                turn_tokens(1, e * 16 + 32, e * 2 + 3)
                            pe.wait_ge(hidT_sb, e * NQ4 + n + 1)
                            w = wgt[kind][n % 2][:, :].rearrange("p (k n) -> p k n", k=FT)
                            for c in range(2):
                                for f in range(FT):
                                    mm = pe.matmul(ps[:, 5 + c, :], hidT[:, n % 2, f, :], w[:, f, c * 512:(c + 1) * 512],
                                                   start=(n == 0 and f == 0), stop=(n == NQ4 - 1 and f == FT - 1))
                            mm.then_inc(piece_done, 1)

            @block.scalar
            def _(act):
                def turned(half, count):
                    act.wait_ge(xeT_ps, count)
                    act.activation(xeT[:, 4 * half:4 * half + 4, :], ps[:, 7, :], ACT.Copy).then_inc(xeT_sb, 1)

                turned(0, 1)
                turned(1, 2)
                with act.Fori(0, NE) as e:
                    def silu(n):
                        act.wait_ge(piece_done, e * NP_ + (NP_ + pos["g", n] + 1))
                        act.wait_ge(hid_done, e * NQ4 + max(n - 1, 0))
                        act.activation(sg[:, n % 2, :], ps[:, 2 * (n % 2), :], ACT.Silu).then_inc(silu_done, 1)

                    def hidden(n):
                        act.wait_ge(hidT_ps, e * NQ4 + n + 1)
                        act.activation(hidT[:, n % 2, :, :], ps[:, 4, :], ACT.Copy).then_inc(hidT_sb, 1)

                    silu(0)
                    silu(1)
                    hidden(0)
                    silu(2)
                    hidden(1)
                    silu(3)
                    hidden(2)
                    act.wait_ge(piece_done, e * NP_ + (NP_ + pos["u", 3] + 1))
                    turned(0, e * 2 + 3)
                    hidden(3)
                    turned(1, e * 2 + 4)

            @block.vector
            def _(dve):
                with dve.Fori(0, NE) as e:
                    for n in range(NQ4):
                        dve.wait_ge(piece_done, e * NP_ + (NP_ + pos["u", n] + 1))
                        dve.wait_ge(silu_done, e * NQ4 + n + 1)
                        dve.wait_ge(hidT_ps, e * NQ4 + max(n - 1, 0))
                        dve.tensor_tensor(hid[:, n % 2, :], sg[:, n % 2, :], ps[:, 2 * (n % 2) + 1, :], ALU.mult).then_inc(hid_done, 1)
                    dve.wait_ge(piece_done, e * NP_ + 2 * NP_)
                    dve.wait_ge(gate_ready, e + 1)
                    dve.wait_ge(scattered, e * 16)
                    dve.scalar_tensor_tensor(out=ye[:, :], in0=ps[:, 5:7, :].rearrange("p b c -> p (b c)"),
                                             scalar=gate[:, 0:1], in1=m["gate2"][:, :], op0=ALU.mult,
                                             op1=ALU.mult).then_inc(ye_done, 1)


def phase_finish(nc, a, m, x2_dram, y):
    with ExitStack() as ctx:
        def sb(name, shape, dt=F32):
            return ctx.enter_context(nc.sbuf_tensor(name, shape, dt))

        def sem(name):
            return ctx.enter_context(nc.semaphore(name))

        x3 = sb("x3", [P, NT, D_MODEL])
        fg = sb("fg", [P, D_MODEL])
        junk = sb("junk_f", [P, D_MODEL])
        ssq = sb("ssq_f", [P, NT])
        ms = sb("ms_f", [P, NT])
        rinv = sb("rinv_f", [P, NT])
        fg_in = sem("fg_in")
        x3_in = [sem(f"x3_in{t}") for t in range(NT)]
        ssq_done = sem("ssq_done_f")
        ms_done = sem("ms_done_f")
        rinv_done = sem("rinv_done_f")
        y_done = sem("y_done")
        y_out = sem("y_out")
        with nc.Block() as block:

            @block.sync
            def _(sp):
                sp.dma_start(fg[:, :], bass.AP(a["final_g"].tensor, 0, [[0, P], [1, D_MODEL]])).then_inc(fg_in, 16)
                x_v = x2_dram.rearrange("(t p) c -> t p c", p=P)
                y_v = y.rearrange("(t p) c -> t p c", p=P)
                for t in range(NT):
                    sp.dma_start(x3[:, t, :], x_v[t]).then_inc(x3_in[t], 16)
                for t in range(NT):
                    sp.wait_ge(y_done, t + 1)
                    sp.dma_start(y_v[t], x3[:, t, :]).then_inc(y_out, 16)
                sp.wait_ge(y_out, 16 * NT)

            @block.scalar
            def _(act):
                for t in range(NT):
                    act.wait_ge(x3_in[t], 16)
                    if t:
                        act.wait_ge(ssq_done, t)
                    act.activation(junk[:, :], x3[:, t, :], ACT.Square, accum_out=ssq[:, t:t + 1]).then_inc(ssq_done, 1)

            @block.gpsimd
            def _(pool):
                for t in range(NT):
                    pool.wait_ge(ms_done, t + 1)
                    pool.tensor_tensor(rinv[:, t:t + 1], ms[:, t:t + 1], m["neghalf"][:, 0:1], ALU.pow).then_inc(rinv_done, 1)

            @block.vector
            def _(dve):
                dve.wait_ge(fg_in, 16)
                for t in range(NT + 1):
                    if t < NT:
                        dve.wait_ge(ssq_done, t + 1)
                        dve.tensor_scalar(ms[:, t:t + 1], ssq[:, t:t + 1], 1.0 / D_MODEL, EPS, ALU.mult, ALU.add).then_inc(ms_done, 1)
                    if t >= 1:
                        v = t - 1
                        dve.wait_ge(rinv_done, v + 1)
                        dve.scalar_tensor_tensor(out=x3[:, v, :], in0=x3[:, v, :], scalar=rinv[:, v:v + 1], in1=fg[:, :],
                                                 op0=ALU.mult, op1=ALU.mult).then_inc(y_done, 1)


def build(nc, a, y):
    x2_dram = nc.dram_tensor("x2_dram", (TOK, D_MODEL), F32).ap()
    h2_dram = nc.dram_tensor("h2_dram", (TOK, D_MODEL), F32).ap()
    with ExitStack() as outer:
        ps = outer.enter_context(nc.psum_tensor("ps", [P, 8, 512], F32))
        m = {}
        for name, shape, dt in (("ident", [P, P], F32), ("neghalf", [P, 16], F32), ("gate2", [P, D_MODEL], F32),
                                ("gates", [P, NE], F32), ("token", [P, NE + 1], U32)):
            m[name] = outer.enter_context(nc.sbuf_tensor(name, shape, dt))
        with ExitStack() as front:
            m.update(shared_buffers(nc, front))
            phase_prepare(nc, a, m, ps)
            phase_deltanet(nc, a, m, ps)
            phase_attention(nc, a, m, ps)
            with ExitStack() as ctx:
                late = late_buffers(nc, ctx)
                phase_merge(nc, a, m, ps, late)
                phase_route(nc, a, m, ps, late, x2_dram, h2_dram)
        phase_experts(nc, a, m, ps, x2_dram, h2_dram)
        phase_finish(nc, a, m, x2_dram, y)


def kernel(**inputs):
    import numpy as np
    import concourse.bacc as bacc
    from concourse.bass_utils import run_bass_kernel_spmd as run

    nc = bacc.Bacc("TRN2", target_bir_lowering=False, num_devices=1)
    arrays = {n: np.ascontiguousarray(v) for n, v in inputs.items()
              if n not in ("x_prompt", "x_sample", "c_prompt", "c_sample", "rpb")}
    arrays["x"] = np.concatenate([inputs["x_prompt"][0], inputs["x_sample"][0]], axis=0)
    arrays["c"] = np.concatenate([inputs["c_prompt"], inputs["c_sample"]], axis=0)
    arrays["final_g"] = np.ascontiguousarray(inputs["final_g"]).reshape(1, D_MODEL)
    table = np.transpose(np.asarray(inputs["rpb"])[0], (0, 2, 1)).reshape(HB, RPB_C * RPB_R)
    arrays["rpb"] = np.stack([np.pad(table, ((0, 0), (RPB_FRONT + r, RPB_LEN + ROWS - RPB_FRONT - RPB_C * RPB_R - r)))
                              [:, :RPB_LEN] for r in range(ROWS)])
    a = {n: nc.dram_tensor(f"in_{n}", v.shape, mybir.dt.from_np(v.dtype), kind="ExternalInput").ap()
         for n, v in arrays.items()}
    y = nc.dram_tensor("out_y", (TOK, D_MODEL), F32, kind="ExternalOutput").ap()
    build(nc, a, y)
    r = run(nc, [{f"in_{n}": v for n, v in arrays.items()}], core_ids=[0])
    got = r.results[0]["out_y"]
    return got[None, :SEQ], got[None, SEQ:]
```

```python
from contextlib import ExitStack

import concourse.bass as bass
from concourse import mybir

F32 = mybir.dt.float32
F32R = mybir.dt.float32r
U32 = mybir.dt.uint32
ALU = mybir.AluOpType
ACT = mybir.ActivationFunctionType
AX_X = mybir.AxisListType.X

P = 128
D_MODEL = 1024
SEQ = 512
GROUPS = 2
TOK = GROUPS * SEQ
KD = D_MODEL // P
TPG = SEQ // P
NT = TOK // P
GRID_W = 64
ROWS = SEQ // GRID_W
HA = 4
DK = 128
CONV_K = 5
CHUNK = 64
NCHUNK = SEQ // CHUNK
HB = 8
DH = 64
PAIRS = HB * DH // P
WIN_ROWS = 8
WIN_COLS = 16
NE = 16
CAP = 2 * SEQ // NE
D_EXPERT = 2048
EPS = 1e-6
BIG = 1e30
A_W = HA * DK
OFF_Z = 3 * A_W
OFF_SMALL = 4 * A_W
OFF_QB = OFF_SMALL + 4 * HA
OFF_GA = OFF_QB + 3 * HB * DH
OFF_GB = OFF_GA + D_MODEL
ADA_BLOCK = 512
ADA_FIRST = 2 * D_MODEL // ADA_BLOCK
ADA_TILES = ADA_BLOCK // P
EARLY_TILES = (3 * HB * DH + 2 * D_MODEL) // P
GATE_TILE = 3 * HB * DH // P
BETA, CUM, ECUM, BECUM, EREST, LOGD, ETOT = range(7)
NQ = 8
VB, VN1, VN2, VC = 0, 48, 56, 64
VROWS = 80
CROWS = 12 * CONV_K + 1
LEVELS = 6
WCOLS = 48
RPB_C = 2 * WIN_COLS - 1
RPB_R = 2 * WIN_ROWS - 1
RPB_FRONT = 15 * RPB_R + 7 + 8
RPB_RUN = WCOLS * RPB_R
RPB_LEN = RPB_FRONT + RPB_RUN
KEY_TILES = [(0, 2), (0, 3), (1, 4), (2, 4)]


class Steps:

    def __init__(self, eng, sem, before=0):
        self.eng, self.sem, self.before, self.n = eng, sem, before, 0

    def did(self, ins):
        ins.then_inc(self.sem, 1)
        self.n += 1

    def settle(self):
        self.eng.wait_ge(self.sem, self.before + self.n)

    def do(self, ins):
        self.did(ins)
        self.settle()


def bcast(ap, axis, n):
    ap = ap.unsqueeze(axis)
    shape = list(ap.shape)
    shape[axis] = n
    return ap.to_broadcast(shape)


def prime(eng, *sems):
    for sem in sems:
        eng.sem_inc(sem, 1)


def shared_buffers(nc, ctx):
    def sb(name, shape, dt=F32):
        return ctx.enter_context(nc.sbuf_tensor(name, shape, dt))

    m = {}
    m["ones"] = sb("ones", [P, P])
    m["upto"] = sb("upto", [P, 2, P])
    m["vecT"] = sb("vecT", [P, VROWS])
    m["convT"] = sb("convT", [P, CROWS])
    m["modT"] = sb("modT", [P, 48, GROUPS])
    m["sc"] = sb("sc", [P, KD, GROUPS])
    m["hT"] = sb("hT", [P, KD, TOK])
    m["oaT"] = sb("oaT", [P, HA, TOK])
    m["obT"] = sb("obT", [P, PAIRS, TOK])
    m["tab"] = sb("tab", [P, NQ, NT, 2 * HA])
    return m


def phase_prepare(nc, a, m, ps):
    with ExitStack() as ctx:
        def sb(name, shape, dt=F32):
            return ctx.enter_context(nc.sbuf_tensor(name, shape, dt))

        def sem(name):
            return ctx.enter_context(nc.semaphore(name))

        rows = sb("rows", [VROWS, P])
        crows = sb("crows", [CROWS, P])
        ada = sb("ada", [P, ADA_FIRST, KD, ADA_BLOCK])
        xt = sb("xt", [P, NT, D_MODEL])
        junk = sb("junk", [P, D_MODEL])
        wsm = sb("wsm", [P, KD, 4 * HA])
        alog = sb("alog", [P, 2 * HA])
        dtb = sb("dtb", [P, 2 * HA])
        ealog = sb("ealog", [P, 2 * HA])
        ssq = sb("ssq", [P, NT])
        ms = sb("ms", [P, NT])
        rinv = sb("rinv", [P, NT])
        mul1 = sb("mul1", [P, KD, GROUPS])
        al = sb("al", [P, NT, 2 * HA])
        nal = sb("nal", [P, NT, 2 * HA])
        sp1 = sb("sp1", [P, NT, 2 * HA])
        eb = sb("eb", [P, NT, 2 * HA])
        rest = sb("rest", [P, NT, 2 * HA])
        same = sb("same", [P, P])
        half = sb("half", [P, 2, P])
        tab = m["tab"]

        vec_in = sem("vec_in")
        ada_in = [sem(f"ada_in{i}") for i in range(ADA_FIRST)]
        x_in = [sem(f"x_in{g}") for g in range(GROUPS)]
        small_in = sem("small_in")
        pool_step = sem("pool_step_a")
        dve_step = sem("dve_step_a")
        consts = sem("consts")
        vec_ps = sem("vec_ps")
        vec_sb = sem("vec_sb")
        mod_ps = sem("mod_ps")
        mul_ready = sem("mul_ready")
        ssq_done = sem("ssq_done")
        ms_done = sem("ms_done")
        rinv_done = sem("rinv_done")
        xn_done = sem("xn_done")
        xT_ps = sem("xT_ps")
        hT_act = sem("hT_act")
        hT_dve = sem("hT_dve")
        small_ps = sem("small_ps")
        al_done = sem("al_done")
        nal_done = sem("nal_done")
        act_step = sem("act_step_a")
        logd_done = sem("logd_done")
        cum_ps = sem("cum_ps")
        cum_sb = sem("cum_sb")

        with nc.Block() as block:

            @block.sync
            def _(sp):
                for dst, src in (
                    (rows[VB:VB + 48, :], a["b_ada"].rearrange("a (r c) -> (a r) c", c=P)),
                    (rows[VN1:VN1 + 8, :], a["norm1_g"].rearrange("a (r c) -> (a r) c", c=P)),
                    (rows[VN2:VN2 + 8, :], a["norm2_g"].rearrange("a (r c) -> (a r) c", c=P)),
                    (rows[VC:VC + 16, :], a["c"].rearrange("a (r c) -> (a r) c", c=P)),
                    (crows[0:60, :], a["conv_w"].rearrange("a t (r c) -> (a t r) c", c=P)),
                    (crows[60:61, :], a["gn_w"]),
                ):
                    sp.dma_start(dst, src).then_inc(vec_in, 16)
                x_v = a["x"].rearrange("(t p) c -> p t c", p=P)
                w_ada = a["w_ada"].rearrange("a (k p) n -> p (a k) n", p=P)
                for g in range(GROUPS):
                    sp.dma_start(xt[:, g * TPG:(g + 1) * TPG, :], x_v[:, g * TPG:(g + 1) * TPG, :]).then_inc(x_in[g], 16)
                    for b in (2 * g, 2 * g + 1):
                        sp.dma_start(ada[:, b, :, :], w_ada[:, :, b * ADA_BLOCK:(b + 1) * ADA_BLOCK]).then_inc(ada_in[b], 16)
                w_in = a["w_in"].rearrange("a (k p) n -> p (a k) n", p=P)
                sp.dma_start(wsm[:, :, :], w_in[:, :, OFF_SMALL:OFF_SMALL + 4 * HA]).then_inc(small_in, 16)
                sp.dma_start(alog[:, :], bass.AP(a["a_log"].tensor, 0, [[0, P], [1, 2 * HA]])).then_inc(small_in, 16)
                sp.dma_start(dtb[:, :], bass.AP(a["dt_bias"].tensor, 0, [[0, P], [1, 2 * HA]])).then_inc(small_in, 16)

            @block.gpsimd
            def _(pool):
                st = Steps(pool, pool_step)
                st.did(pool.memset(m["ident"][:, :], 0.0))
                st.did(pool.memset(m["ones"][:, :], 1.0))
                st.did(pool.memset(m["neghalf"][:, :], -0.5))
                st.did(pool.memset(m["upto"][:, :, :], 1.0))
                st.did(pool.memset(same[:, :], 0.0))
                st.did(pool.memset(half[:, :, :], 0.0))
                st.settle()
                pool.affine_select(out=m["ident"][:, :], in_=m["ident"][:, :], compare_op=ALU.not_equal, fill=1.0,
                                   base=0, pattern=[[-1, P]], channel_multiplier=1).then_inc(consts, 1)
                for d, sign in ((0, 1), (1, -1)):
                    st.did(pool.affine_select(out=m["upto"][:, d, :], in_=m["upto"][:, d, :], compare_op=ALU.is_ge,
                                              fill=0.0, base=0, pattern=[[sign, P]], channel_multiplier=-sign))
                st.settle()
                st.did(pool.memset(m["upto"][0:CHUNK, 0, CHUNK:P], 0.0))
                st.did(pool.memset(m["upto"][CHUNK:P, 1, 0:CHUNK], 0.0))
                for c in range(2):
                    own = slice(c * CHUNK, (c + 1) * CHUNK)
                    st.did(pool.memset(same[own, own], 1.0))
                    st.did(pool.memset(half[own, c, :], 1.0))
                st.settle()
                pool.sem_inc(consts, 1)
                pool.wait_ge(ms_done, 1)
                pool.tensor_tensor(rinv[:, :], ms[:, :], m["neghalf"][:, 0:NT], ALU.pow).then_inc(rinv_done, 1)

            @block.tensor
            def _(pe):
                pe.wait_ge(vec_in, 96)
                pe.wait_ge(consts, 1)
                pe.transpose(ps[:, 0, 0:VROWS], rows[:, :], m["ident"][0:VROWS, 0:VROWS])
                pe.transpose(ps[:, 0, P:P + CROWS], crows[:, :], m["ident"][0:CROWS, 0:CROWS]).then_inc(vec_ps, 1)
                pe.wait_ge(vec_sb, 3)
                for b in range(ADA_FIRST):
                    pe.wait_ge(ada_in[b], 16)
                    for j in range(ADA_TILES):
                        c = 2 * (b * ADA_TILES + j)
                        for k in range(KD):
                            mm = pe.matmul(ps[:, 1, c:c + 2], ada[:, b, k, j * P:(j + 1) * P], m["sc"][:, k, :],
                                           start=(k == 0), stop=(k == KD - 1))
                mm.then_inc(mod_ps, 1)
                for n in range(GROUPS * KD):
                    g, k = divmod(n, KD)
                    if k == 0:
                        pe.wait_ge(xn_done, TPG * (g + 1))
                    if n >= 6:
                        pe.wait_ge(hT_dve if n % 2 == 0 else hT_act, (n - 6) // 2 + 1)
                    for t in range(TPG):
                        mm = pe.transpose(ps[:, 2 + n % 6, t * P:(t + 1) * P], xt[:, g * TPG + t, k * P:(k + 1) * P],
                                          m["ident"][:, :])
                    mm.then_inc(xT_ps, 1)
                pe.wait_ge(hT_dve, KD)
                pe.wait_ge(hT_act, KD)
                pe.wait_ge(small_in, 48)
                for t in range(NT):
                    for k in range(KD):
                        mm = pe.matmul(ps[:, 0, t * 16:(t + 1) * 16], m["hT"][:, k, t * P:(t + 1) * P], wsm[:, k, :],
                                       start=(k == 0), stop=(k == KD - 1))
                mm.then_inc(small_ps, 1)
                pe.wait_ge(logd_done, 1)
                pe.wait_ge(consts, 2)
                logd = tab[:, LOGD, :, :]
                for d in range(2):
                    pe.matmul(ps[:, 1, 32 * d:32 * d + 32], m["upto"][:, d, :], logd[:, :, d * HA:(d + 1) * HA],
                              start=True, stop=True)
                pe.matmul(ps[:, 1, 64:128], same[:, :], logd, start=True, stop=True)
                for c in range(2):
                    mm = pe.matmul(ps[:, 1, 128 + 64 * c:192 + 64 * c], half[:, c, :], logd, start=True, stop=True)
                mm.then_inc(cum_ps, 1)

            @block.scalar
            def _(act):
                st = Steps(act, act_step)
                act.wait_ge(vec_ps, 1)
                act.activation(m["vecT"][:, :], ps[:, 0, 0:VROWS], ACT.Copy).then_inc(vec_sb, 1)
                act.activation(m["convT"][:, :], ps[:, 0, P:P + CROWS], ACT.Copy).then_inc(vec_sb, 1)
                act.activation(m["sc"][:, :, :], ps[:, 0, VC:VC + 16].rearrange("p (g k) -> p k g", g=GROUPS),
                               ACT.Silu).then_inc(vec_sb, 1)
                for t in range(NT):
                    if t % TPG == 0:
                        act.wait_ge(x_in[t // TPG], 16)
                    if t:
                        act.wait_ge(ssq_done, t)
                    act.activation(junk[:, :], xt[:, t, :], ACT.Square, accum_out=ssq[:, t:t + 1]).then_inc(ssq_done, 1)
                act.wait_ge(mul_ready, 2)
                for n in range(1, GROUPS * KD, 2):
                    g, k = divmod(n, KD)
                    act.wait_ge(xT_ps, n + 1)
                    act.activation(m["hT"][:, k, g * SEQ:(g + 1) * SEQ], ps[:, 2 + n % 6, :], ACT.Identity,
                                   bias=m["modT"][:, k, g:g + 1], scale=mul1[:, k, g:g + 1]).then_inc(hT_act, 1)
                act.wait_ge(small_in, 48)
                st.did(act.activation(ealog[:, :], alog[:, :], ACT.Exp))
                small = ps[:, 0, 0:P].rearrange("p (t c) -> p t c", t=NT)
                act.wait_ge(al_done, 1)
                st.did(act.activation(eb[:, :, :], small[:, :, 0:2 * HA], ACT.Exp, scale=-1.0))
                act.activation(nal[:, :, :], nal[:, :, :], ACT.Exp).then_inc(nal_done, 1)
                act.wait_ge(al_done, 2)
                act.activation(sp1[:, :, :], sp1[:, :, :], ACT.Ln).then_inc(nal_done, 1)
                act.wait_ge(cum_sb, 1)
                for d in range(2):
                    act.activation(tab[:, ECUM, :, d * HA:(d + 1) * HA],
                                   ps[:, 1, 32 * d:32 * d + 32].rearrange("p (t h) -> p t h", t=NT),
                                   ACT.Exp).then_inc(act_step, 1)
                act.activation(tab[:, ETOT:ETOT + 2, :, :],
                               ps[:, 1, 128:256].rearrange("p (c t h) -> p c t h", c=2, t=NT), ACT.Exp).then_inc(act_step, 1)
                act.activation(tab[:, EREST, :, :], rest[:, :, :], ACT.Exp).then_inc(act_step, 1)

            @block.vector
            def _(dve):
                st = Steps(dve, dve_step)
                dve.wait_ge(ssq_done, NT)
                dve.tensor_scalar(ms[:, :], ssq[:, :], 1.0 / D_MODEL, EPS, ALU.mult, ALU.add).then_inc(ms_done, 1)
                dve.wait_ge(rinv_done, 1)
                for t in range(NT):
                    dve.tensor_scalar(xt[:, t, :], xt[:, t, :], rinv[:, t:t + 1], None, ALU.mult).then_inc(xn_done, 1)
                dve.wait_ge(mod_ps, 1)
                dve.wait_ge(vec_sb, 2)
                n1 = 2 * KD
                dve.tensor_tensor(m["modT"][:, 0:n1, :], ps[:, 1, 0:2 * n1].rearrange("p (j g) -> p j g", g=GROUPS),
                                  bcast(m["vecT"][:, VB:VB + n1], 2, GROUPS), ALU.add).then_inc(mul_ready, 1)
                dve.wait_ge(mul_ready, 1)
                dve.scalar_tensor_tensor(out=mul1[:, :, :], in0=m["modT"][:, KD:n1, :], scalar=1.0,
                                         in1=bcast(m["vecT"][:, VN1:VN1 + 8], 2, GROUPS),
                                         op0=ALU.add, op1=ALU.mult).then_inc(mul_ready, 1)
                dve.wait_ge(mul_ready, 2)
                for n in range(0, GROUPS * KD, 2):
                    g, k = divmod(n, KD)
                    dve.wait_ge(xT_ps, n + 1)
                    dve.tensor_scalar(m["hT"][:, k, g * SEQ:(g + 1) * SEQ], ps[:, 2 + n % 6, :],
                                      mul1[:, k, g:g + 1], m["modT"][:, k, g:g + 1], ALU.mult, ALU.add).then_inc(hT_dve, 1)
                dve.wait_ge(small_ps, 1)
                dve.wait_ge(small_in, 48)
                small = ps[:, 0, 0:P].rearrange("p (t c) -> p t c", t=NT)
                st.do(dve.tensor_tensor(al[:, :, :], small[:, :, 2 * HA:4 * HA], bcast(dtb[:, :], 1, NT), ALU.add))
                dve.scalar_tensor_tensor(out=nal[:, :, :], in0=al[:, :, :], scalar=-1.0, in1=al[:, :, :],
                                         op0=ALU.mult, op1=ALU.min).then_inc(al_done, 1)
                dve.wait_ge(nal_done, 1)
                dve.tensor_scalar(sp1[:, :, :], nal[:, :, :], 1.0, None, ALU.add).then_inc(al_done, 1)
                dve.wait_ge(nal_done, 2)
                st.do(dve.scalar_tensor_tensor(out=al[:, :, :], in0=al[:, :, :], scalar=0.0, in1=sp1[:, :, :],
                                               op0=ALU.max, op1=ALU.add))
                dve.wait_ge(act_step, 2)
                dve.scalar_tensor_tensor(out=tab[:, LOGD, :, :], in0=al[:, :, :], scalar=-1.0,
                                         in1=bcast(ealog[:, :], 1, NT), op0=ALU.mult, op1=ALU.mult).then_inc(logd_done, 1)
                st.do(dve.tensor_scalar(eb[:, :, :], eb[:, :, :], 1.0, None, ALU.add))
                st.do(dve.reciprocal(tab[:, BETA, :, :], eb[:, :, :]))
                dve.wait_ge(cum_ps, 1)
                for d in range(2):
                    st.did(dve.tensor_copy(tab[:, CUM, :, d * HA:(d + 1) * HA],
                                           ps[:, 1, 32 * d:32 * d + 32].rearrange("p (t h) -> p t h", t=NT)))
                st.settle()
                dve.tensor_tensor(rest[:, :, :], ps[:, 1, 64:128].rearrange("p (t h) -> p t h", t=NT),
                                  tab[:, CUM, :, :], ALU.subtract).then_inc(cum_sb, 1)
                dve.wait_ge(act_step, 5)
                st.do(dve.tensor_tensor(tab[:, BECUM, :, :], tab[:, BETA, :, :], tab[:, ECUM, :, :], ALU.mult))


def phase_deltanet(nc, a, m, ps, early_dram):
    NPROJ = 4 * GROUPS
    ETILES = EARLY_TILES // HA
    EUNITS = ETILES * GROUPS // 2
    with ExitStack() as ctx:
        def sb(name, shape, dt=F32):
            return ctx.enter_context(nc.sbuf_tensor(name, shape, dt))

        sems = []

        def sem(name):
            sems.append(nc.alloc_semaphore(name))
            return sems[-1]

        w4 = sb("w4", [P, 4, KD, P])
        ada = sb("ada_d", [P, KD, ADA_BLOCK])
        posmask = sb("posmask", [P, 2, P])
        levelmask = sb("levelmask", [P, 2, LEVELS, P])
        pre = sb("pre", [P, 2, SEQ + CONV_K - 1])
        conv = sb("conv", [P, 3, GROUPS, SEQ])
        zT = sb("zT", [P, GROUPS, SEQ])
        cw = sb("cw", [P, CONV_K * 3])
        hd = sb("hd", [P, NQ, NT, 2])
        junk = sb("junk_d", [P, P])
        ssqk = sb("ssqk", [P, 2 * TPG])
        msqk = sb("msqk", [P, 2 * TPG])
        rqk = sb("rqk", [P, 2 * TPG])
        qn = sb("qn", [P, TPG, P])
        kn = sb("kn", [P, TPG, P])
        qnT = sb("qnT", [P, TPG, P])
        knT = sb("knT", [P, TPG, P])
        vb = [sb(f"vb{d}", [P, TPG, P]) for d in range(2)]
        kbe = [sb(f"kbe{d}", [P, TPG, P]) for d in range(2)]
        kd = [sb(f"kd{d}", [P, TPG, P]) for d in range(2)]
        qe = [sb(f"qe{d}", [P, TPG, P]) for d in range(2)]
        qeT = [sb(f"qeT{d}", [P, TPG, P]) for d in range(2)]
        gsum = [sb(f"gsum{d}", [P, TPG, P]) for d in range(2)]
        dec = [sb(f"dec{d}", [P, TPG, P]) for d in range(2)]
        xb = [sb(f"xb{d}", [P, TPG, P]) for d in range(2)]
        xbT = [sb(f"xbT{d}", [P, TPG, P]) for d in range(2)]
        qkT = [sb(f"qkT{d}", [P, TPG, P]) for d in range(2)]
        inv = [sb(f"inv{d}", [P, 2, TPG, P]) for d in range(2)]
        vnew = [sb(f"vnew{d}", [P, TPG, P]) for d in range(2)]
        state = [sb(f"state{d}", [P, NCHUNK, P]) for d in range(2)]
        ssqo = sb("ssqo", [P, TPG])
        mso = sb("mso", [P, TPG])
        ro = sb("ro", [P, TPG])
        on = sb("on", [P, TPG, P])

        spare = m["obT"][:, :, :].rearrange("p h t -> p (h t)")
        we = [spare[:, i * D_MODEL:(i + 1) * D_MODEL].rearrange("p (k c) -> p k c", k=KD) for i in range(2)]
        est = [spare[:, 2 * D_MODEL + i * SEQ:2 * D_MODEL + (i + 1) * SEQ] for i in range(GROUPS)]

        w_in_ready = sem("w_in_ready")
        we_in = [sem(f"we_in{i}") for i in range(2)]
        early_ps = sem("early_ps")
        early_sb = sem("early_sb")
        early_out = [sem(f"early_out{g}") for g in range(GROUPS)]
        ada_in = sem("ada_in_d")
        masks = sem("masks_d")
        posmask_done = sem("posmask_done")
        pool_step = sem("pool_step_d")
        dve_step = sem("dve_step_d")
        hd_ready = sem("hd_ready")
        proj_ps = sem("proj_ps")
        proj_read = sem("proj_read")
        conv_done = sem("conv_done")
        silu_done = sem("silu_done")
        mod_ps = sem("mod_ps_d")
        mod_done = sem("mod_done_d")
        tok_ps = sem("tok_ps")
        sq_done = sem("sq_done")
        ms_done = sem("ms_done_d")
        rqk_done = sem("rqk_done")
        qn_done = sem("qn_done")
        kn_done = sem("kn_done")
        vb_done = sem("vb_done")
        chn_ps = sem("chn_ps")
        chn_sb = sem("chn_sb")
        gsum_done = sem("gsum_done")
        row_ps = [sem(f"row_ps{d}") for d in range(2)]
        diff_done = [sem(f"diff_done{d}") for d in range(2)]
        dec_done = [sem(f"dec_done{d}") for d in range(2)]
        qe_done = sem("qe_done")
        qeT_ps = sem("qeT_ps")
        qeT_sb = sem("qeT_sb")
        gram_ps = sem("gram_ps")
        x_done = [sem(f"x_done{d}") for d in range(2)]
        xT_ps = [sem(f"xT_ps_d{d}") for d in range(2)]
        xT_sb = [sem(f"xT_sb_d{d}") for d in range(2)]
        kbe_done = sem("kbe_done")
        inv0_done = [sem(f"inv0_done{d}") for d in range(2)]
        y_ps = [sem(f"y_ps{d}") for d in range(2)]
        y_sb = [sem(f"y_sb{d}") for d in range(2)]
        upd_ps = [sem(f"upd_ps{d}") for d in range(2)]
        inv_done = [sem(f"inv_done{d}") for d in range(2)]
        uw_ps = [sem(f"uw_ps{d}") for d in range(2)]
        uw_sb = [sem(f"uw_sb{d}") for d in range(2)]
        ws_ps = [sem(f"ws_ps{d}") for d in range(2)]
        vnew_done = [sem(f"vnew_done{d}") for d in range(2)]
        kv_ps = [sem(f"kv_ps{d}") for d in range(2)]
        state_done = [sem(f"state_done{d}") for d in range(2)]
        o_ps = sem("o_ps")
        osq_done = sem("osq_done")
        mso_done = sem("mso_done")
        ro_done = sem("ro_done")
        on_done = sem("on_done")
        oT_ps = sem("oT_ps")
        oa_done = sem("oa_done")

        LV = LEVELS - 1
        NC1 = NCHUNK - 1
        FILL = (0, 1)
        D_STEPS = 1 + 3 * GROUPS * (CONV_K - 1)

        def chunks(d):
            return range(NCHUNK) if d == 0 else range(NCHUNK - 1, -1, -1)

        def place(c):
            return c // 2, slice(CHUNK * (c % 2), CHUNK * (c % 2) + CHUNK)

        early_v = early_dram.rearrange("(w p) t -> p w t", p=P)
        with nc.Block() as block:

            @block.sync
            def _(sp):
                w_in = a["w_in"].rearrange("a (k p) n -> p (a k) n", p=P)
                w_ada = a["w_ada"].rearrange("a (k p) n -> p (a k) n", p=P)
                with sp.Fori(0, HA) as h:
                    sp.wait_ge(proj_ps, 1 + h * NPROJ)
                    for b in range(4):
                        sp.dma_start(w4[:, b, :, :], w_in[:, :, bass.ds(h * P + b * A_W, P)]).then_inc(w_in_ready, 16)

                    def early_weights(i):
                        sp.wait_ge(early_ps, 1 + h * (GROUPS * ETILES) + GROUPS * max(i - 1, 0))
                        sp.dma_start(we[i % 2][:, :, :], w_in[:, :, bass.ds(h * (ETILES * P) + (OFF_QB + i * P), P)]).then_inc(
                            we_in[i % 2], 16)

                    early_weights(0)
                    early_weights(1)
                    for b in range(2):
                        sp.wait_ge(mod_ps, 1 + 2 * h + b)
                        sp.dma_start(ada[:, :, :], w_ada[:, :, bass.ds(h * (2 * ADA_BLOCK) + (ADA_FIRST + b) * ADA_BLOCK,
                                                                       ADA_BLOCK)]).then_inc(ada_in, 16)
                    for i in range(2, ETILES):
                        early_weights(i)

            @block.gpsimd
            def _(pool):
                st = Steps(pool, pool_step)
                st.did(pool.memset(levelmask[:, :, :, :], 0.0))
                st.settle()
                for d in range(2):
                    for lv in range(LEVELS):
                        s = 2 ** lv
                        part = levelmask[:, d, lv, :].rearrange("p (b u s) -> p b u s", u=2, s=s)[:, :, d, :]
                        st.do(pool.memset(part, 1.0))
                        lo = s if d == 0 else 0
                        pat = [[-2 * s, P // (2 * s)], [0, s]]
                        st.do(pool.affine_select(out=part, in_=part, compare_op=ALU.is_ge, fill=0.0, base=-lo,
                                                 pattern=pat, channel_multiplier=1))
                        st.do(pool.affine_select(out=part, in_=part, compare_op=ALU.is_ge, fill=0.0, base=lo + s - 1,
                                                 pattern=[[2 * s, P // (2 * s)], [0, s]], channel_multiplier=-1))
                st.did(pool.memset(pre[:, :, 0:2], 0.0))
                st.did(pool.memset(pre[:, :, SEQ + 2:SEQ + 4], 0.0))
                st.settle()
                pool.sem_inc(masks, 1)

                with pool.Fori(0, HA) as h:
                    for g in range(GROUPS):
                        n = h * GROUPS + g
                        tiles = slice(g * TPG, (g + 1) * TPG)
                        if g == 0:
                            pool.wait_ge(hd_ready, h + 1)
                        for d in range(2):
                            if g == 1:
                                pool.wait_ge(row_ps[d], n)
                            pool.tensor_tensor(gsum[d][:, :, :], bcast(m["upto"][:, d, :], 1, TPG),
                                               bcast(hd[:, LOGD, tiles, d], 2, P), ALU.mult).then_inc(gsum_done, 1)
                        pool.wait_ge(ms_done, n + 1)
                        pool.tensor_tensor(rqk[:, :], msqk[:, :], m["neghalf"][:, 0:2 * TPG], ALU.pow).then_inc(rqk_done, 1)
                        pool.wait_ge(qn_done, n + 1)
                        for d in range(2):
                            pool.tensor_tensor(qe[d][:, :, :], qn[:, :, :], bcast(hd[:, ECUM, tiles, d], 2, P),
                                               ALU.mult).then_inc(qe_done, 1)
                        pool.wait_ge(kn_done, n + 1)
                        for d in range(2):
                            pool.tensor_tensor(kbe[d][:, :, :], kn[:, :, :], bcast(hd[:, BECUM, tiles, d], 2, P),
                                               ALU.mult).then_inc(kbe_done, 1)
                            pool.tensor_tensor(kd[d][:, :, :], kn[:, :, :], bcast(hd[:, EREST, tiles, d], 2, P),
                                               ALU.mult).then_inc(kbe_done, 1)
                        for d in range(2):
                            pool.wait_ge(x_done[d], 2 * n + 2)
                            pool.wait_ge(xT_sb[d], 2 * n + 1)
                            for side, src in enumerate((xb[d], xbT[d])):
                                pool.tensor_tensor(inv[d][:, side, :, :], src[:, :, :],
                                                   bcast(levelmask[:, (d + side) % 2, 0, :], 1, TPG),
                                                   ALU.mult).then_inc(inv0_done[d], 1)
                            pool.wait_ge(inv0_done[d], 4 * n + 2)
                            for side in range(2):
                                pool.tensor_tensor(inv[d][:, side, :, :], bcast(m["ident"][:, :], 1, TPG),
                                                   inv[d][:, side, :, :], ALU.subtract).then_inc(inv0_done[d], 1)
                        pool.wait_ge(mso_done, n + 1)
                        pool.tensor_tensor(ro[:, :], mso[:, :], m["neghalf"][:, 0:TPG], ALU.pow).then_inc(ro_done, 1)

            @block.tensor
            def _(pe):
                ident = m["ident"][:, :]
                prime(pe, proj_ps, mod_ps, early_ps)
                with pe.Fori(0, HA) as h:
                    early = iter(range(GROUPS * EUNITS * KD))

                    def fill(products):
                        for _ in range(products):
                            unit, k = divmod(next(early), KD)
                            i, u = divmod(unit, GROUPS)
                            if k == 0:
                                slot_loads = (ETILES + 1 - i % 2) // 2
                                pe.wait_ge(we_in[i % 2], h * (16 * slot_loads) + (i // 2 + 1) * 16)
                                pe.wait_ge(early_sb, 1 + h * (GROUPS * ETILES) + unit)
                                if unit == 0:
                                    pe.wait_ge(mod_done, 1 + 2 * h + 2)
                            mm = pe.matmul(ps[:, 2, :], we[i % 2][:, k, :], m["hT"][:, k, u * SEQ:(u + 1) * SEQ],
                                           start=(k == 0), stop=(k == KD - 1))
                            if k == KD - 1:
                                mm.then_inc(early_ps, 1)

                    pe.wait_ge(w_in_ready, (h + 1) * 64)
                    for u in range(NPROJ):
                        b, g = divmod(u, GROUPS)
                        if u < 2:
                            pe.wait_ge(proj_read, 1 + h * NPROJ)
                            pe.wait_ge(oa_done, 1 + h * GROUPS)
                            pe.wait_ge(uw_sb[1], 1 + h * 2 * GROUPS)
                        else:
                            pe.wait_ge(proj_read, 1 + h * NPROJ + (u - 1))
                        for k in range(KD):
                            mm = pe.matmul(ps[:, u % 2, :], w4[:, b, k, :], m["hT"][:, k, g * SEQ:(g + 1) * SEQ],
                                           start=(k == 0), stop=(k == KD - 1))
                        mm.then_inc(proj_ps, 1)
                    for b in range(2):
                        pe.wait_ge(ada_in, (2 * h + b + 1) * 16)
                        pe.wait_ge(mod_done, 1 + 2 * h + b)
                        pe.wait_ge(early_sb, 1 + h * (GROUPS * ETILES))
                        for j in range(ADA_TILES):
                            for k in range(KD):
                                mm = pe.matmul(ps[:, 2, 2 * j:2 * j + 2], ada[:, k, j * P:(j + 1) * P], m["sc"][:, k, :],
                                               start=(k == 0), stop=(k == KD - 1))
                        mm.then_inc(mod_ps, 1)
                    for g in range(GROUPS):
                        n = h * GROUPS + g
                        pe.wait_ge(on_done, 1 + n)
                        for i in range(3):
                            pe.wait_ge(silu_done, h * 6 + (2 * i + g + 1))
                            for t in range(TPG):
                                mm = pe.transpose(ps[:, 3 + i, t * P:(t + 1) * P], conv[:, i, g, t * P:(t + 1) * P], ident)
                            mm.then_inc(tok_ps, 1)
                        fill(2)
                        pe.wait_ge(gsum_done, 2 * n + 2)
                        pe.wait_ge(proj_read, 1 + h * NPROJ + NPROJ)
                        pe.wait_ge(oa_done, 1 + n)
                        for d in range(2):
                            pe.matmul(ps[:, d, :], m["ones"][:, :], gsum[d][:, :, :], start=True,
                                      stop=True).then_inc(row_ps[d], 1)
                        fill(4)
                        for i, (src, ready) in enumerate(((kn, kn_done), (qn, qn_done))):
                            pe.wait_ge(ready, n + 1)
                            for t in range(TPG):
                                mm = pe.transpose(ps[:, 6 + i, t * P:(t + 1) * P], src[:, t, :], ident)
                            mm.then_inc(chn_ps, 1)
                        fill(2)
                        pe.wait_ge(chn_sb, 2 * n + 2)
                        for i, lhs in enumerate((knT, qnT)):
                            for t in range(TPG):
                                mm = pe.matmul(ps[:, 3 + i, t * P:(t + 1) * P], lhs[:, t, :], knT[:, t, :],
                                               start=True, stop=True)
                        mm.then_inc(gram_ps, 1)
                        fill(1)
                        pe.wait_ge(vb_done, n + 1)
                        for d in range(2):
                            pe.wait_ge(qe_done, 2 * n + d + 1)
                            for t in range(TPG):
                                mm = pe.transpose(ps[:, 5 + d, t * P:(t + 1) * P], qe[d][:, t, :], ident)
                            mm.then_inc(qeT_ps, 1)
                        fill(3)
                        for d in range(2):
                            pe.wait_ge(x_done[d], 2 * n + 2)
                            for t in range(TPG):
                                mm = pe.transpose(ps[:, d, t * P:(t + 1) * P], xb[d][:, t, :], ident)
                            mm.then_inc(xT_ps[d], 1)
                            pe.wait_ge(qeT_sb, 2 * n + 2)
                            for t in range(TPG):
                                mm = pe.transpose(ps[:, 5 + 2 * d, t * P:(t + 1) * P], dec[d][:, t, :], ident)
                            mm.then_inc(xT_ps[d], 1)
                            fill(2)
                        for lv in range(LV):
                            for d in range(2):
                                if lv == 0:
                                    pe.wait_ge(x_done[1 - d], 2 * n + 2)
                                    pe.wait_ge(xT_sb[d], 2 * n + 2)
                                    pe.wait_ge(inv0_done[d], 4 * n + 4)
                                else:
                                    pe.wait_ge(inv_done[d], n * LV + lv)
                                for t in range(TPG):
                                    mm = pe.matmul(ps[:, d, t * P:(t + 1) * P], xbT[d][:, t, :], inv[d][:, 0, t, :],
                                                   start=True, stop=True)
                                mm.then_inc(y_ps[d], 1)
                            fill(FILL[d])
                            for d in range(2):
                                pe.wait_ge(y_sb[d], n * LV + lv + 1)
                                if lv < LV - 1:
                                    for t in range(TPG):
                                        pe.matmul(ps[:, 4 + 2 * d, t * P:(t + 1) * P], inv[d][:, 1, t, :], xb[d][:, t, :],
                                                  start=True, stop=True)
                                for t in range(TPG):
                                    mm = pe.matmul(ps[:, 5 + 2 * d, t * P:(t + 1) * P], xb[d][:, t, :], inv[d][:, 1, t, :],
                                                   start=True, stop=True)
                                mm.then_inc(upd_ps[d], 1)
                            fill(FILL[d])
                        for d in range(2):
                            pe.wait_ge(inv_done[d], n * LV + LV)
                            pe.wait_ge(kbe_done, 4 * n + 2 * d + 1)
                            for t in range(TPG):
                                pe.matmul(ps[:, d, t * P:(t + 1) * P], inv[d][:, 1, t, :], vb[d][:, t, :],
                                          start=True, stop=True)
                            for t in range(TPG):
                                mm = pe.matmul(ps[:, 4 + 2 * d, t * P:(t + 1) * P], kbe[d][:, t, :], inv[d][:, 1, t, :],
                                               start=True, stop=True)
                            mm.then_inc(uw_ps[d], 1)
                        fill(5)
                        pe.wait_ge(kbe_done, 4 * n + 4)
                        for i in range(NCHUNK):
                            for d in range(2):
                                t, rows = place(chunks(d)[i])
                                if i == 0:
                                    pe.wait_ge(uw_sb[d], 1 + 2 * n + 2)
                                else:
                                    pe.wait_ge(state_done[d], n * NC1 + i)
                                    pe.matmul(ps[rows, 5 + 2 * d, 0:P], xbT[d][:, t, rows],
                                              state[d][:, i, :], start=True, stop=True).then_inc(ws_ps[d], 1)
                            if i > 0:
                                fill(FILL[d])
                            for d in range(2):
                                t, rows = place(chunks(d)[i])
                                if i > 0:
                                    pe.wait_ge(vnew_done[d], n * NC1 + i)
                                if i < NC1:
                                    pe.matmul(ps[:, 5 + 2 * d, P:2 * P], kd[d][rows, t, :], vnew[d][rows, t, :],
                                              start=True, stop=True).then_inc(kv_ps[d], 1)
                            if i < NC1:
                                fill(FILL[d])
                        for t in range(TPG):
                            out = ps[:, 3, t * P:(t + 1) * P]
                            pe.matmul(out, qkT[0][:, t, :], vnew[0][:, t, :], start=True, stop=False)
                            terms = [(d, c) for d in range(2) for c in (2 * t, 2 * t + 1) if chunks(d)[0] != c]
                            for d, c in terms:
                                rows = place(c)[1]
                                pe.matmul(ps[rows, 3, t * P:(t + 1) * P], qeT[d][:, t, rows],
                                          state[d][:, chunks(d).index(c), :], start=False, stop=False)
                            mm = pe.matmul(out, qkT[1][:, t, :], vnew[1][:, t, :], start=False, stop=True)
                        mm.then_inc(o_ps, 1)
                        fill(11)
                        pe.wait_ge(on_done, 1 + n + 1)
                        for t in range(TPG):
                            mm = pe.transpose(ps[:, 0, t * P:(t + 1) * P], on[:, t, :], ident)
                        mm.then_inc(oT_ps, 1)
                    assert not list(early)

            @block.scalar
            def _(act):
                act.wait_ge(masks, 1)
                prime(act, proj_read, *uw_sb, sq_done, osq_done, early_sb)
                with act.Fori(0, HA) as h:
                    units = iter(range(GROUPS * EUNITS))

                    def keep_early():
                        unit = next(units)
                        i, u = divmod(unit, GROUPS)
                        act.wait_ge(early_ps, h * (GROUPS * ETILES) + (unit + 2))
                        if i >= 1:
                            act.wait_ge(early_out[u], h * (16 * ETILES) + 16 * i)
                        act.activation(est[u], ps[:, 2, :], ACT.Copy).then_inc(early_sb, 1)
                        act.wait_ge(early_sb, h * (GROUPS * ETILES) + (unit + 2))
                        act.dma_start(early_v[:, bass.ds(h * ETILES + i, 1), u * SEQ:(u + 1) * SEQ],
                                      est[u].unsqueeze(1)).then_inc(early_out[u], 16)

                    def silu(u):
                        b, g = divmod(u, GROUPS)
                        act.wait_ge(conv_done, h * 6 + (u + 1))
                        act.activation(conv[:, b, g, :], conv[:, b, g, :], ACT.Silu).then_inc(silu_done, 1)

                    for u in range(NPROJ):
                        b, g = divmod(u, GROUPS)
                        act.wait_ge(proj_ps, 1 + h * NPROJ + (u + 1))
                        if b < 3:
                            act.activation(pre[:, u % 2, 2:SEQ + 2], ps[:, u % 2, :], ACT.Copy).then_inc(proj_read, 1)
                        else:
                            act.activation(zT[:, g, :], ps[:, u % 2, :], ACT.Silu).then_inc(proj_read, 1)
                        if 1 <= u <= 6:
                            silu(u - 1)
                    for g in range(GROUPS):
                        n = h * GROUPS + g
                        for i in range(2):
                            act.wait_ge(tok_ps, 3 * n + i + 1)
                            for t in range(TPG):
                                c = i * TPG + t
                                act.wait_ge(sq_done, 1 + n * 2 * TPG + c)
                                act.activation(junk[:, :], ps[:, 3 + i, t * P:(t + 1) * P], ACT.Square,
                                               accum_out=ssqk[:, c:c + 1]).then_inc(sq_done, 1)
                        for i, dst in enumerate((knT, qnT)):
                            act.wait_ge(chn_ps, 2 * n + i + 1)
                            act.activation(dst[:, :, :], ps[:, 6 + i, :], ACT.Copy).then_inc(chn_sb, 1)
                        keep_early()
                        for d in range(2):
                            act.wait_ge(diff_done[d], TPG * n + TPG)
                            act.activation(dec[d][:, :, :], dec[d][:, :, :], ACT.Exp, scale=-1.0).then_inc(dec_done[d], 1)
                        for d in range(2):
                            act.wait_ge(qeT_ps, 2 * n + d + 1)
                            act.activation(qeT[d][:, :, :], ps[:, 5 + d, :], ACT.Copy).then_inc(qeT_sb, 1)
                        for d in range(2):
                            act.wait_ge(xT_ps[d], 2 * n + 1)
                            act.activation(xbT[d][:, :, :], ps[:, d, :], ACT.Copy).then_inc(xT_sb[d], 1)
                            act.wait_ge(xT_ps[d], 2 * n + 2)
                            act.activation(qkT[d][:, :, :], ps[:, 5 + 2 * d, :], ACT.Copy).then_inc(xT_sb[d], 1)
                        for _ in range(2):
                            keep_early()
                        for d in range(2):
                            act.wait_ge(uw_ps[d], n + 1)
                            act.activation(vnew[d][:, :, :], ps[:, d, :], ACT.Copy).then_inc(uw_sb[d], 1)
                            act.activation(xbT[d][:, :, :], ps[:, 4 + 2 * d, :], ACT.Copy).then_inc(uw_sb[d], 1)
                        for _ in range(2):
                            keep_early()
                        act.wait_ge(o_ps, n + 1)
                        for t in range(TPG):
                            act.wait_ge(osq_done, 1 + n * TPG + t)
                            act.activation(junk[:, :], ps[:, 3, t * P:(t + 1) * P], ACT.Square,
                                           accum_out=ssqo[:, t:t + 1]).then_inc(osq_done, 1)
                        for _ in range(2):
                            keep_early()
                    for u in range(GROUPS):
                        act.wait_ge(early_out[u], (h + 1) * (16 * ETILES))

            @block.vector
            def _(dve):
                prime(dve, oa_done, mod_done, on_done)
                for d in range(2):
                    dve.tensor_scalar(posmask[:, d, :], m["upto"][:, 1 - d, :], -BIG, BIG, ALU.mult, ALU.add).then_inc(posmask_done, 1)
                dve.wait_ge(posmask_done, 2)
                dve.wait_ge(masks, 1)
                with dve.Fori(0, HA) as h:
                    st = Steps(dve, dve_step, before=h * D_STEPS)
                    dve.tensor_copy(hd[:, :, :, :], m["tab"][:, :, :, :].rearrange("p q t (d h) -> p (q t d) h", d=2)
                                    [:, :, bass.ds(h, 1)]).then_inc(hd_ready, 1)
                    st.do(dve.tensor_copy(cw[:, :], m["convT"][:, 0:60].rearrange("p (r h) -> p r h", h=HA)
                                          [:, :, bass.ds(h, 1)]))
                    for u in range(6):
                        b, g = divmod(u, GROUPS)
                        dve.wait_ge(proj_read, 1 + h * NPROJ + (u + 1))
                        acc = conv[:, b, g, :]
                        st.do(dve.tensor_scalar(acc, pre[:, u % 2, 0:SEQ], cw[:, b:b + 1], None, ALU.mult))
                        for tap in range(1, CONV_K):
                            ins = dve.scalar_tensor_tensor(out=acc, in0=pre[:, u % 2, tap:tap + SEQ],
                                                           scalar=cw[:, 3 * tap + b:3 * tap + b + 1], in1=acc,
                                                           op0=ALU.mult, op1=ALU.add)
                            if tap < CONV_K - 1:
                                st.do(ins)
                            else:
                                ins.then_inc(conv_done, 1)
                    for b in range(2):
                        dve.wait_ge(mod_ps, 1 + 2 * h + b + 1)
                        first = 16 + b * ADA_TILES
                        dve.tensor_tensor(m["modT"][:, :, :].rearrange("p j g -> p (j g)")[:, bass.ds(h * 16 + 2 * first, 8)]
                                          .rearrange("p (j g) -> p j g", g=2),
                                          ps[:, 2, 0:8].rearrange("p (j g) -> p j g", g=2),
                                          bcast(m["vecT"][:, bass.ds(h * 8 + first, 4)], 2, GROUPS), ALU.add).then_inc(mod_done, 1)
                    for g in range(GROUPS):
                        n = h * GROUPS + g
                        tiles = slice(g * TPG, (g + 1) * TPG)
                        dve.wait_ge(sq_done, 1 + (n + 1) * 2 * TPG)
                        dve.tensor_scalar(msqk[:, 0:TPG], ssqk[:, 0:TPG], EPS, float(DK), ALU.add, ALU.mult)
                        dve.tensor_scalar(msqk[:, TPG:], ssqk[:, TPG:], EPS, None, ALU.add).then_inc(ms_done, 1)
                        dve.wait_ge(tok_ps, 3 * n + 3)
                        for d in range(2):
                            ins = dve.tensor_tensor(vb[d][:, :, :], ps[:, 5, :].rearrange("p (t c) -> p t c", t=TPG),
                                                    bcast(hd[:, BETA, tiles, d], 2, P), ALU.mult)
                        ins.then_inc(vb_done, 1)
                        dve.wait_ge(rqk_done, n + 1)
                        dve.tensor_tensor(kn[:, :, :], ps[:, 4, :].rearrange("p (t c) -> p t c", t=TPG),
                                          bcast(rqk[:, TPG:], 2, P), ALU.mult).then_inc(kn_done, 1)
                        dve.tensor_tensor(qn[:, :, :], ps[:, 3, :].rearrange("p (t c) -> p t c", t=TPG),
                                          bcast(rqk[:, 0:TPG], 2, P), ALU.mult).then_inc(qn_done, 1)
                        for d in range(2):
                            dve.wait_ge(row_ps[d], n + 1)
                            for t in range(TPG):
                                dve.scalar_tensor_tensor(out=dec[d][:, t, :], in0=ps[:, d, t * P:(t + 1) * P],
                                                         scalar=hd[:, CUM, g * TPG + t, d:d + 1], in1=posmask[:, d, :],
                                                         op0=ALU.subtract, op1=ALU.add).then_inc(diff_done[d], 1)
                        dve.wait_ge(gram_ps, n + 1)
                        for d in range(2):
                            dve.wait_ge(dec_done[d], n + 1)
                            for t in range(TPG):
                                ins = dve.scalar_tensor_tensor(out=xb[d][:, t, :], in0=ps[:, 3, t * P:(t + 1) * P],
                                                               scalar=hd[:, BETA, g * TPG + t, d:d + 1],
                                                               in1=dec[d][:, t, :], op0=ALU.mult, op1=ALU.mult)
                            ins.then_inc(x_done[d], 1)
                            dve.wait_ge(x_done[d], 2 * n + 1)
                            dve.tensor_tensor(dec[d][:, :, :], ps[:, 4, :], dec[d][:, :, :].rearrange("p t c -> p (t c)"),
                                              ALU.mult).then_inc(x_done[d], 1)
                        for lv in range(LV):
                            for d in range(2):
                                dve.wait_ge(y_ps[d], n * LV + lv + 1)
                                if lv == 0:
                                    dve.wait_ge(inv0_done[d], 4 * n + 4)
                                dve.tensor_tensor(xb[d][:, :, :], ps[:, d, :].rearrange("p (t c) -> p t c", t=TPG),
                                                  bcast(levelmask[:, d, lv + 1, :], 1, TPG), ALU.mult).then_inc(y_sb[d], 1)
                            for d in range(2):
                                dve.wait_ge(upd_ps[d], n * LV + lv + 1)
                                lo = 0 if lv < LV - 1 else 1
                                dve.tensor_tensor(inv[d][:, lo:2, :, :].rearrange("p s t c -> p s (t c)"),
                                                  inv[d][:, lo:2, :, :].rearrange("p s t c -> p s (t c)"),
                                                  ps[:, 4 + 2 * d + lo:6 + 2 * d, :], ALU.subtract).then_inc(inv_done[d], 1)
                        for i in range(NCHUNK):
                            for d in range(2):
                                t, rows = place(chunks(d)[i])
                                if i > 0:
                                    dve.wait_ge(ws_ps[d], n * NC1 + i)
                                    dve.tensor_tensor(vnew[d][rows, t, :], vnew[d][rows, t, :], ps[rows, 5 + 2 * d, 0:P],
                                                      ALU.subtract).then_inc(vnew_done[d], 1)
                            for d in range(2):
                                c = chunks(d)[i]
                                if i < NC1:
                                    dve.wait_ge(kv_ps[d], n * NC1 + i + 1)
                                    kv = ps[:, 5 + 2 * d, P:2 * P]
                                    if i == 0:
                                        dve.tensor_copy(state[d][:, 1, :], kv).then_inc(state_done[d], 1)
                                    else:
                                        dve.scalar_tensor_tensor(out=state[d][:, i + 1, :], in0=state[d][:, i, :],
                                                                 scalar=hd[:, ETOT + c % 2, g * TPG + c // 2, d:d + 1], in1=kv,
                                                                 op0=ALU.mult, op1=ALU.add).then_inc(state_done[d], 1)
                        dve.wait_ge(osq_done, 1 + (n + 1) * TPG)
                        dve.tensor_scalar(mso[:, :], ssqo[:, :], 1.0 / DK, EPS, ALU.mult, ALU.add).then_inc(mso_done, 1)
                        dve.wait_ge(ro_done, n + 1)
                        dve.tensor_tensor(on[:, :, :], ps[:, 3, :].rearrange("p (t c) -> p t c", t=TPG),
                                          bcast(ro[:, :], 2, P), ALU.mult).then_inc(on_done, 1)
                        dve.wait_ge(oT_ps, n + 1)
                        dve.scalar_tensor_tensor(out=m["oaT"][:, :, :].rearrange("p h t -> p (h t)")
                                                 [:, bass.ds(h * TOK + g * SEQ, SEQ)],
                                                 in0=ps[:, 0, :], scalar=m["convT"][:, 60:61], in1=zT[:, g, :],
                                                 op0=ALU.mult, op1=ALU.mult).then_inc(oa_done, 1)
                    assert st.n == D_STEPS
        nc.clear_and_free_semaphores(sems)
        nc.all_engine_barrier()


def phase_attention(nc, a, m, ps, early_dram):
    NPROJ = 3 * GROUPS
    NU = GROUPS * 2 * TPG
    KINDS = [(16, 48), (0, 48), (0, 32)]
    KIND_OF = [0, 1, 1, 2]
    KIND_AT = [0, 256, 640]
    BIAS_W = 896
    with ExitStack() as ctx:
        def sb(name, shape, dt=F32):
            return ctx.enter_context(nc.sbuf_tensor(name, shape, dt))

        def sem(name):
            return ctx.enter_context(nc.semaphore(name))

        raw = sb("raw", [P, 3, TOK])
        rel = sb("rel", [P, HB, RPB_RUN])
        outside = sb("outside", [P, BIAS_W])
        bias = sb("bias", [P, 2, BIAS_W])
        qT = sb("qT", [P, GROUPS, SEQ])
        kT = sb("kT", [P, GROUPS, SEQ])
        vT = sb("vT", [P, GROUPS, SEQ])
        vtok = sb("vtok", [P, GROUPS, TPG, P])
        sc = sb("scores", [P, 2, 3 * P])
        low = sb("low", [P, 2])
        pr = sb("pr", [P, 2, 3 * P])
        den = sb("den", [P, 2])
        rden = sb("rden", [P, 2])
        pT = sb("pT", [P, 2, 3 * P])
        otok = sb("otok", [P, GROUPS, TPG, P])

        raw_in = sem("raw_in")
        rel_in = sem("rel_in")
        outside_done = sem("outside_done")
        bias_done = sem("bias_done")
        take_done = sem("take_done")
        vt_ps = sem("vt_ps")
        vtok_sb = sem("vtok_sb")
        s_ps = sem("s_ps")
        sc_done = sem("sc_done")
        low_done = sem("low_done")
        exp_done = sem("exp_done")
        pT_ps = sem("pT_ps")
        pT_sb = sem("pT_sb")
        pv_ps = sem("pv_ps")
        rden_done = sem("rden_done")
        otok_done = sem("otok_done")
        obT_ps = sem("obT_ps")
        ob_done = sem("ob_done")

        def unit(w):
            g, r = divmod(w, 2 * TPG)
            hp, t = divmod(r, TPG)
            return g, hp, t

        def width(t):
            return (KEY_TILES[t][1] - KEY_TILES[t][0]) * P

        def before(w, lag):
            return max(w - lag + 1, 0)

        with nc.Block() as block:

            @block.sync
            def _(sp):
                rpb = a["rpb"]
                for c in range(16):
                    src = bass.AP(rpb.tensor, RPB_FRONT - 15 * c - 8, [[HB * RPB_LEN, ROWS], [RPB_LEN, HB], [1, RPB_RUN]])
                    sp.dma_start(rel[8 * c:8 * c + 8, :, :], src).then_inc(rel_in, 16)
                early_v = early_dram[0:GATE_TILE * P, :].rearrange("(b h p) t -> p b h t", p=P, b=3)
                with sp.Fori(0, PAIRS) as h:
                    sp.wait_ge(take_done, 1 + h * NPROJ)
                    sp.dma_start(raw[:, :, :].unsqueeze(2), early_v[:, :, bass.ds(h, 1), :]).then_inc(raw_in, 16)

            @block.gpsimd
            def _(pool):
                pool.memset(outside[:, :], 0.0).then_inc(outside_done, 1)
                n = 1

                def keep(kind, x0, x1, base, step, cm):
                    nonlocal n
                    pool.wait_ge(outside_done, n)
                    lo = KINDS[kind][0]
                    part = outside[:, KIND_AT[kind] + (x0 - lo) * 8:KIND_AT[kind] + (x1 - lo) * 8]
                    pool.affine_select(out=part, in_=part, compare_op=ALU.is_ge, fill=BIG, base=base + step * x0,
                                       pattern=[[step, x1 - x0], [0, 8]], channel_multiplier=cm).then_inc(outside_done, 1)
                    n += 1

                keep(0, 16, 48, 7 - 64, 8, -1)
                keep(0, 32, 48, 184, -8, 1)
                keep(1, 0, 48, 7 - 64, 8, -1)
                keep(1, 0, 48, 184, -8, 1)
                keep(2, 0, 16, 7 - 64, 8, -1)
                keep(2, 0, 32, 184, -8, 1)
                pool.wait_ge(outside_done, n)
                pool.wait_ge(rel_in, 16 * 16)
                rel_flat = rel[:, :, :].rearrange("p h x -> p (h x)")
                with pool.Fori(0, PAIRS) as h:
                    pool.wait_ge(sc_done, 1 + h * NU)
                    for hp in range(2):
                        for kind, (x0, x1) in enumerate(KINDS):
                            nx = x1 - x0
                            src = rel_flat[:, bass.ds(h * (2 * RPB_RUN) + (hp * RPB_RUN + x0 * RPB_R), nx * RPB_R)]
                            at = slice(KIND_AT[kind], KIND_AT[kind] + nx * 8)
                            pool.tensor_tensor(bias[:, hp, at].rearrange("p (x r) -> p x r", r=8),
                                               src.rearrange("p (x r) -> p x r", r=RPB_R)[:, :, 0:8],
                                               outside[:, at].rearrange("p (x r) -> p x r", r=8),
                                               ALU.subtract).then_inc(bias_done, 1)

            @block.tensor
            def _(pe):
                ident = m["ident"][:, :]
                prime(pe, pT_ps, pv_ps)
                with pe.Fori(0, PAIRS) as h:
                    for g in range(GROUPS):
                        pe.wait_ge(take_done, 1 + h * NPROJ + (5 + g))
                        pe.wait_ge(sc_done, 1 + h * NU)
                        for t in range(TPG):
                            mm = pe.transpose(ps[:, 2 + g, t * P:(t + 1) * P], vT[:, g, t * P:(t + 1) * P], ident)
                        mm.then_inc(vt_ps, 1)

                    def scores(w):
                        g, hp, t = unit(w)
                        k0, k1 = KEY_TILES[t]
                        if w < 2:
                            pe.wait_ge(vtok_sb, h * GROUPS + GROUPS)
                        pe.wait_ge(sc_done, 1 + h * NU + before(w, 2))
                        rows = slice(hp * DH, (hp + 1) * DH)
                        pe.matmul(ps[:, 2 + w % 2, 0:width(t)], qT[rows, g, t * P:(t + 1) * P],
                                  kT[rows, g, k0 * P:k1 * P], start=True, stop=True).then_inc(s_ps, 1)

                    def turn(w):
                        g, hp, t = unit(w)
                        pe.wait_ge(exp_done, 1 + h * NU + (w + 1))
                        pe.wait_ge(pT_sb, 1 + h * NU + before(w, 2))
                        for i in range(width(t) // P):
                            mm = pe.transpose(ps[:, 4 + w % 2, i * P:(i + 1) * P], pr[:, w % 2, i * P:(i + 1) * P], ident)
                        mm.then_inc(pT_ps, 1)

                    def values(w):
                        g, hp, t = unit(w)
                        k0, k1 = KEY_TILES[t]
                        pe.wait_ge(pT_sb, 1 + h * NU + (w + 1))
                        pe.wait_ge(otok_done, 1 + h * NU + before(w, 2))
                        for i in range(k1 - k0):
                            mm = pe.matmul(ps[:, 6 + w % 2, 0:DH], pT[:, w % 2, i * P:(i + 1) * P],
                                           vtok[:, g, k0 + i, hp * DH:(hp + 1) * DH], start=(i == 0), stop=(i == k1 - k0 - 1))
                        mm.then_inc(pv_ps, 1)

                    for w in range(NU + 3):
                        if w < NU:
                            scores(w)
                        if 2 <= w < NU + 2:
                            turn(w - 2)
                        if w >= 3:
                            values(w - 3)
                    for g in range(GROUPS):
                        pe.wait_ge(otok_done, 1 + h * NU + (g + 1) * 2 * TPG)
                        pe.wait_ge(ob_done, 1 + h * GROUPS)
                        for t in range(TPG):
                            mm = pe.transpose(ps[:, g, t * P:(t + 1) * P], otok[:, g, t, :], ident)
                        mm.then_inc(obT_ps, 1)

            @block.scalar
            def _(act):
                prime(act, take_done, exp_done, pT_sb)
                with act.Fori(0, PAIRS) as h:
                    act.wait_ge(raw_in, (h + 1) * 16)
                    for u in range(NPROJ):
                        b, g = divmod(u, GROUPS)
                        dst = (qT, kT, vT)[b][:, g, :].rearrange("p (c r) -> p r c", r=ROWS)
                        act.activation(dst, raw[:, b, g * SEQ:(g + 1) * SEQ].rearrange("p (r c) -> p r c", r=ROWS), ACT.Copy,
                                       scale=(-DH ** -0.5 if b == 0 else 1.0)).then_inc(take_done, 1)
                    for g in range(GROUPS):
                        act.wait_ge(vt_ps, h * GROUPS + (g + 1))
                        act.activation(vtok[:, g, :, :], ps[:, 2 + g, :], ACT.Copy).then_inc(vtok_sb, 1)
                    for w in range(NU + 1):
                        if w < NU:
                            g, hp, t = unit(w)
                            act.wait_ge(low_done, h * NU + (w + 1))
                            act.wait_ge(pT_ps, 1 + h * NU + before(w, 2))
                            act.wait_ge(rden_done, 1 + h * NU + before(w, 2))
                            act.activation(pr[:, w % 2, 0:width(t)], sc[:, w % 2, 0:width(t)], ACT.Exp, scale=-1.0,
                                           bias=low[:, w % 2:w % 2 + 1],
                                           accum_out=den[:, w % 2:w % 2 + 1]).then_inc(exp_done, 1)
                        if w >= 1:
                            v = w - 1
                            g, hp, t = unit(v)
                            act.wait_ge(pT_ps, 1 + h * NU + (v + 1))
                            act.wait_ge(pv_ps, 1 + h * NU + before(v, 2))
                            act.activation(pT[:, v % 2, 0:width(t)], ps[:, 4 + v % 2, 0:width(t)], ACT.Copy).then_inc(pT_sb, 1)

            @block.vector
            def _(dve):
                prime(dve, sc_done, rden_done, otok_done, ob_done)
                with dve.Fori(0, PAIRS) as h:
                    dve.wait_ge(bias_done, (h + 1) * 6)
                    for w in range(NU + 3):
                        if w < NU:
                            g, hp, t = unit(w)
                            n = width(t)
                            dve.wait_ge(s_ps, h * NU + (w + 1))
                            dve.wait_ge(exp_done, 1 + h * NU + before(w, 2))
                            at = KIND_AT[KIND_OF[t]]
                            dve.tensor_tensor(sc[:, w % 2, 0:n], ps[:, 2 + w % 2, 0:n], bias[:, hp, at:at + n],
                                              ALU.subtract).then_inc(sc_done, 1)
                            dve.wait_ge(sc_done, 1 + h * NU + (w + 1))
                            dve.tensor_reduce(low[:, w % 2:w % 2 + 1], sc[:, w % 2, 0:n], AX_X, ALU.min).then_inc(low_done, 1)
                        if w >= 3:
                            v = w - 3
                            g, hp, t = unit(v)
                            dve.wait_ge(pv_ps, 1 + h * NU + (v + 1))
                            dve.wait_ge(rden_done, 1 + h * NU + (v + 1))
                            dve.tensor_scalar(otok[:, g, t, hp * DH:(hp + 1) * DH], ps[:, 6 + v % 2, 0:DH],
                                              rden[:, v % 2:v % 2 + 1], None, ALU.mult).then_inc(otok_done, 1)
                        if 2 <= w < NU + 2:
                            v = w - 2
                            dve.wait_ge(exp_done, 1 + h * NU + (v + 1))
                            dve.wait_ge(otok_done, 1 + h * NU + before(v, 2))
                            dve.reciprocal(rden[:, v % 2:v % 2 + 1], den[:, v % 2:v % 2 + 1]).then_inc(rden_done, 1)
                    for g in range(GROUPS):
                        dve.wait_ge(obT_ps, h * GROUPS + (g + 1))
                        dst = m["obT"][:, :, :].rearrange("p h t -> p (h t)")[:, bass.ds(h * TOK + g * SEQ, SEQ)]
                        dve.tensor_copy(dst.rearrange("p (r c) -> p r c", r=ROWS),
                                        ps[:, g, :].rearrange("p (c r) -> p r c", r=ROWS)).then_inc(ob_done, 1)


def late_buffers(nc, ctx):
    def sb(name, shape, dt=F32):
        return ctx.enter_context(nc.sbuf_tensor(name, shape, dt))

    late = {}
    late["mergedT"] = sb("mergedT", [P, KD, TOK])
    late["gate1"] = sb("gate1", [P, GROUPS, D_MODEL])
    late["mul2row"] = sb("mul2row", [P, GROUPS, D_MODEL])
    late["shift2"] = sb("shift2", [P, GROUPS, D_MODEL])
    late["wout"] = sb("wout", [P, KD, D_MODEL])
    late["wr"] = sb("wr", [P, KD, NE])
    late["route_in"] = ctx.enter_context(nc.semaphore("route_in"))
    return late


def phase_merge(nc, a, m, ps, late, early_dram):
    JOBS = 2 * GROUPS
    ROWS_OF = 8
    with ExitStack() as ctx:
        def sb(name, shape, dt=F32):
            return ctx.enter_context(nc.sbuf_tensor(name, shape, dt))

        def sem(name):
            return ctx.enter_context(nc.semaphore(name))

        wj = [sb(f"wj{i}", [P, KD, P]) for i in range(2)]
        graw = [sb(f"graw{i}", [P, 2, TOK]) for i in range(2)]
        sig = sb("sig", [P, GROUPS, 2, SEQ])
        wide = sb("wide", [P, GROUPS, 2, SEQ])
        mul2 = sb("mul2", [P, KD, GROUPS])
        diag = sig[:, :, :, :].rearrange("p g b (k c) -> p g (b k) c", c=P)
        halfcols = sb("halfcols", [P, 2, P])

        halfcols_done = sem("halfcols_done")
        mul2_done = sem("mul2_done")
        diag_done = sem("diag_done")
        row_ps = sem("adarow_ps")
        row_sb = sem("adarow_sb")
        wj_in = [sem(f"wj_in{i}") for i in range(2)]
        graw_in = [sem(f"graw_in{i}") for i in range(2)]
        wide_ps = sem("wide_ps")
        sig_done = sem("sig_done")
        wide_done = sem("wide_done")
        merged_done = sem("merged_done")

        def row_jobs():
            mod = m["modT"]
            for g in range(GROUPS):
                yield late["gate1"][:, g, :], mod[:, 2 * KD:3 * KD, g], m["ones"][:, :], True, True
            for g in range(GROUPS):
                yield late["mul2row"][:, g, :], mul2[:, :, g], m["ones"][:, :], True, True
            for g in range(GROUPS):
                yield late["shift2"][:, g, :], mod[:, 3 * KD:4 * KD, g], m["ones"][:, :], True, True
            for g in range(GROUPS):
                yield m["gate2"][:, :], mod[:, 5 * KD:6 * KD, g], halfcols[:, g, :], g == 0, g == 1

        with nc.Block() as block:

            @block.sync
            def _(sp):
                gates_v = early_dram[GATE_TILE * P:, :].rearrange("(b j p) t -> p b j t", p=P, b=2)
                w_oa = a["w_oa"].rearrange("a (k p) n -> p (a k) n", p=P)
                w_ob = a["w_ob"].rearrange("a (k p) n -> p (a k) n", p=P)
                with sp.Fori(0, KD // 2) as jj:
                    for i in range(2):
                        sp.wait_ge(wide_ps, 1 + jj * JOBS)
                        sp.wait_ge(sig_done, 1 + jj * (2 * JOBS))
                        col = jj * (2 * P) + i * P
                        sp.dma_start(graw[i][:, :, :].unsqueeze(2), gates_v[:, :, bass.ds(jj * 2 + i, 1), :]).then_inc(graw_in[i], 16)
                        sp.dma_start(wj[i][:, 0:HA, :], w_oa[:, :, bass.ds(col, P)]).then_inc(wj_in[i], 16)
                        sp.dma_start(wj[i][:, HA:KD, :], w_ob[:, :, bass.ds(col, P)]).then_inc(wj_in[i], 16)
                sp.dma_start(late["wout"][:, :, :], a["w_out"].rearrange("a (k p) n -> p (a k) n", p=P)).then_inc(late["route_in"], 16)
                sp.dma_start(late["wr"][:, :, :], a["w_router"].rearrange("a (k p) n -> p (a k) n", p=P)).then_inc(late["route_in"], 16)

            @block.gpsimd
            def _(pool):
                pool.memset(halfcols[:, :, :], 0.0).then_inc(halfcols_done, 1)
                pool.wait_ge(halfcols_done, 1)
                for g in range(GROUPS):
                    pool.memset(halfcols[:, g, g * CAP:(g + 1) * CAP], 1.0).then_inc(halfcols_done, 1)
                prime(pool, merged_done)
                with pool.Fori(0, KD // 2) as jj:
                    for r in range(JOBS):
                        i, g = divmod(r, GROUPS)
                        pool.wait_ge(wide_done, 1 + jj * 2 * JOBS + (2 * r + 2))
                        dst = late["mergedT"][:, :, :].rearrange("p k t -> p (k t)")[:, bass.ds(
                            jj * (2 * TOK) + (i * TOK + g * SEQ), SEQ)]
                        pool.tensor_tensor(dst, wide[:, g, 0, :], wide[:, g, 1, :], ALU.add).then_inc(merged_done, 1)

            @block.tensor
            def _(pe):
                pe.wait_ge(halfcols_done, 3)
                for r, (_, _, lhs, start, stop) in enumerate(row_jobs()):
                    pe.wait_ge(diag_done, r + 1)
                    if r >= 2:
                        pe.wait_ge(row_sb, r - 1)
                    bank = 2 * (r % 2) if r < 6 else 0
                    for c in range(2):
                        mm = pe.matmul(ps[:, bank + c, :], lhs, diag[:, r % 2, c * 4:(c + 1) * 4, :], start=start, stop=stop)
                    mm.then_inc(row_ps, 1)
                pe.wait_ge(row_sb, ROWS_OF - 1)
                prime(pe, wide_ps)
                with pe.Fori(0, KD // 2) as jj:
                    for r in range(JOBS):
                        i, g = divmod(r, GROUPS)
                        if g == 0:
                            pe.wait_ge(wj_in[i], (jj + 1) * 32)
                        pe.wait_ge(wide_done, 1 + jj * 2 * JOBS + 2 * max(r - 1, 0))
                        cols = slice(g * SEQ, (g + 1) * SEQ)
                        for b, src in enumerate((m["oaT"], m["obT"])):
                            for k in range(HA):
                                mm = pe.matmul(ps[:, 4 * g + 2 + b, :], wj[i][:, b * HA + k, :], src[:, k, cols],
                                               start=(k == 0), stop=(k == HA - 1))
                        mm.then_inc(wide_ps, 1)

            @block.scalar
            def _(act):
                act.wait_ge(row_ps, ROWS_OF)
                prime(act, sig_done)
                with act.Fori(0, KD // 2) as jj:
                    for r in range(JOBS):
                        i, g = divmod(r, GROUPS)
                        if g == 0:
                            act.wait_ge(graw_in[i], (jj + 1) * 16)
                        act.wait_ge(wide_done, 1 + jj * 2 * JOBS + 2 * max(r - 1, 0))
                        for b in range(2):
                            act.activation(sig[:, g, b, :], graw[i][:, b, g * SEQ:(g + 1) * SEQ], ACT.Sigmoid).then_inc(sig_done, 1)

            @block.vector
            def _(dve):
                dve.scalar_tensor_tensor(out=mul2[:, :, :], in0=m["modT"][:, 4 * KD:5 * KD, :], scalar=1.0,
                                         in1=bcast(m["vecT"][:, VN2:VN2 + KD], 2, GROUPS),
                                         op0=ALU.add, op1=ALU.mult).then_inc(mul2_done, 1)
                dve.wait_ge(mul2_done, 1)
                jobs = list(row_jobs())
                for r in range(ROWS_OF + 1):
                    if r < ROWS_OF:
                        if r >= 2:
                            dve.wait_ge(row_ps, r - 1)
                        dve.tensor_tensor(diag[:, r % 2, :, :], bcast(m["ident"][:, :], 1, KD), bcast(jobs[r][1], 2, P),
                                          ALU.mult).then_inc(diag_done, 1)
                    if r >= 1:
                        v = r - 1
                        dve.wait_ge(row_ps, v + 1)
                        if v == 6:
                            continue
                        bank = 2 * (v % 2) if v < 6 else 0
                        dve.tensor_copy(jobs[v][0], ps[:, bank:bank + 2, :].rearrange("p b c -> p (b c)")).then_inc(row_sb, 1)
                prime(dve, wide_done)
                with dve.Fori(0, KD // 2) as jj:
                    for r in range(JOBS):
                        g = r % GROUPS
                        dve.wait_ge(wide_ps, 1 + jj * JOBS + (r + 1))
                        dve.wait_ge(merged_done, 1 + jj * JOBS + max(r - 1, 0))
                        for b in range(2):
                            dve.wait_ge(sig_done, 1 + jj * 2 * JOBS + (2 * r + b + 1))
                            dve.tensor_tensor(wide[:, g, b, :], sig[:, g, b, :], ps[:, 4 * g + 2 + b, :],
                                              ALU.mult).then_inc(wide_done, 1)


def phase_route(nc, a, m, ps, late, x2_dram, h2_dram):
    NR = GROUPS * NE
    xt = m["hT"]
    with ExitStack() as ctx:
        def sb(name, shape, dt=F32):
            return ctx.enter_context(nc.sbuf_tensor(name, shape, dt))

        def sem(name):
            return ctx.enter_context(nc.semaphore(name))

        xm = sb("xm", [P, 2, D_MODEL])
        h2 = sb("h2", [P, 2, D_MODEL])
        junk = sb("junk_r", [P, D_MODEL])
        h2T = sb("h2T", [P, 2, KD, P])
        ssq = sb("ssq_r", [P, NT])
        ms = sb("ms_r", [P, NT])
        rinv = sb("rinv_r", [P, NT])
        negmax = sb("negmax", [P, NT])
        ex = sb("ex", [P, NT, NE])
        den = sb("den_r", [P, NT])
        rden = sb("rden_r", [P, NT])
        probs = sb("probs", [P, TPG, GROUPS, NE])
        work = sb("work", [NR, 2, SEQ])
        vals = sb("vals", [NR, CAP])
        idx = sb("idx", [NR, CAP], U32)
        idxf = sb("idxf", [NR, CAP])
        first = sb("first_token", [NR, 1])
        own = sb("own_half", [NR, GROUPS, CAP])
        pick = sb("pick", [NR, NE])
        spread = sb("spread", [NR, 2, GROUPS, CAP])

        xt_in = sem("xt_in")
        sel_const = sem("sel_const")
        out_ps = sem("out_ps")
        xm_done = sem("xm_done")
        x2_done = sem("x2_done")
        ssq_done = sem("ssq_done_r")
        ms_done = sem("ms_done_r")
        rinv_done = sem("rinv_done_r")
        hm_done = sem("hm_done")
        h2_done = sem("h2_done")
        x2_out = sem("x2_out")
        h2_out = [sem(f"h2_out{i}") for i in range(2)]
        h2T_ps = sem("h2T_ps")
        h2T_sb = sem("h2T_sb")
        logit_ps = sem("logit_ps")
        negmax_done = sem("negmax_done")
        ex_done = sem("ex_done")
        rden_done = sem("rden_done_r")
        probs_done = sem("probs_done")
        probsT_ps = sem("probsT_ps")
        top_step = sem("top_step")
        pick_ps = sem("pick_ps")

        with nc.Block() as block:

            @block.sync
            def _(sp):
                sp.dma_start(xt[:, :, :], a["x"].rearrange("(t p) c -> p t c", p=P)).then_inc(xt_in, 16)
                x2_v = x2_dram.rearrange("(t p) c -> t p c", p=P)
                h2_v = h2_dram.rearrange("(t p) c -> t p c", p=P)
                for t in range(NT):
                    sp.wait_ge(x2_done, t + 1)
                    sp.dma_start(x2_v[t], xt[:, t, :]).then_inc(x2_out, 16)
                    sp.wait_ge(h2_done, t + 1)
                    sp.dma_start(h2_v[t], h2[:, t % 2, :]).then_inc(h2_out[t % 2], 16)
                sp.wait_ge(x2_out, 16 * NT)
                for i in range(2):
                    sp.wait_ge(h2_out[i], 16 * NT // 2)

            @block.gpsimd
            def _(pool):
                st = Steps(pool, sel_const)
                st.did(pool.memset(first[:, :], float(SEQ)))
                st.did(pool.memset(own[:, :, :], 1.0))
                st.did(pool.memset(pick[:, :], 0.0))
                st.settle()
                st.did(pool.affine_select(out=first[:, :], in_=first[:, :], compare_op=ALU.is_ge, fill=0.0, base=-NE,
                                          pattern=[[1, 1]], channel_multiplier=1))
                st.did(pool.affine_select(out=own[:, 0, :], in_=own[:, 0, :], compare_op=ALU.is_ge, fill=0.0, base=NE - 1,
                                          pattern=[[0, CAP]], channel_multiplier=-1))
                st.did(pool.affine_select(out=own[:, 1, :], in_=own[:, 1, :], compare_op=ALU.is_ge, fill=0.0, base=-NE,
                                          pattern=[[0, CAP]], channel_multiplier=1))
                for g in range(GROUPS):
                    st.do(pool.affine_select(out=pick[:, :], in_=pick[:, :], compare_op=ALU.not_equal, fill=1.0,
                                             base=-g * NE, pattern=[[-1, NE]], channel_multiplier=1))
                pool.wait_ge(xt_in, 16)
                for t in range(NT):
                    g = t // TPG
                    pool.wait_ge(xm_done, t + 1)
                    pool.tensor_tensor(xt[:, t, :], xt[:, t, :], xm[:, t % 2, :], ALU.add).then_inc(x2_done, 1)
                    pool.wait_ge(ms_done, t + 1)
                    pool.tensor_tensor(rinv[:, t:t + 1], ms[:, t:t + 1], m["neghalf"][:, 0:1], ALU.pow).then_inc(rinv_done, 1)
                    pool.wait_ge(hm_done, t + 1)
                    pool.tensor_tensor(h2[:, t % 2, :], h2[:, t % 2, :], late["shift2"][:, g, :], ALU.add).then_inc(h2_done, 1)

            @block.tensor
            def _(pe):
                ident = m["ident"][:, :]
                pe.wait_ge(late["route_in"], 32)

                def project(t):
                    if t >= 2:
                        pe.wait_ge(xm_done, t - 1)
                    for c in range(2):
                        for k in range(KD):
                            mm = pe.matmul(ps[:, 2 * (t % 2) + c, :], late["mergedT"][:, k, t * P:(t + 1) * P],
                                           late["wout"][:, k, c * 512:(c + 1) * 512], start=(k == 0), stop=(k == KD - 1))
                    mm.then_inc(out_ps, 1)

                def route(t):
                    pe.wait_ge(h2_done, t + 1)
                    if t >= 1:
                        pe.wait_ge(h2T_sb, t)
                    for k in range(KD):
                        mm = pe.transpose(ps[:, 4 + k // 4, (k % 4) * P:(k % 4 + 1) * P],
                                          h2[:, t % 2, k * P:(k + 1) * P], ident)
                    mm.then_inc(h2T_ps, 1)

                def logits(t):
                    pe.wait_ge(h2T_sb, t + 1)
                    if t >= 2:
                        pe.wait_ge(ex_done, t - 1)
                    for k in range(KD):
                        mm = pe.matmul(ps[:, 6 + t % 2, 0:NE], h2T[:, t % 2, k, :], late["wr"][:, k, :],
                                       start=(k == 0), stop=(k == KD - 1))
                    mm.then_inc(logit_ps, 1)

                for t in range(NT + 2):
                    if t < NT:
                        project(t)
                    if 1 <= t <= NT:
                        route(t - 1)
                    if t >= 2:
                        logits(t - 2)
                for t in range(TPG):
                    pe.wait_ge(probs_done, TPG + t + 1)
                    mm = pe.transpose(ps[0:NR, 0, t * P:(t + 1) * P], probs[:, t, :, :].rearrange("p g e -> p (g e)"), ident)
                mm.then_inc(probsT_ps, 1)
                pe.wait_ge(top_step, 3 + 3 * (CAP // 8) + 1)
                for i in range(2):
                    mm = pe.matmul(ps[:, 1, i * NE:(i + 1) * NE], spread[:, i, :, :].rearrange("p g c -> p (g c)"), pick[:, :],
                                   start=True, stop=True)
                mm.then_inc(pick_ps, 1)

            @block.scalar
            def _(act):
                for t in range(NT + 1):
                    if t < NT:
                        act.wait_ge(x2_done, t + 1)
                        if t:
                            act.wait_ge(ssq_done, t)
                        act.activation(junk[:, :], xt[:, t, :], ACT.Square, accum_out=ssq[:, t:t + 1]).then_inc(ssq_done, 1)
                        act.wait_ge(h2T_ps, t + 1)
                        if t >= 2:
                            act.wait_ge(logit_ps, t - 1)
                        act.activation(h2T[:, t % 2, :, :], ps[:, 4:6, :].rearrange("p b (k c) -> p (b k) c", c=P),
                                       ACT.Copy).then_inc(h2T_sb, 1)
                    if t >= 1:
                        v = t - 1
                        act.wait_ge(negmax_done, v + 1)
                        act.activation(ex[:, v, :], ps[:, 6 + v % 2, 0:NE], ACT.Exp, bias=negmax[:, v:v + 1],
                                       accum_out=den[:, v:v + 1]).then_inc(ex_done, 1)

            @block.vector
            def _(dve):
                def softmax_tail(v):
                    dve.wait_ge(logit_ps, v + 1)
                    dve.tensor_reduce(negmax[:, v:v + 1], ps[:, 6 + v % 2, 0:NE], AX_X, ALU.max, negate=True).then_inc(negmax_done, 1)
                    dve.wait_ge(ex_done, v + 1)
                    dve.reciprocal(rden[:, v:v + 1], den[:, v:v + 1]).then_inc(rden_done, 1)
                    dve.wait_ge(rden_done, v + 1)
                    dve.tensor_scalar(probs[:, v % TPG, v // TPG, :], ex[:, v, :], rden[:, v:v + 1], None,
                                      ALU.mult).then_inc(probs_done, 1)

                for t in range(NT + 1):
                    if t < NT:
                        g = t // TPG
                        dve.wait_ge(out_ps, t + 1)
                        if t >= 2:
                            dve.wait_ge(x2_done, t - 1)
                        dve.tensor_tensor(xm[:, t % 2, :], ps[:, 2 * (t % 2):2 * (t % 2) + 2, :].rearrange("p b c -> p (b c)"),
                                          late["gate1"][:, g, :], ALU.mult).then_inc(xm_done, 1)
                        dve.wait_ge(ssq_done, t + 1)
                        dve.tensor_scalar(ms[:, t:t + 1], ssq[:, t:t + 1], 1.0 / D_MODEL, EPS, ALU.mult, ALU.add).then_inc(ms_done, 1)
                        dve.wait_ge(rinv_done, t + 1)
                        if t >= 2:
                            dve.wait_ge(h2_out[t % 2], 16 * (t // 2))
                            dve.wait_ge(h2T_ps, t - 1)
                        dve.scalar_tensor_tensor(out=h2[:, t % 2, :], in0=xt[:, t, :], scalar=rinv[:, t:t + 1],
                                                 in1=late["mul2row"][:, g, :], op0=ALU.mult, op1=ALU.mult).then_inc(hm_done, 1)
                    if t >= 1:
                        softmax_tail(t - 1)
                st = Steps(dve, top_step)
                dve.wait_ge(probsT_ps, 1)
                st.do(dve.tensor_copy(work[:, 0, :], ps[0:NR, 0, :]))
                for r in range(CAP // 8):
                    got = slice(8 * r, 8 * r + 8)
                    st.do(dve.max(vals[:, got], work[:, r % 2, :]))
                    st.did(dve.max_index(idx[:, got], vals[:, got], work[:, r % 2, :]))
                    st.do(dve.match_replace(work[:, 1 - r % 2, :], vals[:, got], work[:, r % 2, :], -1.0))
                dve.wait_ge(sel_const, 8)
                st.do(dve.tensor_scalar(idxf[:, :], idx[:, :], first[:, 0:1], None, ALU.add))
                st.did(dve.tensor_tensor(spread[:, 0, :, :], bcast(vals[:, :], 1, GROUPS), own[:, :, :], ALU.mult))
                st.do(dve.tensor_tensor(spread[:, 1, :, :], bcast(idxf[:, :], 1, GROUPS), own[:, :, :], ALU.mult))
                assert st.n == 3 + 3 * (CAP // 8) + 1
                dve.wait_ge(pick_ps, 1)
                st.did(dve.tensor_copy(m["gates"][:, :], ps[:, 1, 0:NE]))
                st.did(dve.tensor_copy(m["token"][:, 0:NE], ps[:, 1, NE:2 * NE]))
                st.settle()


def phase_experts(nc, a, m, ps, x2_dram, h2_dram):
    NQ4 = 4
    FW = D_EXPERT // NQ4
    FT = FW // P
    ORDER = [("g", 0), ("u", 0), ("g", 1), ("u", 1), ("d", 0), ("g", 2), ("u", 2), ("d", 1), ("g", 3), ("u", 3),
             ("d", 2), ("d", 3)]
    NP_ = len(ORDER)
    PW = KD * FW
    RAW_SLOTS, PART_SLOTS, AHEAD = 4, 3, 2
    pos = {piece: i for i, piece in enumerate(ORDER)}
    TURN_AT = {pos["u", 1]: 0, pos["u", 2]: 1, pos["u", 3]: 2, pos["d", 2]: 3}
    with ExitStack() as ctx:
        def sb(name, shape, dt=F32):
            return ctx.enter_context(nc.sbuf_tensor(name, shape, dt))

        def sem(name):
            return ctx.enter_context(nc.semaphore(name))

        raw = [sb(f"wraw{i}", [P, PW]) for i in range(RAW_SLOTS)]
        whigh = [sb(f"whigh{i}", [P, PW], F32R) for i in range(PART_SLOTS)]
        wlow = [sb(f"wlow{i}", [P, PW], F32R) for i in range(PART_SLOTS)]
        tok_g = sb("tok_g", [P, 1], U32)
        tok_s = sb("tok_s", [P, 1], U32)
        gate = sb("gate_e", [P, 1])
        xe = sb("xe", [P, D_MODEL])
        xeT = sb("xeT", [P, 2, KD, P], F32R)
        sg = sb("sg", [P, 2, FW])
        hid = sb("hid", [P, 2, FW])
        hidT = sb("hidT", [P, 2, 2, FT, P], F32R)
        ye = sb("ye", [P, D_MODEL])

        raw_in = [sem(f"raw_in_e{i}") for i in range(RAW_SLOTS)]
        high_done = sem("high_done")
        low_done = sem("low_done")
        piece_done = sem("piece_done")
        tok_ready = sem("tok_ready")
        xe_in = sem("xe_in")
        xeT_ps = sem("xeT_ps")
        xeT_high = sem("xeT_high")
        xeT_low = sem("xeT_low")
        silu_done = sem("silu_done_e")
        hid_done = sem("hid_done")
        hidT_ps = sem("hidT_ps")
        hidT_high = sem("hidT_high")
        hidT_low = sem("hidT_low")
        ye_done = sem("ye_done")
        gate_ready = sem("gate_ready")
        scattered = sem("scattered")
        gather_go = sem("gather_go")
        scatter_go = sem("scatter_go")
        ye_free = sem("ye_free")

        def loop(eng, body):
            with eng.Fori(0, NE - 1) as e:
                body(e, False)
            body(NE - 1, True)

        def multiplied(eng, e, p):
            eng.wait_ge(piece_done, e * NP_ + (NP_ + p + 1))

        with nc.Block() as block:

            @block.sync
            def _(sp):
                wg = a["w_gate"].rearrange("a e (k p) n -> p (a e) k n", p=P)
                wu = a["w_up"].rearrange("a e (k p) n -> p (a e) k n", p=P)
                wd = a["w_down"].rearrange("a e (k p) n -> p (a e) k n", p=P)
                with sp.Fori(0, NE) as e:
                    for p, (kind, n) in enumerate(ORDER):
                        sp.wait_ge(low_done, e * NP_ + (NP_ + p - RAW_SLOTS + 1))
                        if kind == "d":
                            src = wd[:, bass.ds(e, 1), n * FT:(n + 1) * FT, :]
                        else:
                            src = (wg if kind == "g" else wu)[:, bass.ds(e, 1), :, n * FW:(n + 1) * FW]
                        k = FT if kind == "d" else KD
                        sp.dma_start(raw[p % RAW_SLOTS][:, :].rearrange("p (k n) -> p k n", k=k),
                                     src.rearrange("p e k n -> p (e k) n")).then_inc(raw_in[p % RAW_SLOTS], 16)

            @block.gpsimd
            def _(pool):
                def gather(e_tok, count):
                    pool.tensor_copy(tok_g[:, :], m["token"][:, e_tok]).then_inc(tok_ready, 1)
                    pool.wait_ge(tok_ready, count)
                    pool.sem_inc(gather_go, 1)
                    pool.indirect_dma_start(out=xe[:, :], out_offset=None, in_=h2_dram[:, :],
                                            in_offset=bass.IndirectOffsetOnAxis(ap=tok_g[:, 0:1], axis=0)).then_inc(xe_in, 16)

                prime(pool, ye_free)
                gather(slice(0, 1), 1)

                def body(e, last):
                    pool.wait_ge(xe_in, e * 16 + 16)
                    pool.wait_ge(xeT_ps, e * 2 + 2)
                    if not last:
                        gather(bass.ds(e + 1, 1), e * 2 + 2)
                    pool.tensor_copy(gate[:, :], m["gates"][:, bass.ds(e, 1)]).then_inc(gate_ready, 1)
                    pool.tensor_copy(tok_s[:, :], m["token"][:, bass.ds(e, 1)]).then_inc(tok_ready, 1)
                    pool.wait_ge(tok_ready, e * 2 + (2 if last else 3))
                    pool.wait_ge(ye_done, 1 + e + 1)
                    pool.sem_inc(scatter_go, 1)
                    pool.indirect_dma_start(out=x2_dram[:, :], out_offset=bass.IndirectOffsetOnAxis(ap=tok_s[:, 0:1], axis=0),
                                            in_=ye[:, :], in_offset=None, compute_op=ALU.add).then_inc(scattered, 16)
                    pool.wait_ge(scattered, e * 16 + 16)
                    pool.sem_inc(ye_free, 1)

                loop(pool, body)

            @block.tensor
            def _(pe):
                ident = m["ident"][:, :]
                pe.sem_inc(piece_done, NP_)
                prime(pe, hidT_ps)

                def turn_tokens(half, count_in, count_out):
                    pe.wait_ge(xe_in, count_in)
                    pe.wait_ge(xeT_low, count_out)
                    for k in range(4):
                        mm = pe.transpose(ps[:, 7, k * P:(k + 1) * P], xe[:, (4 * half + k) * P:(4 * half + k + 1) * P], ident)
                    mm.then_inc(xeT_ps, 1)

                def three(out, lhs, rhs, start, stop):
                    for i, (x, y) in enumerate(((0, 0), (0, 1), (1, 0))):
                        mm = pe.matmul(out, lhs[x], rhs[y], start=start and i == 0, stop=stop and i == 2)
                    return mm

                turn_tokens(0, 16, 0)
                turn_tokens(1, 16, 1)

                def body(e, last):
                    def turn_hidden(n):
                        pe.wait_ge(hid_done, 1 + e * NQ4 + n + 1)
                        pe.wait_ge(hidT_low, 1 + e * NQ4 + n)
                        for f in range(FT):
                            mm = pe.transpose(ps[:, 4, f * P:(f + 1) * P], hid[:, n % 2, f * P:(f + 1) * P], ident)
                        mm.then_inc(hidT_ps, 1)

                    for p, (kind, n) in enumerate(ORDER):
                        if kind in "gu":
                            if p in TURN_AT:
                                turn_hidden(TURN_AT[p])
                            pe.wait_ge(low_done, e * NP_ + (NP_ + p + 1))
                            if p == 0:
                                pe.wait_ge(xeT_low, e * 2 + 2)
                            pe.wait_ge(silu_done if kind == "g" else hid_done, 1 + e * NQ4 + max(n - 1, 0))
                            w = [x.rearrange("p (k n) -> p k n", k=KD) for x in (whigh[p % PART_SLOTS][:, :], wlow[p % PART_SLOTS][:, :])]
                            for k in range(KD):
                                mm = three(ps[:, 2 * (n % 2) + (kind == "u"), :], [xeT[:, i, k, :] for i in range(2)],
                                           [w[i][:, k, :] for i in range(2)], k == 0, k == KD - 1)
                            mm.then_inc(piece_done, 1)
                        else:
                            pe.wait_ge(low_done, e * NP_ + (NP_ + p + 1))
                            if n == 0:
                                pe.wait_ge(ye_done, 1 + e)
                            pe.wait_ge(hidT_low, 1 + e * NQ4 + n + 1)
                            w = [x.rearrange("p (k n) -> p k n", k=FT) for x in (whigh[p % PART_SLOTS][:, :], wlow[p % PART_SLOTS][:, :])]
                            for c in range(2):
                                if c == 1 and p in TURN_AT:
                                    turn_hidden(TURN_AT[p])
                                if c == 1 and n >= 2 and not last:
                                    turn_tokens(n - 2, e * 16 + 32, e * 2 + n)
                                for f in range(FT):
                                    mm = three(ps[:, 5 + c, :], [hidT[:, n % 2, i, f, :] for i in range(2)],
                                               [w[i][:, f, c * 512:(c + 1) * 512] for i in range(2)],
                                               n == 0 and f == 0, n == NQ4 - 1 and f == FT - 1)
                            mm.then_inc(piece_done, 1)

                loop(pe, body)

            @block.scalar
            def _(act):
                prime(act, silu_done)

                def tokens(half, count):
                    act.wait_ge(xeT_ps, count)
                    act.activation(xeT[:, 0, 4 * half:4 * half + 4, :], ps[:, 7, :], ACT.Copy).then_inc(xeT_high, 1)

                def high(e, p):
                    slot = p % NP_ % RAW_SLOTS
                    act.wait_ge(raw_in[slot], e * (16 * NP_ // RAW_SLOTS) + 16 * (p // RAW_SLOTS + 1))
                    multiplied(act, e, p - PART_SLOTS)
                    act.activation(whigh[p % PART_SLOTS][:, :], raw[slot][:, :], ACT.Copy).then_inc(high_done, 1)

                tokens(0, 1)
                tokens(1, 2)
                for p in range(AHEAD):
                    high(0, p)

                def body(e, last):
                    def silu(n):
                        multiplied(act, e, pos["g", n])
                        act.wait_ge(hid_done, 1 + e * NQ4 + max(n - 1, 0))
                        act.activation(sg[:, n % 2, :], ps[:, 2 * (n % 2), :], ACT.Silu).then_inc(silu_done, 1)

                    for p, (kind, n) in enumerate(ORDER):
                        if p in TURN_AT:
                            t = TURN_AT[p]
                            multiplied(act, e, pos["d", t - 2] if t >= 2 else pos["d", t + 2] - NP_)
                            act.wait_ge(hidT_ps, 1 + e * NQ4 + t + 1)
                            act.activation(hidT[:, t % 2, 0, :, :], ps[:, 4, :], ACT.Copy).then_inc(hidT_high, 1)
                        if not last or p + AHEAD < NP_:
                            high(e, p + AHEAD)
                        if kind == "g":
                            silu(n)
                        if kind == "d" and n >= 2 and not last:
                            multiplied(act, e, pos["u", 3])
                            tokens(n - 2, e * 2 + (n + 1))

                loop(act, body)

            @block.vector
            def _(dve):
                prime(dve, hid_done, ye_done, hidT_low)
                dve.sem_inc(low_done, NP_)

                def tokens(half, count):
                    dve.wait_ge(xeT_high, count)
                    dve.tensor_tensor(xeT[:, 1, 4 * half:4 * half + 4, :].rearrange("p k c -> p (k c)"), ps[:, 7, :],
                                      xeT[:, 0, 4 * half:4 * half + 4, :].rearrange("p k c -> p (k c)").bitcast(F32),
                                      ALU.subtract).then_inc(xeT_low, 1)

                def low(e, p):
                    slot = p % NP_ % RAW_SLOTS
                    dve.wait_ge(high_done, e * NP_ + (p + 1))
                    dve.tensor_tensor(wlow[p % PART_SLOTS][:, :], raw[slot][:, :], whigh[p % PART_SLOTS][:, :].bitcast(F32),
                                      ALU.subtract).then_inc(low_done, 1)

                tokens(0, 1)
                tokens(1, 2)
                for p in range(AHEAD):
                    low(0, p)

                def body(e, last):
                    for p, (kind, n) in enumerate(ORDER):
                        if p in TURN_AT:
                            t = TURN_AT[p]
                            dve.wait_ge(hidT_high, e * NQ4 + t + 1)
                            dve.tensor_tensor(hidT[:, t % 2, 1, :, :].rearrange("p f c -> p (f c)"), ps[:, 4, :],
                                              hidT[:, t % 2, 0, :, :].rearrange("p f c -> p (f c)").bitcast(F32),
                                              ALU.subtract).then_inc(hidT_low, 1)
                        if not last or p + AHEAD < NP_:
                            low(e, p + AHEAD)
                        if kind == "u":
                            multiplied(dve, e, p)
                            dve.wait_ge(silu_done, 1 + e * NQ4 + n + 1)
                            dve.wait_ge(hidT_ps, 1 + e * NQ4 + max(n - 1, 0))
                            dve.tensor_tensor(hid[:, n % 2, :], sg[:, n % 2, :], ps[:, 2 * (n % 2) + 1, :],
                                              ALU.mult).then_inc(hid_done, 1)
                        if kind == "d" and n >= 2 and not last:
                            tokens(n - 2, e * 2 + (n + 1))
                    multiplied(dve, e, NP_ - 1)
                    dve.wait_ge(gate_ready, e + 1)
                    dve.wait_ge(ye_free, 1 + e)
                    dve.scalar_tensor_tensor(out=ye[:, :], in0=ps[:, 5:7, :].rearrange("p b c -> p (b c)"),
                                             scalar=gate[:, 0:1], in1=m["gate2"][:, :], op0=ALU.mult,
                                             op1=ALU.mult).then_inc(ye_done, 1)

                loop(dve, body)


def phase_finish(nc, a, m, x2_dram, y):
    with ExitStack() as ctx:
        def sb(name, shape, dt=F32):
            return ctx.enter_context(nc.sbuf_tensor(name, shape, dt))

        def sem(name):
            return ctx.enter_context(nc.semaphore(name))

        x3 = sb("x3", [P, NT, D_MODEL])
        fg = sb("fg", [P, D_MODEL])
        junk = sb("junk_f", [P, D_MODEL])
        ssq = sb("ssq_f", [P, NT])
        ms = sb("ms_f", [P, NT])
        rinv = sb("rinv_f", [P, NT])
        fg_in = sem("fg_in")
        x3_in = [sem(f"x3_in{t}") for t in range(NT)]
        ssq_done = sem("ssq_done_f")
        ms_done = sem("ms_done_f")
        rinv_done = sem("rinv_done_f")
        y_done = sem("y_done")
        y_out = sem("y_out")
        with nc.Block() as block:

            @block.sync
            def _(sp):
                sp.dma_start(fg[:, :], bass.AP(a["final_g"].tensor, 0, [[0, P], [1, D_MODEL]])).then_inc(fg_in, 16)
                x_v = x2_dram.rearrange("(t p) c -> t p c", p=P)
                y_v = y.rearrange("(t p) c -> t p c", p=P)
                for t in range(NT):
                    sp.dma_start(x3[:, t, :], x_v[t]).then_inc(x3_in[t], 16)
                for t in range(NT):
                    sp.wait_ge(y_done, t + 1)
                    sp.dma_start(y_v[t], x3[:, t, :]).then_inc(y_out, 16)
                sp.wait_ge(y_out, 16 * NT)

            @block.scalar
            def _(act):
                for t in range(NT):
                    act.wait_ge(x3_in[t], 16)
                    if t:
                        act.wait_ge(ssq_done, t)
                    act.activation(junk[:, :], x3[:, t, :], ACT.Square, accum_out=ssq[:, t:t + 1]).then_inc(ssq_done, 1)

            @block.gpsimd
            def _(pool):
                for t in range(NT):
                    pool.wait_ge(ms_done, t + 1)
                    pool.tensor_tensor(rinv[:, t:t + 1], ms[:, t:t + 1], m["neghalf"][:, 0:1], ALU.pow).then_inc(rinv_done, 1)

            @block.vector
            def _(dve):
                dve.wait_ge(fg_in, 16)
                for t in range(NT + 1):
                    if t < NT:
                        dve.wait_ge(ssq_done, t + 1)
                        dve.tensor_scalar(ms[:, t:t + 1], ssq[:, t:t + 1], 1.0 / D_MODEL, EPS, ALU.mult, ALU.add).then_inc(ms_done, 1)
                    if t >= 1:
                        v = t - 1
                        dve.wait_ge(rinv_done, v + 1)
                        dve.scalar_tensor_tensor(out=x3[:, v, :], in0=x3[:, v, :], scalar=rinv[:, v:v + 1], in1=fg[:, :],
                                                 op0=ALU.mult, op1=ALU.mult).then_inc(y_done, 1)


def build(nc, a, y):
    x2_dram = nc.dram_tensor("x2_dram", (TOK, D_MODEL), F32).ap()
    h2_dram = nc.dram_tensor("h2_dram", (TOK, D_MODEL), F32).ap()
    early_dram = nc.dram_tensor("early_dram", (EARLY_TILES * P, TOK), F32).ap()
    with ExitStack() as outer:
        ps = outer.enter_context(nc.psum_tensor("ps", [P, 8, 512], F32))
        m = {}
        for name, shape, dt in (("ident", [P, P], F32), ("neghalf", [P, 16], F32), ("gate2", [P, D_MODEL], F32),
                                ("gates", [P, NE], F32), ("token", [P, NE], U32)):
            m[name] = outer.enter_context(nc.sbuf_tensor(name, shape, dt))
        with ExitStack() as front:
            m.update(shared_buffers(nc, front))
            phase_prepare(nc, a, m, ps)
            phase_deltanet(nc, a, m, ps, early_dram)
            phase_attention(nc, a, m, ps, early_dram)
            with ExitStack() as ctx:
                late = late_buffers(nc, ctx)
                phase_merge(nc, a, m, ps, late, early_dram)
                phase_route(nc, a, m, ps, late, x2_dram, h2_dram)
        phase_experts(nc, a, m, ps, x2_dram, h2_dram)
        phase_finish(nc, a, m, x2_dram, y)


def kernel(**inputs):
    import numpy as np
    import concourse.bacc as bacc
    from concourse.bass_utils import run_bass_kernel_spmd as run

    nc = bacc.Bacc("TRN2", target_bir_lowering=False, num_devices=1)
    arrays = {n: np.ascontiguousarray(v) for n, v in inputs.items()
              if n not in ("x_prompt", "x_sample", "c_prompt", "c_sample", "rpb")}
    arrays["x"] = np.concatenate([inputs["x_prompt"][0], inputs["x_sample"][0]], axis=0)
    arrays["c"] = np.concatenate([inputs["c_prompt"], inputs["c_sample"]], axis=0)
    arrays["final_g"] = np.ascontiguousarray(inputs["final_g"]).reshape(1, D_MODEL)
    table = np.transpose(np.asarray(inputs["rpb"])[0], (0, 2, 1)).reshape(HB, RPB_C * RPB_R)
    arrays["rpb"] = np.stack([np.pad(table, ((0, 0), (RPB_FRONT + r, RPB_LEN + ROWS - RPB_FRONT - RPB_C * RPB_R - r)))
                              [:, :RPB_LEN] for r in range(ROWS)])
    a = {n: nc.dram_tensor(f"in_{n}", v.shape, mybir.dt.from_np(v.dtype), kind="ExternalInput").ap()
         for n, v in arrays.items()}
    y = nc.dram_tensor("out_y", (TOK, D_MODEL), F32, kind="ExternalOutput").ap()
    build(nc, a, y)
    r = run(nc, [{f"in_{n}": v for n, v in arrays.items()}], core_ids=[0])
    got = r.results[0]["out_y"]
    return got[None, :SEQ], got[None, SEQ:]
```

```python
from contextlib import ExitStack

import concourse.bass as bass
from concourse import mybir

F32 = mybir.dt.float32
F32R = mybir.dt.float32r
U32 = mybir.dt.uint32
ALU = mybir.AluOpType
ACT = mybir.ActivationFunctionType
AX_X = mybir.AxisListType.X

P = 128
D_MODEL = 1024
SEQ = 512
GROUPS = 2
TOK = GROUPS * SEQ
KD = D_MODEL // P
TPG = SEQ // P
NT = TOK // P
GRID_W = 64
ROWS = SEQ // GRID_W
HA = 4
DK = 128
CONV_K = 5
CHUNK = 64
NCHUNK = SEQ // CHUNK
HB = 8
DH = 64
PAIRS = HB * DH // P
WIN_ROWS = 8
WIN_COLS = 16
NE = 16
CAP = 2 * SEQ // NE
D_EXPERT = 2048
EPS = 1e-6
BIG = 1e30
A_W = HA * DK
OFF_Z = 3 * A_W
OFF_SMALL = 4 * A_W
OFF_QB = OFF_SMALL + 4 * HA
OFF_GA = OFF_QB + 3 * HB * DH
OFF_GB = OFF_GA + D_MODEL
ADA_BLOCK = 512
ADA_FIRST = 2 * D_MODEL // ADA_BLOCK
ADA_TILES = ADA_BLOCK // P
EARLY_TILES = (3 * HB * DH + 2 * D_MODEL) // P
GATE_TILE = 3 * HB * DH // P
BETA, CUM, ECUM, BECUM, EREST, LOGD, ETOT = range(7)
NQ = 8
VB, VN1, VC = 0, 16, 24
VROWS = 40
CROWS = 12 * CONV_K + 1
LEVELS = 6
WCOLS = 48
RPB_C = 2 * WIN_COLS - 1
RPB_R = 2 * WIN_ROWS - 1
RPB_FRONT = 15 * RPB_R + 7 + 8
RPB_RUN = WCOLS * RPB_R
RPB_LEN = RPB_FRONT + RPB_RUN
KEY_TILES = [(0, 2), (0, 3), (1, 4), (2, 4)]


class Steps:

    def __init__(self, eng, sem, before=0):
        self.eng, self.sem, self.before, self.n = eng, sem, before, 0

    def did(self, ins):
        ins.then_inc(self.sem, 1)
        self.n += 1

    def settle(self):
        self.eng.wait_ge(self.sem, self.before + self.n)

    def do(self, ins):
        self.did(ins)
        self.settle()


def bcast(ap, axis, n):
    ap = ap.unsqueeze(axis)
    shape = list(ap.shape)
    shape[axis] = n
    return ap.to_broadcast(shape)


def prime(eng, *sems):
    for sem in sems:
        eng.sem_inc(sem, 1)


def shared_buffers(nc, ctx, outer):
    def sb(name, shape, dt=F32):
        return ctx.enter_context(nc.sbuf_tensor(name, shape, dt))

    m = {name: outer.enter_context(nc.sbuf_tensor(name, shape, F32))
         for name, shape in (("hT", [P, KD, TOK]), ("oaT", [P, HA, TOK]), ("obT", [P, PAIRS, TOK]))}

    m["ones"] = sb("ones", [P, P])
    m["upto"] = sb("upto", [P, 2, P])
    m["vecT"] = sb("vecT", [P, VROWS])
    m["convT"] = sb("convT", [P, CROWS])
    m["modT"] = sb("modT", [P, 2 * KD, GROUPS])
    m["sc"] = sb("sc", [P, KD, GROUPS])
    m["tab"] = sb("tab", [P, NQ, NT, 2 * HA])
    return m


def first_buffers(nc, ctx):
    first = {"w4": ctx.enter_context(nc.sbuf_tensor("w4", [P, 4, KD, P], F32)),
             "levelmask": ctx.enter_context(nc.sbuf_tensor("levelmask", [P, 2, LEVELS, P], F32)),
             "posmask": ctx.enter_context(nc.sbuf_tensor("posmask", [P, 2, P], F32)),
             "w4_in": ctx.enter_context(nc.semaphore("w4_in"))}
    return first


def load_w4(eng, a, first, h, ahead=0):
    w_in = a["w_in"].rearrange("a (k p) n -> p (a k) n", p=P)
    for b in range(4):
        eng.dma_start(first["w4"][:, b, :, :], w_in[:, :, bass.ds(h * P + (b * A_W + ahead * P), P)]).then_inc(first["w4_in"], 16)


def phase_prepare(nc, a, m, ps, first):
    with ExitStack() as ctx:
        def sb(name, shape, dt=F32):
            return ctx.enter_context(nc.sbuf_tensor(name, shape, dt))

        def sem(name):
            return ctx.enter_context(nc.semaphore(name))

        rows = sb("rows", [VROWS, P])
        crows = sb("crows", [CROWS, P])
        ada = sb("ada", [P, ADA_FIRST, KD, ADA_BLOCK])
        xt = sb("xt", [P, NT, D_MODEL])
        junk = sb("junk", [P, D_MODEL])
        smallT = junk[0:4 * HA, :].rearrange("p (g t) -> p g t", g=GROUPS)
        wsm = sb("wsm", [P, KD, 4 * HA])
        alog = sb("alog", [P, 2 * HA])
        dtb = sb("dtb", [P, 2 * HA])
        ealog = sb("ealog", [P, 2 * HA])
        ssq = sb("ssq", [P, NT])
        ms = sb("ms", [P, NT])
        rinv = sb("rinv", [P, NT])
        modrow = m["oaT"][0:GROUPS, 0:2, :].rearrange("p h (b c) -> p (h b) c", c=ADA_BLOCK)
        mul1 = sb("mul1", [P, KD, GROUPS])
        al = sb("al", [P, NT, 2 * HA])
        nal = sb("nal", [P, NT, 2 * HA])
        sp1 = sb("sp1", [P, NT, 2 * HA])
        eb = sb("eb", [P, NT, 2 * HA])
        rest = sb("rest", [P, NT, 2 * HA])
        same = sb("same", [P, P])
        half = sb("half", [P, 2, P])
        tab = m["tab"]

        vec_in = sem("vec_in")
        ada_in = [sem(f"ada_in{i}") for i in range(ADA_FIRST)]
        x_in = [sem(f"x_in{g}") for g in range(GROUPS)]
        small_in = sem("small_in")
        pool_step = sem("pool_step_a")
        dve_step = sem("dve_step_a")
        consts = sem("consts")
        vec_ps = sem("vec_ps")
        vec_sb = sem("vec_sb")
        mod_ps = sem("mod_ps")
        modrow_ps = sem("modrow_ps")
        modrow_sb = sem("modrow_sb")
        smallT_ps = sem("smallT_ps")
        smallT_sb = sem("smallT_sb")
        mul_ready = sem("mul_ready")
        ssq_done = sem("ssq_done")
        ms_done = sem("ms_done")
        rinv_done = sem("rinv_done")
        xn_done = sem("xn_done")
        xT_ps = sem("xT_ps")
        hT_act = sem("hT_act")
        hT_dve = sem("hT_dve")
        small_ps = sem("small_ps")
        al_done = sem("al_done")
        nal_done = sem("nal_done")
        act_step = sem("act_step_a")
        logd_done = sem("logd_done")
        cum_ps = sem("cum_ps")
        cum_sb = sem("cum_sb")

        with nc.Block() as block:

            @block.sync
            def _(sp):
                for dst, src in (
                    (rows[VB:VB + 16, :], a["b_ada"][:, 0:2 * D_MODEL].rearrange("a (r c) -> (a r) c", c=P)),
                    (rows[VN1:VN1 + 8, :], a["norm1_g"].rearrange("a (r c) -> (a r) c", c=P)),
                    (rows[VC:VC + 16, :], a["c"].rearrange("a (r c) -> (a r) c", c=P)),
                    (crows[0:60, :], a["conv_w"].rearrange("a t (r c) -> (a t r) c", c=P)),
                    (crows[60:61, :], a["gn_w"]),
                ):
                    sp.dma_start(dst, src).then_inc(vec_in, 16)
                x_v = a["x"].rearrange("(t p) c -> p t c", p=P)
                w_ada = a["w_ada"].rearrange("a (k p) n -> p (a k) n", p=P)
                for g in range(GROUPS):
                    sp.dma_start(xt[:, g * TPG:(g + 1) * TPG, :], x_v[:, g * TPG:(g + 1) * TPG, :]).then_inc(x_in[g], 16)
                    for b in (2 * g, 2 * g + 1):
                        sp.dma_start(ada[:, b, :, :], w_ada[:, :, b * ADA_BLOCK:(b + 1) * ADA_BLOCK]).then_inc(ada_in[b], 16)
                w_in = a["w_in"].rearrange("a (k p) n -> p (a k) n", p=P)
                sp.dma_start(wsm[:, :, :], w_in[:, :, OFF_SMALL:OFF_SMALL + 4 * HA]).then_inc(small_in, 16)
                sp.dma_start(alog[:, :], bass.AP(a["a_log"].tensor, 0, [[0, P], [1, 2 * HA]])).then_inc(small_in, 16)
                sp.dma_start(dtb[:, :], bass.AP(a["dt_bias"].tensor, 0, [[0, P], [1, 2 * HA]])).then_inc(small_in, 16)

                load_w4(sp, a, first, 0)

            @block.gpsimd
            def _(pool):
                st = Steps(pool, pool_step)
                st.did(pool.memset(m["ident"][:, :], 0.0))
                st.did(pool.memset(m["ones"][:, :], 1.0))
                st.did(pool.memset(m["neghalf"][:, :], -0.5))
                st.did(pool.memset(m["upto"][:, :, :], 1.0))
                st.did(pool.memset(same[:, :], 0.0))
                st.did(pool.memset(half[:, :, :], 0.0))
                st.settle()
                pool.affine_select(out=m["ident"][:, :], in_=m["ident"][:, :], compare_op=ALU.not_equal, fill=1.0,
                                   base=0, pattern=[[-1, P]], channel_multiplier=1).then_inc(consts, 1)
                for d, sign in ((0, 1), (1, -1)):
                    st.did(pool.affine_select(out=m["upto"][:, d, :], in_=m["upto"][:, d, :], compare_op=ALU.is_ge,
                                              fill=0.0, base=0, pattern=[[sign, P]], channel_multiplier=-sign))
                st.settle()
                st.did(pool.memset(m["upto"][0:CHUNK, 0, CHUNK:P], 0.0))
                st.did(pool.memset(m["upto"][CHUNK:P, 1, 0:CHUNK], 0.0))
                for c in range(2):
                    own = slice(c * CHUNK, (c + 1) * CHUNK)
                    st.did(pool.memset(same[own, own], 1.0))
                    st.did(pool.memset(half[own, c, :], 1.0))
                st.settle()
                pool.sem_inc(consts, 1)
                pool.wait_ge(ms_done, 1)
                pool.tensor_tensor(rinv[:, :], ms[:, :], m["neghalf"][:, 0:NT], ALU.pow).then_inc(rinv_done, 1)
                levelmask = first["levelmask"]
                st.did(pool.memset(levelmask[:, :, :, :], 0.0))
                st.settle()
                for d in range(2):
                    for lv in range(LEVELS):
                        s = 2 ** lv
                        part = levelmask[:, d, lv, :].rearrange("p (b u s) -> p b u s", u=2, s=s)[:, :, d, :]
                        st.do(pool.memset(part, 1.0))
                        lo = s if d == 0 else 0
                        pat = [[-2 * s, P // (2 * s)], [0, s]]
                        st.do(pool.affine_select(out=part, in_=part, compare_op=ALU.is_ge, fill=0.0, base=-lo,
                                                 pattern=pat, channel_multiplier=1))
                        st.do(pool.affine_select(out=part, in_=part, compare_op=ALU.is_ge, fill=0.0, base=lo + s - 1,
                                                 pattern=[[2 * s, P // (2 * s)], [0, s]], channel_multiplier=-1))

            @block.tensor
            def _(pe):
                pe.wait_ge(vec_in, 80)
                pe.wait_ge(consts, 1)
                pe.transpose(ps[:, 0, 0:VROWS], rows[:, :], m["ident"][0:VROWS, 0:VROWS])
                pe.transpose(ps[:, 0, P:P + CROWS], crows[:, :], m["ident"][0:CROWS, 0:CROWS]).then_inc(vec_ps, 1)
                pe.wait_ge(vec_sb, 3)
                for b in range(ADA_FIRST):
                    pe.wait_ge(ada_in[b], 16)
                    for k in range(KD):
                        mm = pe.matmul(ps[0:GROUPS, 2 + b, :], m["sc"][:, k, :], ada[:, b, k, :],
                                       start=(k == 0), stop=(k == KD - 1))
                    mm.then_inc(modrow_ps, 1)
                for b in range(ADA_FIRST):
                    pe.wait_ge(modrow_sb, b + 1)
                    for j in range(ADA_TILES):
                        c = 2 * (b * ADA_TILES + j)
                        mm = pe.transpose(ps[:, 1, c:c + 2], modrow[:, b, j * P:(j + 1) * P], m["ident"][0:GROUPS, 0:GROUPS])
                mm.then_inc(mod_ps, 1)
                for n in range(GROUPS * KD):
                    g, k = divmod(n, KD)
                    if k == 0:
                        pe.wait_ge(xn_done, TPG * (g + 1))
                    if n >= 6:
                        pe.wait_ge(hT_dve if n % 2 == 0 else hT_act, (n - 6) // 2 + 1)
                    for t in range(TPG):
                        mm = pe.transpose(ps[:, 2 + n % 6, t * P:(t + 1) * P], xt[:, g * TPG + t, k * P:(k + 1) * P],
                                          m["ident"][:, :])
                    mm.then_inc(xT_ps, 1)
                pe.wait_ge(hT_dve, KD)
                pe.wait_ge(hT_act, KD)
                pe.wait_ge(small_in, 48)
                for g in range(GROUPS):
                    for k in range(KD):
                        mm = pe.matmul(ps[0:4 * HA, 2 + g, :], wsm[:, k, :], m["hT"][:, k, g * SEQ:(g + 1) * SEQ],
                                       start=(k == 0), stop=(k == KD - 1))
                    mm.then_inc(smallT_ps, 1)
                for t in range(NT):
                    g = t // TPG
                    pe.wait_ge(smallT_sb, g + 1)
                    mm = pe.transpose(ps[:, 0, t * 16:(t + 1) * 16], smallT[:, g, (t % TPG) * P:(t % TPG + 1) * P],
                                      m["ident"][0:4 * HA, 0:4 * HA])
                mm.then_inc(small_ps, 1)
                pe.wait_ge(logd_done, 1)
                pe.wait_ge(consts, 2)
                logd = tab[:, LOGD, :, :]
                for d in range(2):
                    pe.matmul(ps[:, 1, 32 * d:32 * d + 32], m["upto"][:, d, :], logd[:, :, d * HA:(d + 1) * HA],
                              start=True, stop=True)
                pe.matmul(ps[:, 1, 64:128], same[:, :], logd, start=True, stop=True)
                for c in range(2):
                    mm = pe.matmul(ps[:, 1, 128 + 64 * c:192 + 64 * c], half[:, c, :], logd, start=True, stop=True)
                mm.then_inc(cum_ps, 1)

            @block.scalar
            def _(act):
                st = Steps(act, act_step)
                act.wait_ge(vec_ps, 1)
                act.activation(m["vecT"][:, :], ps[:, 0, 0:VROWS], ACT.Copy).then_inc(vec_sb, 1)
                act.activation(m["convT"][:, :], ps[:, 0, P:P + CROWS], ACT.Copy).then_inc(vec_sb, 1)
                act.activation(m["sc"][:, :, :], ps[:, 0, VC:VC + 16].rearrange("p (g k) -> p k g", g=GROUPS),
                               ACT.Silu).then_inc(vec_sb, 1)
                for t in range(NT):
                    if t % TPG == 0:
                        act.wait_ge(x_in[t // TPG], 16)
                    if t:
                        act.wait_ge(ssq_done, t)
                    act.activation(junk[:, :], xt[:, t, :], ACT.Square, accum_out=ssq[:, t:t + 1]).then_inc(ssq_done, 1)
                act.wait_ge(mul_ready, 2)
                for n in range(1, GROUPS * KD, 2):
                    g, k = divmod(n, KD)
                    act.wait_ge(xT_ps, n + 1)
                    act.activation(m["hT"][:, k, g * SEQ:(g + 1) * SEQ], ps[:, 2 + n % 6, :], ACT.Identity,
                                   bias=m["modT"][:, k, g:g + 1], scale=mul1[:, k, g:g + 1]).then_inc(hT_act, 1)
                for g in range(GROUPS):
                    act.wait_ge(smallT_ps, g + 1)
                    act.wait_ge(ssq_done, NT)
                    act.activation(smallT[:, g, :], ps[0:4 * HA, 2 + g, :], ACT.Copy).then_inc(smallT_sb, 1)
                act.wait_ge(small_in, 48)
                st.did(act.activation(ealog[:, :], alog[:, :], ACT.Exp))
                small = ps[:, 0, 0:P].rearrange("p (t c) -> p t c", t=NT)
                act.wait_ge(al_done, 1)
                st.did(act.activation(eb[:, :, :], small[:, :, 0:2 * HA], ACT.Exp, scale=-1.0))
                act.activation(nal[:, :, :], nal[:, :, :], ACT.Exp).then_inc(nal_done, 1)
                act.wait_ge(al_done, 2)
                act.activation(sp1[:, :, :], sp1[:, :, :], ACT.Ln).then_inc(nal_done, 1)
                act.wait_ge(cum_sb, 1)
                for d in range(2):
                    act.activation(tab[:, ECUM, :, d * HA:(d + 1) * HA],
                                   ps[:, 1, 32 * d:32 * d + 32].rearrange("p (t h) -> p t h", t=NT),
                                   ACT.Exp).then_inc(act_step, 1)
                act.activation(tab[:, ETOT:ETOT + 2, :, :],
                               ps[:, 1, 128:256].rearrange("p (c t h) -> p c t h", c=2, t=NT), ACT.Exp).then_inc(act_step, 1)
                act.activation(tab[:, EREST, :, :], rest[:, :, :], ACT.Exp).then_inc(act_step, 1)

            @block.vector
            def _(dve):
                st = Steps(dve, dve_step)
                dve.wait_ge(consts, 2)
                for d in range(2):
                    st.did(dve.tensor_scalar(first["posmask"][:, d, :], m["upto"][:, 1 - d, :], -BIG, BIG, ALU.mult, ALU.add))
                dve.wait_ge(ssq_done, NT)
                dve.tensor_scalar(ms[:, :], ssq[:, :], 1.0 / D_MODEL, EPS, ALU.mult, ALU.add).then_inc(ms_done, 1)
                dve.wait_ge(rinv_done, 1)
                for t in range(NT):
                    dve.tensor_scalar(xt[:, t, :], xt[:, t, :], rinv[:, t:t + 1], None, ALU.mult).then_inc(xn_done, 1)
                for b in range(ADA_FIRST):
                    dve.wait_ge(modrow_ps, b + 1)
                    dve.tensor_copy(modrow[:, b, :], ps[0:GROUPS, 2 + b, :]).then_inc(modrow_sb, 1)
                dve.wait_ge(mod_ps, 1)
                dve.wait_ge(vec_sb, 2)
                n1 = 2 * KD
                dve.tensor_tensor(m["modT"][:, 0:n1, :], ps[:, 1, 0:2 * n1].rearrange("p (j g) -> p j g", g=GROUPS),
                                  bcast(m["vecT"][:, VB:VB + n1], 2, GROUPS), ALU.add).then_inc(mul_ready, 1)
                dve.wait_ge(mul_ready, 1)
                dve.scalar_tensor_tensor(out=mul1[:, :, :], in0=m["modT"][:, KD:n1, :], scalar=1.0,
                                         in1=bcast(m["vecT"][:, VN1:VN1 + 8], 2, GROUPS),
                                         op0=ALU.add, op1=ALU.mult).then_inc(mul_ready, 1)
                dve.wait_ge(mul_ready, 2)
                for n in range(0, GROUPS * KD, 2):
                    g, k = divmod(n, KD)
                    dve.wait_ge(xT_ps, n + 1)
                    dve.tensor_scalar(m["hT"][:, k, g * SEQ:(g + 1) * SEQ], ps[:, 2 + n % 6, :],
                                      mul1[:, k, g:g + 1], m["modT"][:, k, g:g + 1], ALU.mult, ALU.add).then_inc(hT_dve, 1)
                dve.wait_ge(small_ps, 1)
                dve.wait_ge(small_in, 48)
                small = ps[:, 0, 0:P].rearrange("p (t c) -> p t c", t=NT)
                st.do(dve.tensor_tensor(al[:, :, :], small[:, :, 2 * HA:4 * HA], bcast(dtb[:, :], 1, NT), ALU.add))
                dve.scalar_tensor_tensor(out=nal[:, :, :], in0=al[:, :, :], scalar=-1.0, in1=al[:, :, :],
                                         op0=ALU.mult, op1=ALU.min).then_inc(al_done, 1)
                dve.wait_ge(nal_done, 1)
                dve.tensor_scalar(sp1[:, :, :], nal[:, :, :], 1.0, None, ALU.add).then_inc(al_done, 1)
                dve.wait_ge(nal_done, 2)
                st.do(dve.scalar_tensor_tensor(out=al[:, :, :], in0=al[:, :, :], scalar=0.0, in1=sp1[:, :, :],
                                               op0=ALU.max, op1=ALU.add))
                dve.wait_ge(act_step, 2)
                dve.scalar_tensor_tensor(out=tab[:, LOGD, :, :], in0=al[:, :, :], scalar=-1.0,
                                         in1=bcast(ealog[:, :], 1, NT), op0=ALU.mult, op1=ALU.mult).then_inc(logd_done, 1)
                st.do(dve.tensor_scalar(eb[:, :, :], eb[:, :, :], 1.0, None, ALU.add))
                st.do(dve.reciprocal(tab[:, BETA, :, :], eb[:, :, :]))
                dve.wait_ge(cum_ps, 1)
                for d in range(2):
                    st.did(dve.tensor_copy(tab[:, CUM, :, d * HA:(d + 1) * HA],
                                           ps[:, 1, 32 * d:32 * d + 32].rearrange("p (t h) -> p t h", t=NT)))
                st.settle()
                dve.tensor_tensor(rest[:, :, :], ps[:, 1, 64:128].rearrange("p (t h) -> p t h", t=NT),
                                  tab[:, CUM, :, :], ALU.subtract).then_inc(cum_sb, 1)
                dve.wait_ge(act_step, 5)
                st.do(dve.tensor_tensor(tab[:, BECUM, :, :], tab[:, BETA, :, :], tab[:, ECUM, :, :], ALU.mult))


def phase_deltanet(nc, a, m, ps, early_dram, mod_dram, first):
    NPROJ = 4 * GROUPS
    ETILES = EARLY_TILES // HA
    EUNITS = ETILES * GROUPS // 2
    with ExitStack() as ctx:
        def sb(name, shape, dt=F32):
            return ctx.enter_context(nc.sbuf_tensor(name, shape, dt))

        sems = []

        def sem(name):
            sems.append(nc.alloc_semaphore(name))
            return sems[-1]

        w4, levelmask, posmask = first["w4"], first["levelmask"], first["posmask"]
        ada = sb("ada_d", [P, KD, ADA_BLOCK])
        pickrow = sb("pickrow", [P, GROUPS, GROUPS])
        brow = sb("brow", [GROUPS, ADA_BLOCK])
        modrow = sb("modrow_d", [GROUPS, ADA_BLOCK])
        pre = sb("pre", [P, 2, SEQ + CONV_K - 1])
        conv = sb("conv", [P, 3, GROUPS, SEQ])
        zT = sb("zT", [P, GROUPS, SEQ])
        cw = sb("cw", [P, CONV_K * 3])
        hd = sb("hd", [P, NQ, NT, 2])
        junk = sb("junk_d", [P, P])
        ssqk = sb("ssqk", [P, 2 * TPG])
        msqk = sb("msqk", [P, 2 * TPG])
        rqk = sb("rqk", [P, 2 * TPG])
        qn = sb("qn", [P, TPG, P])
        kn = sb("kn", [P, TPG, P])
        qnT = sb("qnT", [P, TPG, P])
        knT = sb("knT", [P, TPG, P])
        vb = [sb(f"vb{d}", [P, TPG, P]) for d in range(2)]
        kbe = [sb(f"kbe{d}", [P, TPG, P]) for d in range(2)]
        kd = [sb(f"kd{d}", [P, TPG, P]) for d in range(2)]
        qe = [sb(f"qe{d}", [P, TPG, P]) for d in range(2)]
        qeT = [sb(f"qeT{d}", [P, TPG, P]) for d in range(2)]
        gsum = [sb(f"gsum{d}", [P, TPG, P]) for d in range(2)]
        dec = [sb(f"dec{d}", [P, TPG, P]) for d in range(2)]
        xb = [sb(f"xb{d}", [P, TPG, P]) for d in range(2)]
        xbT = [sb(f"xbT{d}", [P, TPG, P]) for d in range(2)]
        qkT = [sb(f"qkT{d}", [P, TPG, P]) for d in range(2)]
        inv = [sb(f"inv{d}", [P, 2, TPG, P]) for d in range(2)]
        vnew = [sb(f"vnew{d}", [P, TPG, P]) for d in range(2)]
        state = [sb(f"state{d}", [P, NCHUNK, P]) for d in range(2)]
        ssqo = sb("ssqo", [P, TPG])
        mso = sb("mso", [P, TPG])
        ro = sb("ro", [P, TPG])
        on = sb("on", [P, TPG, P])

        spare = m["obT"][:, :, :].rearrange("p h t -> p (h t)")
        we = [spare[:, i * D_MODEL:(i + 1) * D_MODEL].rearrange("p (k c) -> p k c", k=KD) for i in range(2)]
        modacc = spare[:, 2 * D_MODEL + GROUPS * SEQ:].rearrange("p (g c) -> p g c", g=GROUPS)
        est = [spare[:, 2 * D_MODEL + i * SEQ:2 * D_MODEL + (i + 1) * SEQ] for i in range(GROUPS)]

        we_in = [sem(f"we_in{i}") for i in range(2)]
        early_ps = sem("early_ps")
        early_sb = sem("early_sb")
        early_out = [sem(f"early_out{g}") for g in range(GROUPS)]
        ada_in = sem("ada_in_d")
        acc_done = sem("acc_done")
        brow_in = sem("brow_in")
        row_out = sem("row_out")
        row_free = sem("row_free")
        pads = sem("pads")
        pool_step = sem("pool_step_d")
        dve_step = sem("dve_step_d")
        hd_ready = sem("hd_ready")
        proj_ps = sem("proj_ps")
        proj_read = sem("proj_read")
        conv_done = sem("conv_done")
        silu_done = sem("silu_done")
        mod_ps = sem("mod_ps_d")
        mod_done = sem("mod_done_d")
        tok_ps = sem("tok_ps")
        sq_done = sem("sq_done")
        ms_done = sem("ms_done_d")
        rqk_done = sem("rqk_done")
        qn_done = sem("qn_done")
        kn_done = sem("kn_done")
        vb_done = sem("vb_done")
        chn_ps = sem("chn_ps")
        chn_sb = sem("chn_sb")
        gsum_done = sem("gsum_done")
        row_ps = [sem(f"row_ps{d}") for d in range(2)]
        diff_done = [sem(f"diff_done{d}") for d in range(2)]
        dec_done = [sem(f"dec_done{d}") for d in range(2)]
        qe_done = sem("qe_done")
        qeT_ps = sem("qeT_ps")
        qeT_sb = sem("qeT_sb")
        gram_ps = sem("gram_ps")
        x_done = [sem(f"x_done{d}") for d in range(2)]
        xT_ps = [sem(f"xT_ps_d{d}") for d in range(2)]
        xT_sb = [sem(f"xT_sb_d{d}") for d in range(2)]
        kbe_done = sem("kbe_done")
        inv0_done = [sem(f"inv0_done{d}") for d in range(2)]
        y_ps = [sem(f"y_ps{d}") for d in range(2)]
        y_sb = [sem(f"y_sb{d}") for d in range(2)]
        upd_ps = [sem(f"upd_ps{d}") for d in range(2)]
        inv_done = [sem(f"inv_done{d}") for d in range(2)]
        invT_ps = [sem(f"invT_ps{d}") for d in range(2)]
        invT_sb = [sem(f"invT_sb{d}") for d in range(2)]
        uw_ps = [sem(f"uw_ps{d}") for d in range(2)]
        uw_sb = [sem(f"uw_sb{d}") for d in range(2)]
        ws_ps = [sem(f"ws_ps{d}") for d in range(2)]
        vnew_done = [sem(f"vnew_done{d}") for d in range(2)]
        kv_ps = [sem(f"kv_ps{d}") for d in range(2)]
        state_done = [sem(f"state_done{d}") for d in range(2)]
        o_ps = sem("o_ps")
        osq_done = sem("osq_done")
        mso_done = sem("mso_done")
        ro_done = sem("ro_done")
        on_done = sem("on_done")
        oT_ps = sem("oT_ps")
        oa_done = sem("oa_done")

        LV = LEVELS - 1
        NC1 = NCHUNK - 1
        FILL = (0, 1)
        D_STEPS = 1 + 3 * GROUPS * (CONV_K - 1)

        def chunks(d):
            return range(NCHUNK) if d == 0 else range(NCHUNK - 1, -1, -1)

        def place(c):
            return c // 2, slice(CHUNK * (c % 2), CHUNK * (c % 2) + CHUNK)

        early_v = early_dram.rearrange("(w p) t -> p w t", p=P)
        with nc.Block() as block:

            @block.sync
            def _(sp):
                w_in = a["w_in"].rearrange("a (k p) n -> p (a k) n", p=P)
                w_ada = a["w_ada"].rearrange("a (k p) n -> p (a k) n", p=P)
                b_ada = bass.AP(a["b_ada"].tensor, 0, [[0, GROUPS], [1, 6 * D_MODEL]])
                prime(sp, row_free)

                def store_row(h, g):
                    sp.wait_ge(mod_done, h * GROUPS + (g + 1))
                    sp.dma_start(mod_dram[:, bass.ds(h * (GROUPS * ADA_BLOCK) + (ADA_FIRST + g) * ADA_BLOCK, ADA_BLOCK)],
                                 modrow[:, :]).then_inc(row_out, 16)
                    sp.wait_ge(row_out, h * (16 * GROUPS) + 16 * (g + 1))
                    sp.sem_inc(row_free, 1)

                def body(h, last):
                    def early_weights(i):
                        sp.wait_ge(early_ps, 1 + h * (GROUPS * ETILES) + GROUPS * max(i - 1, 0))
                        sp.dma_start(we[i % 2][:, :, :], w_in[:, :, bass.ds(h * (ETILES * P) + (OFF_QB + i * P), P)]).then_inc(
                            we_in[i % 2], 16)

                    early_weights(0)
                    early_weights(1)
                    for b in range(2):
                        if b == 1:
                            early_weights(2)
                        sp.wait_ge(mod_ps, 1 + 2 * h + b)
                        if b == 1:
                            store_row(h, 0)
                        sp.dma_start(brow[:, :], b_ada[:, bass.ds(h * (2 * ADA_BLOCK) + (ADA_FIRST + b) * ADA_BLOCK,
                                                                  ADA_BLOCK)]).then_inc(brow_in, 16)
                        sp.dma_start(ada[:, :, :], w_ada[:, :, bass.ds(h * (2 * ADA_BLOCK) + (ADA_FIRST + b) * ADA_BLOCK,
                                                                       ADA_BLOCK)]).then_inc(ada_in, 16)
                    for i in range(3, ETILES):
                        early_weights(i)
                    store_row(h, 1)
                    if not last:
                        sp.wait_ge(proj_ps, 1 + h * NPROJ + NPROJ)
                        load_w4(sp, a, first, h, ahead=1)

                with sp.Fori(0, HA - 1) as h:
                    body(h, False)
                body(HA - 1, True)

            @block.gpsimd
            def _(pool):
                st = Steps(pool, pool_step)
                st.do(pool.memset(pickrow[:, :, :], 0.0))
                for g in range(GROUPS):
                    st.did(pool.memset(pickrow[:, g, g:g + 1], 1.0))
                st.did(pool.memset(pre[:, :, 0:2], 0.0))
                st.did(pool.memset(pre[:, :, SEQ + 2:SEQ + 4], 0.0))
                st.settle()
                pool.sem_inc(pads, 1)

                with pool.Fori(0, HA) as h:
                    for g in range(GROUPS):
                        n = h * GROUPS + g
                        tiles = slice(g * TPG, (g + 1) * TPG)
                        if g == 0:
                            pool.wait_ge(hd_ready, h + 1)
                        for d in range(2):
                            if g == 1:
                                pool.wait_ge(row_ps[d], n)
                            pool.tensor_tensor(gsum[d][:, :, :], bcast(m["upto"][:, d, :], 1, TPG),
                                               bcast(hd[:, LOGD, tiles, d], 2, P), ALU.mult).then_inc(gsum_done, 1)
                        pool.wait_ge(ms_done, n + 1)
                        pool.tensor_tensor(rqk[:, :], msqk[:, :], m["neghalf"][:, 0:2 * TPG], ALU.pow).then_inc(rqk_done, 1)
                        pool.wait_ge(qn_done, n + 1)
                        for d in range(2):
                            pool.tensor_tensor(qe[d][:, :, :], qn[:, :, :], bcast(hd[:, ECUM, tiles, d], 2, P),
                                               ALU.mult).then_inc(qe_done, 1)
                        for d in range(2):
                            pool.wait_ge(x_done[d], 2 * n + 2)
                            pool.wait_ge(xT_sb[d], 2 * n + 1)
                            for side, src in enumerate((xb[d], xbT[d])):
                                pool.tensor_tensor(inv[d][:, side, :, :], src[:, :, :],
                                                   bcast(levelmask[:, (d + side) % 2, 0, :], 1, TPG),
                                                   ALU.mult).then_inc(inv0_done[d], 1)
                            pool.wait_ge(inv0_done[d], 4 * n + 2)
                            for side in range(2):
                                pool.tensor_tensor(inv[d][:, side, :, :], bcast(m["ident"][:, :], 1, TPG),
                                                   inv[d][:, side, :, :], ALU.subtract).then_inc(inv0_done[d], 1)
                        pool.wait_ge(kn_done, n + 1)
                        for d in range(2):
                            pool.tensor_tensor(kbe[d][:, :, :], kn[:, :, :], bcast(hd[:, BECUM, tiles, d], 2, P),
                                               ALU.mult).then_inc(kbe_done, 1)
                            pool.tensor_tensor(kd[d][:, :, :], kn[:, :, :], bcast(hd[:, EREST, tiles, d], 2, P),
                                               ALU.mult).then_inc(kbe_done, 1)
                        pool.wait_ge(mso_done, n + 1)
                        pool.tensor_tensor(ro[:, :], mso[:, :], m["neghalf"][:, 0:TPG], ALU.pow).then_inc(ro_done, 1)

            @block.tensor
            def _(pe):
                ident = m["ident"][:, :]
                prime(pe, proj_ps, mod_ps, early_ps)
                pe.wait_ge(pads, 1)
                with pe.Fori(0, HA) as h:
                    early = iter(range(GROUPS * EUNITS * KD))

                    def fill(products):
                        for _ in range(products):
                            unit, k = divmod(next(early), KD)
                            i, u = divmod(unit, GROUPS)
                            if k == 0:
                                slot_loads = (ETILES + 1 - i % 2) // 2
                                pe.wait_ge(we_in[i % 2], h * (16 * slot_loads) + (i // 2 + 1) * 16)
                                pe.wait_ge(early_sb, 1 + h * (GROUPS * ETILES) + unit)
                            mm = pe.matmul(ps[:, 2, :], we[i % 2][:, k, :], m["hT"][:, k, u * SEQ:(u + 1) * SEQ],
                                           start=(k == 0), stop=(k == KD - 1))
                            if k == KD - 1:
                                mm.then_inc(early_ps, 1)

                    pe.wait_ge(first["w4_in"], (h + 1) * 64)
                    for u in range(NPROJ):
                        b, g = divmod(u, GROUPS)
                        if u < 2:
                            pe.wait_ge(proj_read, 1 + h * NPROJ)
                            pe.wait_ge(oa_done, 1 + h * GROUPS)
                            pe.wait_ge(uw_sb[1], 1 + h * 2 * GROUPS)
                        else:
                            pe.wait_ge(proj_read, 1 + h * NPROJ + (u - 1))
                        for k in range(KD):
                            mm = pe.matmul(ps[:, u % 2, :], w4[:, b, k, :], m["hT"][:, k, g * SEQ:(g + 1) * SEQ],
                                           start=(k == 0), stop=(k == KD - 1))
                        mm.then_inc(proj_ps, 1)
                    for g in range(GROUPS):
                        n = h * GROUPS + g
                        pe.wait_ge(on_done, 1 + n)
                        for i in range(3):
                            pe.wait_ge(silu_done, h * 6 + (2 * i + g + 1))
                            for t in range(TPG):
                                mm = pe.transpose(ps[:, 3 + i, t * P:(t + 1) * P], conv[:, i, g, t * P:(t + 1) * P], ident)
                            mm.then_inc(tok_ps, 1)
                        pe.wait_ge(gsum_done, 2 * n + 2)
                        pe.wait_ge(proj_read, 1 + h * NPROJ + NPROJ)
                        pe.wait_ge(oa_done, 1 + n)
                        for d in range(2):
                            pe.matmul(ps[:, d, :], m["ones"][:, :], gsum[d][:, :, :], start=True,
                                      stop=True).then_inc(row_ps[d], 1)
                        fill(4)
                        for i, (src, ready) in enumerate(((kn, kn_done), (qn, qn_done))):
                            pe.wait_ge(ready, n + 1)
                            for t in range(TPG):
                                mm = pe.transpose(ps[:, 6 + i, t * P:(t + 1) * P], src[:, t, :], ident)
                            mm.then_inc(chn_ps, 1)
                        fill(4)
                        pe.wait_ge(chn_sb, 2 * n + 2)
                        for i, lhs in enumerate((knT, qnT)):
                            for t in range(TPG):
                                mm = pe.matmul(ps[:, 3 + i, t * P:(t + 1) * P], lhs[:, t, :], knT[:, t, :],
                                               start=True, stop=True)
                        mm.then_inc(gram_ps, 1)
                        fill(1)
                        pe.wait_ge(vb_done, n + 1)
                        for d in range(2):
                            pe.wait_ge(qe_done, 2 * n + d + 1)
                            for t in range(TPG):
                                mm = pe.transpose(ps[:, 5 + d, t * P:(t + 1) * P], qe[d][:, t, :], ident)
                            mm.then_inc(qeT_ps, 1)
                        fill(3)
                        for d in range(2):
                            pe.wait_ge(x_done[d], 2 * n + 2)
                            for t in range(TPG):
                                mm = pe.transpose(ps[:, d, t * P:(t + 1) * P], xb[d][:, t, :], ident)
                            mm.then_inc(xT_ps[d], 1)
                            pe.wait_ge(qeT_sb, 2 * n + 2)
                            for t in range(TPG):
                                mm = pe.transpose(ps[:, 5 + 2 * d, t * P:(t + 1) * P], dec[d][:, t, :], ident)
                            mm.then_inc(xT_ps[d], 1)
                            fill((2, 6)[d])
                        for lv in range(LV):
                            for d in range(2):
                                if lv == 0:
                                    pe.wait_ge(x_done[1 - d], 2 * n + 2)
                                    pe.wait_ge(xT_sb[d], 2 * n + 2)
                                    pe.wait_ge(inv0_done[d], 4 * n + 4)
                                else:
                                    pe.wait_ge(inv_done[d], n * LV + lv)
                                for t in range(TPG):
                                    mm = pe.matmul(ps[:, d, t * P:(t + 1) * P], xbT[d][:, t, :], inv[d][:, 0, t, :],
                                                   start=True, stop=True)
                                mm.then_inc(y_ps[d], 1)
                                if lv > 0:
                                    for t in range(TPG):
                                        mm = pe.transpose(ps[:, 5 + 2 * d, t * P:(t + 1) * P], inv[d][:, 0, t, :], ident)
                                    mm.then_inc(invT_ps[d], 1)
                            fill(FILL[d])
                            for d in range(2):
                                pe.wait_ge(y_sb[d], n * LV + lv + 1)
                                if lv > 0:
                                    pe.wait_ge(invT_sb[d], n * (LV - 1) + lv)
                                for t in range(TPG):
                                    if lv < LV - 1:
                                        mm = pe.matmul(ps[:, 4 + 2 * d, t * P:(t + 1) * P], inv[d][:, 1, t, :], xb[d][:, t, :],
                                                       start=True, stop=True)
                                    else:
                                        mm = pe.matmul(ps[:, 5 + 2 * d, t * P:(t + 1) * P], xb[d][:, t, :], inv[d][:, 1, t, :],
                                                       start=True, stop=True)
                                mm.then_inc(upd_ps[d], 1)
                            fill(FILL[d])
                        for d in range(2):
                            pe.wait_ge(inv_done[d], n * LV + LV)
                            pe.wait_ge(kbe_done, 4 * n + 2 * d + 1)
                            for t in range(TPG):
                                pe.matmul(ps[:, d, t * P:(t + 1) * P], inv[d][:, 1, t, :], vb[d][:, t, :],
                                          start=True, stop=True)
                            for t in range(TPG):
                                mm = pe.matmul(ps[:, 4 + 2 * d, t * P:(t + 1) * P], kbe[d][:, t, :], inv[d][:, 1, t, :],
                                               start=True, stop=True)
                            mm.then_inc(uw_ps[d], 1)
                        fill(5)
                        pe.wait_ge(acc_done, (n + 1) * GROUPS * KD)
                        for v in range(GROUPS):
                            mm = pe.matmul(ps[0:GROUPS, 3, :], pickrow[:, v, :], modacc[:, v, :],
                                           start=(v == 0), stop=(v == GROUPS - 1))
                        mm.then_inc(mod_ps, 1)
                        pe.wait_ge(kbe_done, 4 * n + 4)
                        for i in range(NCHUNK):
                            for d in range(2):
                                t, rows = place(chunks(d)[i])
                                if i == 0:
                                    pe.wait_ge(uw_sb[d], 1 + 2 * n + 2)
                                else:
                                    pe.wait_ge(state_done[d], n * NC1 + i)
                                    pe.matmul(ps[rows, 5 + 2 * d, 0:P], xbT[d][:, t, rows],
                                              state[d][:, i, :], start=True, stop=True).then_inc(ws_ps[d], 1)
                            if i > 0:
                                fill(FILL[d])
                            for d in range(2):
                                t, rows = place(chunks(d)[i])
                                if i > 0:
                                    pe.wait_ge(vnew_done[d], n * NC1 + i)
                                if i < NC1:
                                    pe.matmul(ps[:, 5 + 2 * d, P:2 * P], kd[d][rows, t, :], vnew[d][rows, t, :],
                                              start=True, stop=True).then_inc(kv_ps[d], 1)
                            if i < NC1:
                                fill(FILL[d])
                        pe.wait_ge(mod_done, n + 1)
                        for t in range(TPG):
                            out = ps[:, 3, t * P:(t + 1) * P]
                            pe.matmul(out, qkT[0][:, t, :], vnew[0][:, t, :], start=True, stop=False)
                            terms = [(d, c) for d in range(2) for c in (2 * t, 2 * t + 1) if chunks(d)[0] != c]
                            for d, c in terms:
                                rows = place(c)[1]
                                pe.matmul(ps[rows, 3, t * P:(t + 1) * P], qeT[d][:, t, rows],
                                          state[d][:, chunks(d).index(c), :], start=False, stop=False)
                            mm = pe.matmul(out, qkT[1][:, t, :], vnew[1][:, t, :], start=False, stop=True)
                        mm.then_inc(o_ps, 1)
                        fill(7)
                        pe.wait_ge(on_done, 1 + n + 1)
                        for t in range(TPG):
                            mm = pe.transpose(ps[:, 0, t * P:(t + 1) * P], on[:, t, :], ident)
                        mm.then_inc(oT_ps, 1)
                    assert not list(early)

            @block.scalar
            def _(act):
                act.wait_ge(pads, 1)
                prime(act, proj_read, *uw_sb, sq_done, osq_done, early_sb)
                with act.Fori(0, HA) as h:
                    units = iter(range(GROUPS * EUNITS))

                    def keep_early():
                        unit = next(units)
                        i, u = divmod(unit, GROUPS)
                        act.wait_ge(early_ps, h * (GROUPS * ETILES) + (unit + 2))
                        if i >= 1:
                            act.wait_ge(early_out[u], h * (16 * ETILES) + 16 * i)
                        act.activation(est[u], ps[:, 2, :], ACT.Copy).then_inc(early_sb, 1)
                        act.wait_ge(early_sb, h * (GROUPS * ETILES) + (unit + 2))
                        act.dma_start(early_v[:, bass.ds(h * ETILES + i, 1), u * SEQ:(u + 1) * SEQ],
                                      est[u].unsqueeze(1)).then_inc(early_out[u], 16)

                    def silu(u):
                        b, g = divmod(u, GROUPS)
                        act.wait_ge(conv_done, h * 6 + (u + 1))
                        act.activation(conv[:, b, g, :], conv[:, b, g, :], ACT.Silu).then_inc(silu_done, 1)

                    for u in range(NPROJ):
                        b, g = divmod(u, GROUPS)
                        act.wait_ge(proj_ps, 1 + h * NPROJ + (u + 1))
                        if b < 3:
                            act.activation(pre[:, u % 2, 2:SEQ + 2], ps[:, u % 2, :], ACT.Copy).then_inc(proj_read, 1)
                        else:
                            act.activation(zT[:, g, :], ps[:, u % 2, :], ACT.Silu).then_inc(proj_read, 1)
                        if 1 <= u <= 6:
                            silu(u - 1)
                    for g in range(GROUPS):
                        n = h * GROUPS + g
                        for i in range(2):
                            act.wait_ge(tok_ps, 3 * n + i + 1)
                            for t in range(TPG):
                                c = i * TPG + t
                                act.wait_ge(sq_done, 1 + n * 2 * TPG + c)
                                act.activation(junk[:, :], ps[:, 3 + i, t * P:(t + 1) * P], ACT.Square,
                                               accum_out=ssqk[:, c:c + 1]).then_inc(sq_done, 1)
                        for i, dst in enumerate((knT, qnT)):
                            act.wait_ge(chn_ps, 2 * n + i + 1)
                            act.activation(dst[:, :, :], ps[:, 6 + i, :], ACT.Copy).then_inc(chn_sb, 1)
                        keep_early()
                        for d in range(2):
                            act.wait_ge(diff_done[d], TPG * n + TPG)
                            act.activation(dec[d][:, :, :], dec[d][:, :, :], ACT.Exp, scale=-1.0).then_inc(dec_done[d], 1)
                        for d in range(2):
                            act.wait_ge(qeT_ps, 2 * n + d + 1)
                            act.activation(qeT[d][:, :, :], ps[:, 5 + d, :], ACT.Copy).then_inc(qeT_sb, 1)
                        for d in range(2):
                            act.wait_ge(xT_ps[d], 2 * n + 1)
                            act.activation(xbT[d][:, :, :], ps[:, d, :], ACT.Copy).then_inc(xT_sb[d], 1)
                            act.wait_ge(xT_ps[d], 2 * n + 2)
                            act.activation(qkT[d][:, :, :], ps[:, 5 + 2 * d, :], ACT.Copy).then_inc(xT_sb[d], 1)
                        keep_early()
                        for lv in range(1, LV):
                            for d in range(2):
                                act.wait_ge(invT_ps[d], n * (LV - 1) + lv)
                                act.activation(inv[d][:, 1, :, :], ps[:, 5 + 2 * d, :], ACT.Copy).then_inc(invT_sb[d], 1)
                            if lv == 1:
                                keep_early()
                        for d in range(2):
                            act.wait_ge(uw_ps[d], n + 1)
                            act.activation(vnew[d][:, :, :], ps[:, d, :], ACT.Copy).then_inc(uw_sb[d], 1)
                            act.activation(xbT[d][:, :, :], ps[:, 4 + 2 * d, :], ACT.Copy).then_inc(uw_sb[d], 1)
                        for _ in range(3):
                            keep_early()
                        act.wait_ge(o_ps, n + 1)
                        for t in range(TPG):
                            act.wait_ge(osq_done, 1 + n * TPG + t)
                            act.activation(junk[:, :], ps[:, 3, t * P:(t + 1) * P], ACT.Square,
                                           accum_out=ssqo[:, t:t + 1]).then_inc(osq_done, 1)
                        keep_early()
                    for u in range(GROUPS):
                        act.wait_ge(early_out[u], (h + 1) * (16 * ETILES))

            @block.vector
            def _(dve):
                prime(dve, oa_done, on_done)
                dve.wait_ge(pads, 1)
                with dve.Fori(0, HA) as h:
                    st = Steps(dve, dve_step, before=h * D_STEPS)
                    dve.tensor_copy(hd[:, :, :, :], m["tab"][:, :, :, :].rearrange("p q t (d h) -> p (q t d) h", d=2)
                                    [:, :, bass.ds(h, 1)]).then_inc(hd_ready, 1)
                    st.do(dve.tensor_copy(cw[:, :], m["convT"][:, 0:60].rearrange("p (r h) -> p r h", h=HA)
                                          [:, :, bass.ds(h, 1)]))
                    for u in range(6):
                        b, g = divmod(u, GROUPS)
                        dve.wait_ge(proj_read, 1 + h * NPROJ + (u + 1))
                        acc = conv[:, b, g, :]
                        st.do(dve.tensor_scalar(acc, pre[:, u % 2, 0:SEQ], cw[:, b:b + 1], None, ALU.mult))
                        for tap in range(1, CONV_K):
                            ins = dve.scalar_tensor_tensor(out=acc, in0=pre[:, u % 2, tap:tap + SEQ],
                                                           scalar=cw[:, 3 * tap + b:3 * tap + b + 1], in1=acc,
                                                           op0=ALU.mult, op1=ALU.add)
                            if tap < CONV_K - 1:
                                st.do(ins)
                            else:
                                ins.then_inc(conv_done, 1)
                    for g in range(GROUPS):
                        n = h * GROUPS + g
                        tiles = slice(g * TPG, (g + 1) * TPG)
                        dve.wait_ge(sq_done, 1 + (n + 1) * 2 * TPG)
                        dve.tensor_scalar(msqk[:, 0:TPG], ssqk[:, 0:TPG], EPS, float(DK), ALU.add, ALU.mult)
                        dve.tensor_scalar(msqk[:, TPG:], ssqk[:, TPG:], EPS, None, ALU.add).then_inc(ms_done, 1)
                        dve.wait_ge(tok_ps, 3 * n + 3)
                        for d in range(2):
                            ins = dve.tensor_tensor(vb[d][:, :, :], ps[:, 5, :].rearrange("p (t c) -> p t c", t=TPG),
                                                    bcast(hd[:, BETA, tiles, d], 2, P), ALU.mult)
                        ins.then_inc(vb_done, 1)
                        dve.wait_ge(rqk_done, n + 1)
                        dve.tensor_tensor(kn[:, :, :], ps[:, 4, :].rearrange("p (t c) -> p t c", t=TPG),
                                          bcast(rqk[:, TPG:], 2, P), ALU.mult).then_inc(kn_done, 1)
                        dve.tensor_tensor(qn[:, :, :], ps[:, 3, :].rearrange("p (t c) -> p t c", t=TPG),
                                          bcast(rqk[:, 0:TPG], 2, P), ALU.mult).then_inc(qn_done, 1)
                        for d in range(2):
                            dve.wait_ge(row_ps[d], n + 1)
                            for t in range(TPG):
                                dve.scalar_tensor_tensor(out=dec[d][:, t, :], in0=ps[:, d, t * P:(t + 1) * P],
                                                         scalar=hd[:, CUM, g * TPG + t, d:d + 1], in1=posmask[:, d, :],
                                                         op0=ALU.subtract, op1=ALU.add).then_inc(diff_done[d], 1)
                        dve.wait_ge(gram_ps, n + 1)
                        for d in range(2):
                            dve.wait_ge(dec_done[d], n + 1)
                            for t in range(TPG):
                                ins = dve.scalar_tensor_tensor(out=xb[d][:, t, :], in0=ps[:, 3, t * P:(t + 1) * P],
                                                               scalar=hd[:, BETA, g * TPG + t, d:d + 1],
                                                               in1=dec[d][:, t, :], op0=ALU.mult, op1=ALU.mult)
                            ins.then_inc(x_done[d], 1)
                            dve.wait_ge(x_done[d], 2 * n + 1)
                            dve.tensor_tensor(dec[d][:, :, :], ps[:, 4, :], dec[d][:, :, :].rearrange("p t c -> p (t c)"),
                                              ALU.mult).then_inc(x_done[d], 1)
                        products = iter([(v, k) for k in range(KD) for v in range(GROUPS)])

                        def accumulate(count):
                            for _ in range(count):
                                v, k = next(products)
                                if v == 0 and k == 0:
                                    dve.wait_ge(ada_in, (n + 1) * 16)
                                    dve.wait_ge(mod_ps, 1 + n)
                                done = n * (GROUPS * KD) + k * GROUPS + v
                                if k == 0:
                                    dve.tensor_scalar(modacc[:, v, :], ada[:, k, :], m["sc"][:, k, v:v + 1], None,
                                                      ALU.mult).then_inc(acc_done, 1)
                                else:
                                    dve.wait_ge(acc_done, done - 1)
                                    dve.scalar_tensor_tensor(out=modacc[:, v, :], in0=ada[:, k, :], scalar=m["sc"][:, k, v:v + 1],
                                                             in1=modacc[:, v, :], op0=ALU.mult, op1=ALU.add).then_inc(acc_done, 1)

                        for lv in range(LV):
                            for d in range(2):
                                dve.wait_ge(y_ps[d], n * LV + lv + 1)
                                if lv == 0:
                                    dve.wait_ge(inv0_done[d], 4 * n + 4)
                                dve.tensor_tensor(xb[d][:, :, :], ps[:, d, :].rearrange("p (t c) -> p t c", t=TPG),
                                                  bcast(levelmask[:, d, lv + 1, :], 1, TPG), ALU.mult).then_inc(y_sb[d], 1)
                            for d in range(2):
                                dve.wait_ge(upd_ps[d], n * LV + lv + 1)
                                side = 0 if lv < LV - 1 else 1
                                part = inv[d][:, side, :, :].rearrange("p t c -> p (t c)")
                                dve.tensor_tensor(part, part, ps[:, 4 + 2 * d + side, :], ALU.subtract).then_inc(inv_done[d], 1)
                            accumulate(4 if lv < LV - 1 else 0)
                        dve.wait_ge(mod_ps, 1 + n + 1)
                        dve.wait_ge(brow_in, (n + 1) * 16)
                        dve.wait_ge(row_free, 1 + n)
                        dve.tensor_tensor(modrow[:, :], ps[0:GROUPS, 3, :], brow[:, :], ALU.add).then_inc(mod_done, 1)
                        for i in range(NCHUNK):
                            for d in range(2):
                                t, rows = place(chunks(d)[i])
                                if i > 0:
                                    dve.wait_ge(ws_ps[d], n * NC1 + i)
                                    dve.tensor_tensor(vnew[d][rows, t, :], vnew[d][rows, t, :], ps[rows, 5 + 2 * d, 0:P],
                                                      ALU.subtract).then_inc(vnew_done[d], 1)
                            for d in range(2):
                                c = chunks(d)[i]
                                if i < NC1:
                                    dve.wait_ge(kv_ps[d], n * NC1 + i + 1)
                                    kv = ps[:, 5 + 2 * d, P:2 * P]
                                    if i == 0:
                                        dve.tensor_copy(state[d][:, 1, :], kv).then_inc(state_done[d], 1)
                                    else:
                                        dve.scalar_tensor_tensor(out=state[d][:, i + 1, :], in0=state[d][:, i, :],
                                                                 scalar=hd[:, ETOT + c % 2, g * TPG + c // 2, d:d + 1], in1=kv,
                                                                 op0=ALU.mult, op1=ALU.add).then_inc(state_done[d], 1)
                        dve.wait_ge(osq_done, 1 + (n + 1) * TPG)
                        dve.tensor_scalar(mso[:, :], ssqo[:, :], 1.0 / DK, EPS, ALU.mult, ALU.add).then_inc(mso_done, 1)
                        dve.wait_ge(ro_done, n + 1)
                        dve.tensor_tensor(on[:, :, :], ps[:, 3, :].rearrange("p (t c) -> p t c", t=TPG),
                                          bcast(ro[:, :], 2, P), ALU.mult).then_inc(on_done, 1)
                        dve.wait_ge(oT_ps, n + 1)
                        dve.scalar_tensor_tensor(out=m["oaT"][:, :, :].rearrange("p h t -> p (h t)")
                                                 [:, bass.ds(h * TOK + g * SEQ, SEQ)],
                                                 in0=ps[:, 0, :], scalar=m["convT"][:, 60:61], in1=zT[:, g, :],
                                                 op0=ALU.mult, op1=ALU.mult).then_inc(oa_done, 1)
                    assert st.n == D_STEPS
        nc.clear_and_free_semaphores(sems)
        nc.all_engine_barrier()


def phase_attention(nc, a, m, ps, early_dram, x_in):
    NPROJ = 3 * GROUPS
    NU = GROUPS * 2 * TPG
    KINDS = [(16, 48), (0, 48), (0, 32)]
    KIND_OF = [0, 1, 1, 2]
    KIND_AT = [0, 256, 640]
    BIAS_W = 896
    with ExitStack() as ctx:
        def sb(name, shape, dt=F32):
            return ctx.enter_context(nc.sbuf_tensor(name, shape, dt))

        def sem(name):
            return ctx.enter_context(nc.semaphore(name))

        raw = sb("raw", [P, 3, TOK])
        rel = sb("rel", [P, HB, RPB_RUN])
        outside = sb("outside", [P, BIAS_W])
        bias = sb("bias", [P, 2, BIAS_W])
        qT = sb("qT", [P, GROUPS, SEQ])
        kT = sb("kT", [P, GROUPS, SEQ])
        vT = sb("vT", [P, GROUPS, SEQ])
        vtok = sb("vtok", [P, GROUPS, TPG, P])
        sc = sb("scores", [P, 2, 3 * P])
        low = sb("low", [P, 2])
        pr = sb("pr", [P, 2, 3 * P])
        den = sb("den", [P, 2])
        rden = sb("rden", [P, 2])
        pT = sb("pT", [P, 2, 3 * P])
        otok = sb("otok", [P, GROUPS, TPG, P])

        raw_in = sem("raw_in")
        rel_first = sem("rel_first")
        rel_in = sem("rel_in")
        outside_done = sem("outside_done")
        bias_done = sem("bias_done")
        take_done = sem("take_done")
        vt_ps = sem("vt_ps")
        vtok_sb = sem("vtok_sb")
        s_ps = sem("s_ps")
        sc_done = sem("sc_done")
        low_done = sem("low_done")
        exp_done = sem("exp_done")
        pT_ps = sem("pT_ps")
        pT_sb = sem("pT_sb")
        pv_ps = sem("pv_ps")
        rden_done = sem("rden_done")
        otok_done = sem("otok_done")
        obT_ps = sem("obT_ps")
        ob_done = sem("ob_done")

        def unit(w):
            g, r = divmod(w, 2 * TPG)
            hp, t = divmod(r, TPG)
            return g, hp, t

        def width(t):
            return (KEY_TILES[t][1] - KEY_TILES[t][0]) * P

        def before(w, lag):
            return max(w - lag + 1, 0)

        with nc.Block() as block:

            @block.sync
            def _(sp):
                rpb = a["rpb"]

                def load_rel(h0, h1, sem):
                    for c in range(16):
                        src = bass.AP(rpb.tensor, h0 * RPB_LEN + RPB_FRONT - 15 * c - 8,
                                      [[HB * RPB_LEN, ROWS], [RPB_LEN, h1 - h0], [1, RPB_RUN]])
                        sp.dma_start(rel[8 * c:8 * c + 8, h0:h1, :], src).then_inc(sem, 16)

                load_rel(0, 2, rel_first)
                early_v = early_dram[0:GATE_TILE * P, :].rearrange("(b h p) t -> p b h t", p=P, b=3)
                sp.dma_start(raw[:, :, :].unsqueeze(2), early_v[:, :, 0:1, :]).then_inc(raw_in, 16)
                load_rel(2, HB, rel_in)
                sp.dma_start(m["hT"][:, :, :], a["x"].rearrange("(t p) c -> p t c", p=P)).then_inc(x_in, 16)
                with sp.Fori(0, PAIRS - 1) as h:
                    sp.wait_ge(take_done, h * NPROJ + NPROJ)
                    sp.dma_start(raw[:, :, :].unsqueeze(2), early_v[:, :, 1:, :][:, :, bass.ds(h, 1), :]).then_inc(raw_in, 16)

            @block.gpsimd
            def _(pool):
                pool.memset(outside[:, :], 0.0).then_inc(outside_done, 1)
                n = 1

                def keep(kind, x0, x1, base, step, cm):
                    nonlocal n
                    pool.wait_ge(outside_done, n)
                    lo = KINDS[kind][0]
                    part = outside[:, KIND_AT[kind] + (x0 - lo) * 8:KIND_AT[kind] + (x1 - lo) * 8]
                    pool.affine_select(out=part, in_=part, compare_op=ALU.is_ge, fill=BIG, base=base + step * x0,
                                       pattern=[[step, x1 - x0], [0, 8]], channel_multiplier=cm).then_inc(outside_done, 1)
                    n += 1

                keep(0, 16, 48, 7 - 64, 8, -1)
                keep(0, 32, 48, 184, -8, 1)
                keep(1, 0, 48, 7 - 64, 8, -1)
                keep(1, 0, 48, 184, -8, 1)
                keep(2, 0, 16, 7 - 64, 8, -1)
                keep(2, 0, 32, 184, -8, 1)
                pool.wait_ge(outside_done, n)
                pool.wait_ge(rel_first, 16 * 16)
                rel_flat = rel[:, :, :].rearrange("p h x -> p (h x)")
                with pool.Fori(0, PAIRS) as h:
                    for hp in range(2):
                        pool.wait_ge(sc_done, h * NU + (NU - (1 - hp) * TPG))
                        for kind, (x0, x1) in enumerate(KINDS):
                            nx = x1 - x0
                            src = rel_flat[:, bass.ds(h * (2 * RPB_RUN) + (hp * RPB_RUN + x0 * RPB_R), nx * RPB_R)]
                            at = slice(KIND_AT[kind], KIND_AT[kind] + nx * 8)
                            pool.tensor_tensor(bias[:, hp, at].rearrange("p (x r) -> p x r", r=8),
                                               src.rearrange("p (x r) -> p x r", r=RPB_R)[:, :, 0:8],
                                               outside[:, at].rearrange("p (x r) -> p x r", r=8),
                                               ALU.subtract).then_inc(bias_done, 1)
                    pool.wait_ge(rel_in, 16 * 16)

            @block.tensor
            def _(pe):
                ident = m["ident"][:, :]
                prime(pe, pT_ps, pv_ps)
                with pe.Fori(0, PAIRS) as h:
                    def turn_v():
                        pe.wait_ge(ob_done, 1 + h * GROUPS)
                        for g in range(GROUPS):
                            pe.wait_ge(take_done, h * NPROJ + (5 + g))
                            for t in range(TPG):
                                mm = pe.transpose(ps[:, g, t * P:(t + 1) * P], vT[:, g, t * P:(t + 1) * P], ident)
                            mm.then_inc(vt_ps, 1)

                    def scores(w):
                        g, hp, t = unit(w)
                        k0, k1 = KEY_TILES[t]
                        if w == 0:
                            pe.wait_ge(take_done, h * NPROJ + 3)
                        pe.wait_ge(sc_done, NU + h * NU + before(w, 2))
                        rows = slice(hp * DH, (hp + 1) * DH)
                        pe.matmul(ps[:, 2 + w % 2, 0:width(t)], qT[rows, g, t * P:(t + 1) * P],
                                  kT[rows, g, k0 * P:k1 * P], start=True, stop=True).then_inc(s_ps, 1)

                    def turn(w):
                        g, hp, t = unit(w)
                        pe.wait_ge(exp_done, 1 + h * NU + (w + 1))
                        pe.wait_ge(pT_sb, 1 + h * NU + before(w, 2))
                        for i in range(width(t) // P):
                            mm = pe.transpose(ps[:, 4 + w % 2, i * P:(i + 1) * P], pr[:, w % 2, i * P:(i + 1) * P], ident)
                        mm.then_inc(pT_ps, 1)

                    def values(w):
                        g, hp, t = unit(w)
                        k0, k1 = KEY_TILES[t]
                        pe.wait_ge(vtok_sb, h * GROUPS + GROUPS)
                        pe.wait_ge(pT_sb, 1 + h * NU + (w + 1))
                        pe.wait_ge(otok_done, 1 + h * NU + before(w, 2))
                        for i in range(k1 - k0):
                            mm = pe.matmul(ps[:, 6 + w % 2, 0:DH], pT[:, w % 2, i * P:(i + 1) * P],
                                           vtok[:, g, k0 + i, hp * DH:(hp + 1) * DH], start=(i == 0), stop=(i == k1 - k0 - 1))
                        mm.then_inc(pv_ps, 1)

                    for w in range(NU + 3):
                        if w < NU:
                            scores(w)
                        if w == 1:
                            turn_v()
                        if 2 <= w < NU + 2:
                            turn(w - 2)
                        if w >= 3:
                            values(w - 3)
                    for g in range(GROUPS):
                        pe.wait_ge(otok_done, 1 + h * NU + (g + 1) * 2 * TPG)
                        pe.wait_ge(ob_done, 1 + h * GROUPS)
                        for t in range(TPG):
                            mm = pe.transpose(ps[:, g, t * P:(t + 1) * P], otok[:, g, t, :], ident)
                        mm.then_inc(obT_ps, 1)

            @block.scalar
            def _(act):
                prime(act, exp_done, pT_sb)
                with act.Fori(0, PAIRS) as h:
                    act.wait_ge(raw_in, (h + 1) * 16)
                    for u in range(NPROJ):
                        b, g = divmod(u, GROUPS)
                        dst = (qT, kT, vT)[b][:, g, :].rearrange("p (c r) -> p r c", r=ROWS)
                        act.activation(dst, raw[:, b, g * SEQ:(g + 1) * SEQ].rearrange("p (r c) -> p r c", r=ROWS), ACT.Copy,
                                       scale=(-DH ** -0.5 if b == 0 else 1.0)).then_inc(take_done, 1)
                    for g in range(GROUPS):
                        act.wait_ge(vt_ps, h * GROUPS + (g + 1))
                        act.activation(vtok[:, g, :, :], ps[:, g, :], ACT.Copy).then_inc(vtok_sb, 1)
                    for w in range(NU + 1):
                        if w < NU:
                            g, hp, t = unit(w)
                            act.wait_ge(low_done, h * NU + (w + 1))
                            act.wait_ge(pT_ps, 1 + h * NU + before(w, 2))
                            act.wait_ge(rden_done, 1 + h * NU + before(w, 2))
                            act.activation(pr[:, w % 2, 0:width(t)], sc[:, w % 2, 0:width(t)], ACT.Exp, scale=-1.0,
                                           bias=low[:, w % 2:w % 2 + 1],
                                           accum_out=den[:, w % 2:w % 2 + 1]).then_inc(exp_done, 1)
                        if w >= 1:
                            v = w - 1
                            g, hp, t = unit(v)
                            act.wait_ge(pT_ps, 1 + h * NU + (v + 1))
                            act.wait_ge(pv_ps, 1 + h * NU + before(v, 2))
                            act.activation(pT[:, v % 2, 0:width(t)], ps[:, 4 + v % 2, 0:width(t)], ACT.Copy).then_inc(pT_sb, 1)

            @block.vector
            def _(dve):
                dve.sem_inc(sc_done, NU)
                prime(dve, rden_done, otok_done, ob_done)
                with dve.Fori(0, PAIRS) as h:
                    for w in range(NU + 3):
                        if w < NU:
                            g, hp, t = unit(w)
                            n = width(t)
                            if g == 0 and t == 0:
                                dve.wait_ge(bias_done, h * 6 + 3 * (hp + 1))
                            dve.wait_ge(s_ps, h * NU + (w + 1))
                            dve.wait_ge(exp_done, 1 + h * NU + before(w, 2))
                            at = KIND_AT[KIND_OF[t]]
                            dve.tensor_tensor(sc[:, w % 2, 0:n], ps[:, 2 + w % 2, 0:n], bias[:, hp, at:at + n],
                                              ALU.subtract).then_inc(sc_done, 1)
                            dve.wait_ge(sc_done, NU + h * NU + (w + 1))
                            dve.tensor_reduce(low[:, w % 2:w % 2 + 1], sc[:, w % 2, 0:n], AX_X, ALU.min).then_inc(low_done, 1)
                        if w >= 3:
                            v = w - 3
                            g, hp, t = unit(v)
                            dve.wait_ge(pv_ps, 1 + h * NU + (v + 1))
                            dve.wait_ge(rden_done, 1 + h * NU + (v + 1))
                            dve.tensor_scalar(otok[:, g, t, hp * DH:(hp + 1) * DH], ps[:, 6 + v % 2, 0:DH],
                                              rden[:, v % 2:v % 2 + 1], None, ALU.mult).then_inc(otok_done, 1)
                        if 2 <= w < NU + 2:
                            v = w - 2
                            dve.wait_ge(exp_done, 1 + h * NU + (v + 1))
                            dve.wait_ge(otok_done, 1 + h * NU + before(v, 2))
                            dve.reciprocal(rden[:, v % 2:v % 2 + 1], den[:, v % 2:v % 2 + 1]).then_inc(rden_done, 1)
                    for g in range(GROUPS):
                        dve.wait_ge(obT_ps, h * GROUPS + (g + 1))
                        dst = m["obT"][:, :, :].rearrange("p h t -> p (h t)")[:, bass.ds(h * TOK + g * SEQ, SEQ)]
                        dve.tensor_copy(dst.rearrange("p (r c) -> p r c", r=ROWS),
                                        ps[:, g, :].rearrange("p (c r) -> p r c", r=ROWS)).then_inc(ob_done, 1)


QUARTERS = 4
FW = D_EXPERT // QUARTERS
FT = FW // P
ORDER = [("g", 0), ("u", 0), ("g", 1), ("u", 1), ("d", 0), ("g", 2), ("u", 2), ("d", 1), ("g", 3), ("u", 3),
         ("d", 2), ("d", 3)]
RAW_SLOTS = 4


def load_piece(eng, a, raw, raw_in, e, p, ahead=0):
    kind, n = ORDER[p]
    w = a[{"g": "w_gate", "u": "w_up", "d": "w_down"}[kind]].rearrange("a e (k p) n -> p (a e) k n", p=P)[:, ahead:]
    if kind == "d":
        src, k = w[:, bass.ds(e, 1), n * FT:(n + 1) * FT, :], FT
    else:
        src, k = w[:, bass.ds(e, 1), :, n * FW:(n + 1) * FW], KD
    slot = p % RAW_SLOTS
    eng.dma_start(raw[slot].rearrange("p (k n) -> p k n", k=k), src.rearrange("p e k n -> p (e k) n")).then_inc(raw_in[slot], 16)


def late_buffers(nc, ctx):
    def sb(name, shape, dt=F32):
        return ctx.enter_context(nc.sbuf_tensor(name, shape, dt))

    late = {}
    late["mergedT"] = sb("mergedT", [P, KD, TOK])
    late["gate1"] = sb("gate1", [P, GROUPS, D_MODEL])
    late["mul2row"] = sb("mul2row", [P, GROUPS, D_MODEL])
    late["shift2"] = sb("shift2", [P, GROUPS, D_MODEL])
    late["wout"] = sb("wout", [P, KD, D_MODEL])
    late["wr"] = sb("wr", [P, KD, NE])
    late["route_in"] = ctx.enter_context(nc.semaphore("route_in"))
    return late


def phase_merge(nc, a, m, ps, late, early_dram, mod_dram):
    JOBS = 2 * GROUPS
    with ExitStack() as ctx:
        def sb(name, shape, dt=F32):
            return ctx.enter_context(nc.sbuf_tensor(name, shape, dt))

        def sem(name):
            return ctx.enter_context(nc.semaphore(name))

        wj = [sb(f"wj{i}", [P, KD, P]) for i in range(2)]
        graw = [sb(f"graw{i}", [P, 2, TOK]) for i in range(2)]
        sig = sb("sig", [P, GROUPS, 2, SEQ])
        wide = sb("wide", [P, GROUPS, 2, SEQ])
        norm2 = sb("norm2", [P, D_MODEL])

        rows_in = sem("rows_in")
        mul2_done = sem("mul2_done")
        wj_in = [sem(f"wj_in{i}") for i in range(2)]
        graw_in = [sem(f"graw_in{i}") for i in range(2)]
        wide_ps = sem("wide_ps")
        sig_done = sem("sig_done")
        wide_done = sem("wide_done")
        merged_done = sem("merged_done")

        with nc.Block() as block:

            @block.sync
            def _(sp):
                gates_v = early_dram[GATE_TILE * P:, :].rearrange("(b j p) t -> p b j t", p=P, b=2)
                w_oa = a["w_oa"].rearrange("a (k p) n -> p (a k) n", p=P)
                w_ob = a["w_ob"].rearrange("a (k p) n -> p (a k) n", p=P)
                with sp.Fori(0, KD // 2) as jj:
                    for i in range(2):
                        sp.wait_ge(wide_done, jj * (2 * JOBS) + 4 * (i + 1))
                        col = jj * (2 * P) + i * P
                        sp.dma_start(graw[i][:, :, :].unsqueeze(2), gates_v[:, :, bass.ds(jj * 2 + i, 1), :]).then_inc(graw_in[i], 16)
                        sp.dma_start(wj[i][:, 0:HA, :], w_oa[:, :, bass.ds(col, P)]).then_inc(wj_in[i], 16)
                        sp.dma_start(wj[i][:, HA:KD, :], w_ob[:, :, bass.ds(col, P)]).then_inc(wj_in[i], 16)

            @block.gpsimd
            def _(pool):
                prime(pool, merged_done)
                with pool.Fori(0, KD // 2) as jj:
                    for r in range(JOBS):
                        i, g = divmod(r, GROUPS)
                        pool.wait_ge(wide_done, 2 * JOBS + jj * 2 * JOBS + (2 * r + 2))
                        dst = late["mergedT"][:, :, :].rearrange("p k t -> p (k t)")[:, bass.ds(
                            jj * (2 * TOK) + (i * TOK + g * SEQ), SEQ)]
                        pool.tensor_tensor(dst, wide[:, g, 0, :], wide[:, g, 1, :], ALU.add).then_inc(merged_done, 1)

            @block.tensor
            def _(pe):
                with pe.Fori(0, KD // 2) as jj:
                    for r in range(JOBS):
                        i, g = divmod(r, GROUPS)
                        if g == 0:
                            pe.wait_ge(wj_in[i], (jj + 1) * 32)
                        pe.wait_ge(wide_done, 2 * JOBS + jj * 2 * JOBS + 2 * max(r - 1, 0))
                        cols = slice(g * SEQ, (g + 1) * SEQ)
                        for b, src in enumerate((m["oaT"], m["obT"])):
                            for k in range(HA):
                                mm = pe.matmul(ps[:, 4 * g + 2 + b, :], wj[i][:, b * HA + k, :], src[:, k, cols],
                                               start=(k == 0), stop=(k == HA - 1))
                        mm.then_inc(wide_ps, 1)

            @block.scalar
            def _(act):
                act.wait_ge(graw_in[0], 16)
                for dst, src in ((late["wout"][:, :, :], a["w_out"].rearrange("a (k p) n -> p (a k) n", p=P)),
                                 (late["wr"][:, :, :], a["w_router"].rearrange("a (k p) n -> p (a k) n", p=P))):
                    act.dma_start(dst, src).then_inc(late["route_in"], 16)

                def vector(i, count, g=0, groups=1):
                    return bass.AP(mod_dram.tensor, (g * 6 + i) * D_MODEL, [[0, count], [6 * D_MODEL, groups], [1, D_MODEL]])

                act.dma_start(late["mul2row"][:, :, :], vector(4, P, groups=GROUPS)).then_inc(rows_in, 16)
                act.dma_start(norm2[:, :], bass.AP(a["norm2_g"].tensor, 0, [[0, P], [1, D_MODEL]])).then_inc(rows_in, 16)
                act.dma_start(late["gate1"][:, :, :], vector(2, P, groups=GROUPS)).then_inc(late["route_in"], 16)
                act.dma_start(late["shift2"][:, :, :], vector(3, P, groups=GROUPS)).then_inc(late["route_in"], 16)
                for g in range(GROUPS):
                    act.dma_start(m["gate2"][g * CAP:(g + 1) * CAP, :].unsqueeze(1), vector(5, CAP, g)).then_inc(late["route_in"], 16)
                with act.Fori(0, KD // 2) as jj:
                    for r in range(JOBS):
                        i, g = divmod(r, GROUPS)
                        if g == 0:
                            act.wait_ge(graw_in[i], (jj + 1) * 16)
                        act.wait_ge(wide_done, 2 * JOBS + jj * 2 * JOBS + 2 * max(r - 1, 0))
                        for b in range(2):
                            act.activation(sig[:, g, b, :], graw[i][:, b, g * SEQ:(g + 1) * SEQ], ACT.Sigmoid).then_inc(sig_done, 1)

            @block.vector
            def _(dve):
                dve.sem_inc(wide_done, 2 * JOBS)
                with dve.Fori(0, KD // 2) as jj:
                    for r in range(JOBS):
                        g = r % GROUPS
                        dve.wait_ge(wide_ps, jj * JOBS + (r + 1))
                        dve.wait_ge(merged_done, 1 + jj * JOBS + max(r - 1, 0))
                        for b in range(2):
                            dve.wait_ge(sig_done, jj * 2 * JOBS + (2 * r + b + 1))
                            dve.tensor_tensor(wide[:, g, b, :], sig[:, g, b, :], ps[:, 4 * g + 2 + b, :],
                                              ALU.mult).then_inc(wide_done, 1)
                dve.wait_ge(rows_in, 32)
                for g in range(GROUPS):
                    dve.scalar_tensor_tensor(out=late["mul2row"][:, g, :], in0=late["mul2row"][:, g, :], scalar=1.0,
                                             in1=norm2[:, :], op0=ALU.add, op1=ALU.mult).then_inc(mul2_done, 1)


def phase_route(nc, a, m, ps, late, x2_dram, h2_dram, raw, raw_in, x_in):
    NR = GROUPS * NE
    xt = m["hT"]
    with ExitStack() as ctx:
        def sb(name, shape, dt=F32):
            return ctx.enter_context(nc.sbuf_tensor(name, shape, dt))

        def sem(name):
            return ctx.enter_context(nc.semaphore(name))

        xm = sb("xm", [P, 2, D_MODEL])
        h2 = sb("h2", [P, 2, D_MODEL])
        junk = sb("junk_r", [P, D_MODEL])
        h2T = sb("h2T", [P, 2, KD, P])
        ssq = sb("ssq_r", [P, NT])
        ms = sb("ms_r", [P, NT])
        rinv = sb("rinv_r", [P, NT])
        negmax = sb("negmax", [P, NT])
        ex = sb("ex", [P, NT, NE])
        den = sb("den_r", [P, NT])
        rden = sb("rden_r", [P, NT])
        probs = sb("probs", [P, TPG, GROUPS, NE])
        work = sb("work", [NR, 2, SEQ])
        vals = sb("vals", [NR, CAP])
        idx = sb("idx", [NR, CAP], U32)
        idxf = sb("idxf", [NR, CAP])
        first = sb("first_token", [NR, 1])
        own = sb("own_half", [NR, GROUPS, CAP])
        pick = sb("pick", [NR, NE])
        spread = sb("spread", [NR, 2, GROUPS, CAP])

        ROUTE_LOADS = 6 * 16
        sel_const = sem("sel_const")
        out_ps = sem("out_ps")
        xm_done = sem("xm_done")
        x2_done = sem("x2_done")
        ssq_done = sem("ssq_done_r")
        ms_done = sem("ms_done_r")
        rinv_done = sem("rinv_done_r")
        hm_done = sem("hm_done")
        h2_done = sem("h2_done")
        x2_out = sem("x2_out")
        h2_out = [sem(f"h2_out{i}") for i in range(2)]
        h2T_ps = sem("h2T_ps")
        h2T_sb = sem("h2T_sb")
        logit_ps = sem("logit_ps")
        negmax_done = sem("negmax_done")
        ex_done = sem("ex_done")
        rden_done = sem("rden_done_r")
        probs_done = sem("probs_done")
        probsT_ps = sem("probsT_ps")
        top_step = sem("top_step")
        pick_ps = sem("pick_ps")

        with nc.Block() as block:

            @block.sync
            def _(sp):
                load_piece(sp, a, raw, raw_in, 0, 0)
                load_piece(sp, a, raw, raw_in, 0, 1)
                x2_v = x2_dram.rearrange("(t p) c -> t p c", p=P)
                h2_v = h2_dram.rearrange("(t p) c -> t p c", p=P)
                for t in range(NT):
                    sp.wait_ge(x2_done, t + 1)
                    sp.dma_start(x2_v[t], xt[:, t, :]).then_inc(x2_out, 16)
                    sp.wait_ge(h2_done, t + 1)
                    sp.dma_start(h2_v[t], h2[:, t % 2, :]).then_inc(h2_out[t % 2], 16)
                sp.wait_ge(x2_out, 16 * NT)
                sp.wait_ge(hm_done, NT)
                sp.wait_ge(ssq_done, NT)
                load_piece(sp, a, raw, raw_in, 0, 2)
                load_piece(sp, a, raw, raw_in, 0, 3)
                for i in range(2):
                    sp.wait_ge(h2_out[i], 16 * NT // 2)

            @block.gpsimd
            def _(pool):
                st = Steps(pool, sel_const)
                st.did(pool.memset(first[:, :], float(SEQ)))
                st.did(pool.memset(own[:, :, :], 1.0))
                st.did(pool.memset(pick[:, :], 0.0))
                st.settle()
                st.did(pool.affine_select(out=first[:, :], in_=first[:, :], compare_op=ALU.is_ge, fill=0.0, base=-NE,
                                          pattern=[[1, 1]], channel_multiplier=1))
                st.did(pool.affine_select(out=own[:, 0, :], in_=own[:, 0, :], compare_op=ALU.is_ge, fill=0.0, base=NE - 1,
                                          pattern=[[0, CAP]], channel_multiplier=-1))
                st.did(pool.affine_select(out=own[:, 1, :], in_=own[:, 1, :], compare_op=ALU.is_ge, fill=0.0, base=-NE,
                                          pattern=[[0, CAP]], channel_multiplier=1))
                for g in range(GROUPS):
                    st.do(pool.affine_select(out=pick[:, :], in_=pick[:, :], compare_op=ALU.not_equal, fill=1.0,
                                             base=-g * NE, pattern=[[-1, NE]], channel_multiplier=1))
                pool.wait_ge(late["route_in"], ROUTE_LOADS)
                pool.wait_ge(x_in, 16)
                for t in range(NT):
                    g = t // TPG
                    pool.wait_ge(xm_done, t + 1)
                    pool.tensor_tensor(xt[:, t, :], xt[:, t, :], xm[:, t % 2, :], ALU.add).then_inc(x2_done, 1)
                    pool.wait_ge(ms_done, t + 1)
                    pool.tensor_tensor(rinv[:, t:t + 1], ms[:, t:t + 1], m["neghalf"][:, 0:1], ALU.pow).then_inc(rinv_done, 1)
                    pool.wait_ge(hm_done, t + 1)
                    pool.tensor_tensor(h2[:, t % 2, :], h2[:, t % 2, :], late["shift2"][:, g, :], ALU.add).then_inc(h2_done, 1)

            @block.tensor
            def _(pe):
                ident = m["ident"][:, :]
                pe.wait_ge(late["route_in"], ROUTE_LOADS)

                def project(t):
                    if t >= 2:
                        pe.wait_ge(xm_done, t - 1)
                    for c in range(2):
                        for k in range(KD):
                            mm = pe.matmul(ps[:, 2 * (t % 2) + c, :], late["mergedT"][:, k, t * P:(t + 1) * P],
                                           late["wout"][:, k, c * 512:(c + 1) * 512], start=(k == 0), stop=(k == KD - 1))
                    mm.then_inc(out_ps, 1)

                def route(t):
                    pe.wait_ge(h2_done, t + 1)
                    if t >= 1:
                        pe.wait_ge(h2T_sb, t)
                    for k in range(KD):
                        mm = pe.transpose(ps[:, 4 + k // 4, (k % 4) * P:(k % 4 + 1) * P],
                                          h2[:, t % 2, k * P:(k + 1) * P], ident)
                    mm.then_inc(h2T_ps, 1)

                def logits(t):
                    pe.wait_ge(h2T_sb, t + 1)
                    if t >= 2:
                        pe.wait_ge(ex_done, t - 1)
                    for k in range(KD):
                        mm = pe.matmul(ps[:, 6 + t % 2, 0:NE], h2T[:, t % 2, k, :], late["wr"][:, k, :],
                                       start=(k == 0), stop=(k == KD - 1))
                    mm.then_inc(logit_ps, 1)

                for t in range(NT + 2):
                    if t < NT:
                        project(t)
                    if 1 <= t <= NT:
                        route(t - 1)
                    if t >= 2:
                        logits(t - 2)
                for t in range(TPG):
                    pe.wait_ge(probs_done, TPG + t + 1)
                    mm = pe.transpose(ps[0:NR, 0, t * P:(t + 1) * P], probs[:, t, :, :].rearrange("p g e -> p (g e)"), ident)
                mm.then_inc(probsT_ps, 1)
                pe.wait_ge(top_step, 3 + 3 * (CAP // 8) + 1)
                for i in range(2):
                    mm = pe.matmul(ps[:, 1, i * NE:(i + 1) * NE], spread[:, i, :, :].rearrange("p g c -> p (g c)"), pick[:, :],
                                   start=True, stop=True)
                mm.then_inc(pick_ps, 1)

            @block.scalar
            def _(act):
                for t in range(NT + 1):
                    if t < NT:
                        act.wait_ge(x2_done, t + 1)
                        if t:
                            act.wait_ge(ssq_done, t)
                        act.activation(junk[:, :], xt[:, t, :], ACT.Square, accum_out=ssq[:, t:t + 1]).then_inc(ssq_done, 1)
                        act.wait_ge(h2T_ps, t + 1)
                        if t >= 2:
                            act.wait_ge(logit_ps, t - 1)
                        act.activation(h2T[:, t % 2, :, :], ps[:, 4:6, :].rearrange("p b (k c) -> p (b k) c", c=P),
                                       ACT.Copy).then_inc(h2T_sb, 1)
                    if t >= 1:
                        v = t - 1
                        act.wait_ge(negmax_done, v + 1)
                        act.activation(ex[:, v, :], ps[:, 6 + v % 2, 0:NE], ACT.Exp, bias=negmax[:, v:v + 1],
                                       accum_out=den[:, v:v + 1]).then_inc(ex_done, 1)

            @block.vector
            def _(dve):
                def softmax_tail(v):
                    dve.wait_ge(logit_ps, v + 1)
                    dve.tensor_reduce(negmax[:, v:v + 1], ps[:, 6 + v % 2, 0:NE], AX_X, ALU.max, negate=True).then_inc(negmax_done, 1)
                    dve.wait_ge(ex_done, v + 1)
                    dve.reciprocal(rden[:, v:v + 1], den[:, v:v + 1]).then_inc(rden_done, 1)
                    dve.wait_ge(rden_done, v + 1)
                    dve.tensor_scalar(probs[:, v % TPG, v // TPG, :], ex[:, v, :], rden[:, v:v + 1], None,
                                      ALU.mult).then_inc(probs_done, 1)

                dve.wait_ge(late["route_in"], ROUTE_LOADS)
                for t in range(NT + 1):
                    if t < NT:
                        g = t // TPG
                        dve.wait_ge(out_ps, t + 1)
                        if t >= 2:
                            dve.wait_ge(x2_done, t - 1)
                        dve.tensor_tensor(xm[:, t % 2, :], ps[:, 2 * (t % 2):2 * (t % 2) + 2, :].rearrange("p b c -> p (b c)"),
                                          late["gate1"][:, g, :], ALU.mult).then_inc(xm_done, 1)
                        dve.wait_ge(ssq_done, t + 1)
                        dve.tensor_scalar(ms[:, t:t + 1], ssq[:, t:t + 1], 1.0 / D_MODEL, EPS, ALU.mult, ALU.add).then_inc(ms_done, 1)
                        dve.wait_ge(rinv_done, t + 1)
                        if t >= 2:
                            dve.wait_ge(h2_out[t % 2], 16 * (t // 2))
                            dve.wait_ge(h2T_ps, t - 1)
                        dve.scalar_tensor_tensor(out=h2[:, t % 2, :], in0=xt[:, t, :], scalar=rinv[:, t:t + 1],
                                                 in1=late["mul2row"][:, g, :], op0=ALU.mult, op1=ALU.mult).then_inc(hm_done, 1)
                    if t >= 1:
                        softmax_tail(t - 1)
                st = Steps(dve, top_step)
                dve.wait_ge(probsT_ps, 1)
                st.do(dve.tensor_copy(work[:, 0, :], ps[0:NR, 0, :]))
                for r in range(CAP // 8):
                    got = slice(8 * r, 8 * r + 8)
                    st.do(dve.max(vals[:, got], work[:, r % 2, :]))
                    st.did(dve.max_index(idx[:, got], vals[:, got], work[:, r % 2, :]))
                    st.do(dve.match_replace(work[:, 1 - r % 2, :], vals[:, got], work[:, r % 2, :], -1.0))
                dve.wait_ge(sel_const, 8)
                st.do(dve.tensor_scalar(idxf[:, :], idx[:, :], first[:, 0:1], None, ALU.add))
                st.did(dve.tensor_tensor(spread[:, 0, :, :], bcast(vals[:, :], 1, GROUPS), own[:, :, :], ALU.mult))
                st.do(dve.tensor_tensor(spread[:, 1, :, :], bcast(idxf[:, :], 1, GROUPS), own[:, :, :], ALU.mult))
                assert st.n == 3 + 3 * (CAP // 8) + 1
                dve.wait_ge(pick_ps, 1)
                st.did(dve.tensor_copy(m["gates"][:, :], ps[:, 1, 0:NE]))
                st.did(dve.tensor_copy(m["token"][:, 0:NE], ps[:, 1, NE:2 * NE]))
                st.settle()


def phase_experts(nc, a, m, ps, x2_dram, h2_dram, raw, raw_in):
    NQ4 = QUARTERS
    NP_ = len(ORDER)
    PW = KD * FW
    PART_SLOTS, AHEAD = 3, 2
    pos = {piece: i for i, piece in enumerate(ORDER)}
    TURN_AT = {pos["u", 1]: 0, pos["u", 2]: 1, pos["u", 3]: 2, pos["d", 2]: 3}
    with ExitStack() as ctx:
        def sb(name, shape, dt=F32):
            return ctx.enter_context(nc.sbuf_tensor(name, shape, dt))

        def sem(name):
            return ctx.enter_context(nc.semaphore(name))

        whigh = [sb(f"whigh{i}", [P, PW], F32R) for i in range(PART_SLOTS)]
        wlow = [sb(f"wlow{i}", [P, PW], F32R) for i in range(PART_SLOTS)]
        tok_g = sb("tok_g", [P, 1], U32)
        tok_s = sb("tok_s", [P, 1], U32)
        gate = sb("gate_e", [P, 1])
        xe = sb("xe", [P, D_MODEL])
        xeT = sb("xeT", [P, 2, KD, P], F32R)
        sg = sb("sg", [P, 2, FW])
        hid = sb("hid", [P, 2, FW])
        hidT = sb("hidT", [P, 2, 2, FT, P], F32R)
        ye = sb("ye", [P, D_MODEL])

        high_done = sem("high_done")
        low_done = sem("low_done")
        piece_done = sem("piece_done")
        tok_ready = sem("tok_ready")
        xe_in = sem("xe_in")
        xeT_ps = sem("xeT_ps")
        xeT_high = sem("xeT_high")
        xeT_low = sem("xeT_low")
        silu_done = sem("silu_done_e")
        hid_done = sem("hid_done")
        hidT_ps = sem("hidT_ps")
        hidT_high = sem("hidT_high")
        hidT_low = sem("hidT_low")
        ye_done = sem("ye_done")
        gate_ready = sem("gate_ready")
        scattered = sem("scattered")
        gather_go = sem("gather_go")
        scatter_go = sem("scatter_go")
        ye_free = sem("ye_free")

        def loop(eng, body):
            with eng.Fori(0, NE - 1) as e:
                body(e, False)
            body(NE - 1, True)

        def multiplied(eng, e, p):
            eng.wait_ge(piece_done, e * NP_ + (NP_ + p + 1))

        with nc.Block() as block:

            @block.sync
            def _(sp):
                def body(e, last):
                    for p in range(RAW_SLOTS, NP_ if last else NP_ + RAW_SLOTS):
                        sp.wait_ge(low_done, e * NP_ + (p - RAW_SLOTS + 1))
                        load_piece(sp, a, raw, raw_in, e, p % NP_, ahead=p // NP_)

                loop(sp, body)

            @block.gpsimd
            def _(pool):
                def gather(e_tok, count):
                    pool.tensor_copy(tok_g[:, :], m["token"][:, e_tok]).then_inc(tok_ready, 1)
                    pool.wait_ge(tok_ready, count)
                    pool.sem_inc(gather_go, 1)
                    pool.indirect_dma_start(out=xe[:, :], out_offset=None, in_=h2_dram[:, :],
                                            in_offset=bass.IndirectOffsetOnAxis(ap=tok_g[:, 0:1], axis=0)).then_inc(xe_in, 16)

                prime(pool, ye_free)
                gather(slice(0, 1), 1)

                def body(e, last):
                    pool.wait_ge(xe_in, e * 16 + 16)
                    pool.wait_ge(xeT_ps, e * 2 + 2)
                    if not last:
                        gather(bass.ds(e + 1, 1), e * 2 + 2)
                    pool.tensor_copy(gate[:, :], m["gates"][:, bass.ds(e, 1)]).then_inc(gate_ready, 1)
                    pool.tensor_copy(tok_s[:, :], m["token"][:, bass.ds(e, 1)]).then_inc(tok_ready, 1)
                    pool.wait_ge(tok_ready, e * 2 + (2 if last else 3))
                    pool.wait_ge(ye_done, 1 + e + 1)
                    pool.sem_inc(scatter_go, 1)
                    pool.indirect_dma_start(out=x2_dram[:, :], out_offset=bass.IndirectOffsetOnAxis(ap=tok_s[:, 0:1], axis=0),
                                            in_=ye[:, :], in_offset=None, compute_op=ALU.add).then_inc(scattered, 16)
                    pool.wait_ge(scattered, e * 16 + 16)
                    pool.sem_inc(ye_free, 1)

                loop(pool, body)

            @block.tensor
            def _(pe):
                ident = m["ident"][:, :]
                pe.sem_inc(piece_done, NP_)
                prime(pe, hidT_ps)

                def turn_tokens(half, count_in, count_out):
                    pe.wait_ge(xe_in, count_in)
                    pe.wait_ge(xeT_low, count_out)
                    for k in range(4):
                        mm = pe.transpose(ps[:, 7, k * P:(k + 1) * P], xe[:, (4 * half + k) * P:(4 * half + k + 1) * P], ident)
                    mm.then_inc(xeT_ps, 1)

                def three(out, lhs, rhs, start, stop):
                    for i, (x, y) in enumerate(((0, 0), (0, 1), (1, 0))):
                        mm = pe.matmul(out, lhs[x], rhs[y], start=start and i == 0, stop=stop and i == 2)
                    return mm

                turn_tokens(0, 16, 0)
                turn_tokens(1, 16, 1)

                def body(e, last):
                    def turn_hidden(n):
                        pe.wait_ge(hid_done, 1 + e * NQ4 + n + 1)
                        pe.wait_ge(hidT_low, 1 + e * NQ4 + n)
                        for f in range(FT):
                            mm = pe.transpose(ps[:, 4, f * P:(f + 1) * P], hid[:, n % 2, f * P:(f + 1) * P], ident)
                        mm.then_inc(hidT_ps, 1)

                    for p, (kind, n) in enumerate(ORDER):
                        if kind in "gu":
                            if p in TURN_AT:
                                turn_hidden(TURN_AT[p])
                            pe.wait_ge(low_done, e * NP_ + (p + 1))
                            if p == 0:
                                pe.wait_ge(xeT_low, e * 2 + 2)
                            pe.wait_ge(silu_done if kind == "g" else hid_done, 1 + e * NQ4 + max(n - 1, 0))
                            w = [x.rearrange("p (k n) -> p k n", k=KD) for x in (whigh[p % PART_SLOTS][:, :], wlow[p % PART_SLOTS][:, :])]
                            for k in range(KD):
                                mm = three(ps[:, 2 * (n % 2) + (kind == "u"), :], [xeT[:, i, k, :] for i in range(2)],
                                           [w[i][:, k, :] for i in range(2)], k == 0, k == KD - 1)
                            mm.then_inc(piece_done, 1)
                        else:
                            pe.wait_ge(low_done, e * NP_ + (p + 1))
                            if n == 0:
                                pe.wait_ge(ye_done, 1 + e)
                            pe.wait_ge(hidT_low, 1 + e * NQ4 + n + 1)
                            w = [x.rearrange("p (k n) -> p k n", k=FT) for x in (whigh[p % PART_SLOTS][:, :], wlow[p % PART_SLOTS][:, :])]
                            for c in range(2):
                                if c == 1 and p in TURN_AT:
                                    turn_hidden(TURN_AT[p])
                                if c == 1 and n >= 2 and not last:
                                    turn_tokens(n - 2, e * 16 + 32, e * 2 + n)
                                for f in range(FT):
                                    mm = three(ps[:, 5 + c, :], [hidT[:, n % 2, i, f, :] for i in range(2)],
                                               [w[i][:, f, c * 512:(c + 1) * 512] for i in range(2)],
                                               n == 0 and f == 0, n == NQ4 - 1 and f == FT - 1)
                            mm.then_inc(piece_done, 1)

                loop(pe, body)

            @block.scalar
            def _(act):
                prime(act, silu_done)

                def tokens(half, count):
                    act.wait_ge(xeT_ps, count)
                    act.activation(xeT[:, 0, 4 * half:4 * half + 4, :], ps[:, 7, :], ACT.Copy).then_inc(xeT_high, 1)

                def high(e, p):
                    slot = p % NP_ % RAW_SLOTS
                    act.wait_ge(raw_in[slot], e * (16 * NP_ // RAW_SLOTS) + 16 * (p // RAW_SLOTS + 1))
                    multiplied(act, e, p - PART_SLOTS)
                    act.activation(whigh[p % PART_SLOTS][:, :], raw[slot], ACT.Copy).then_inc(high_done, 1)

                for p in range(AHEAD):
                    high(0, p)
                tokens(0, 1)
                tokens(1, 2)

                def body(e, last):
                    def silu(n):
                        multiplied(act, e, pos["g", n])
                        act.wait_ge(hid_done, 1 + e * NQ4 + max(n - 1, 0))
                        act.activation(sg[:, n % 2, :], ps[:, 2 * (n % 2), :], ACT.Silu).then_inc(silu_done, 1)

                    for p, (kind, n) in enumerate(ORDER):
                        if p in TURN_AT:
                            t = TURN_AT[p]
                            multiplied(act, e, pos["d", t - 2] if t >= 2 else pos["d", t + 2] - NP_)
                            act.wait_ge(hidT_ps, 1 + e * NQ4 + t + 1)
                            act.activation(hidT[:, t % 2, 0, :, :], ps[:, 4, :], ACT.Copy).then_inc(hidT_high, 1)
                        if not last or p + AHEAD < NP_:
                            high(e, p + AHEAD)
                        if kind == "g":
                            silu(n)
                        if kind == "d" and n >= 2 and not last:
                            multiplied(act, e, pos["u", 3])
                            tokens(n - 2, e * 2 + (n + 1))

                loop(act, body)

            @block.vector
            def _(dve):
                prime(dve, hid_done, ye_done, hidT_low)

                def tokens(half, count):
                    dve.wait_ge(xeT_high, count)
                    dve.tensor_tensor(xeT[:, 1, 4 * half:4 * half + 4, :].rearrange("p k c -> p (k c)"), ps[:, 7, :],
                                      xeT[:, 0, 4 * half:4 * half + 4, :].rearrange("p k c -> p (k c)").bitcast(F32),
                                      ALU.subtract).then_inc(xeT_low, 1)

                def low(e, p):
                    slot = p % NP_ % RAW_SLOTS
                    dve.wait_ge(high_done, e * NP_ + (p + 1))
                    dve.tensor_tensor(wlow[p % PART_SLOTS][:, :], raw[slot], whigh[p % PART_SLOTS][:, :].bitcast(F32),
                                      ALU.subtract).then_inc(low_done, 1)

                for p in range(AHEAD):
                    low(0, p)
                tokens(0, 1)
                tokens(1, 2)

                def body(e, last):
                    for p, (kind, n) in enumerate(ORDER):
                        if p in TURN_AT:
                            t = TURN_AT[p]
                            dve.wait_ge(hidT_high, e * NQ4 + t + 1)
                            dve.tensor_tensor(hidT[:, t % 2, 1, :, :].rearrange("p f c -> p (f c)"), ps[:, 4, :],
                                              hidT[:, t % 2, 0, :, :].rearrange("p f c -> p (f c)").bitcast(F32),
                                              ALU.subtract).then_inc(hidT_low, 1)
                        if not last or p + AHEAD < NP_:
                            low(e, p + AHEAD)
                        if kind == "u":
                            multiplied(dve, e, p)
                            dve.wait_ge(silu_done, 1 + e * NQ4 + n + 1)
                            dve.wait_ge(hidT_ps, 1 + e * NQ4 + max(n - 1, 0))
                            dve.tensor_tensor(hid[:, n % 2, :], sg[:, n % 2, :], ps[:, 2 * (n % 2) + 1, :],
                                              ALU.mult).then_inc(hid_done, 1)
                        if kind == "d" and n >= 2 and not last:
                            tokens(n - 2, e * 2 + (n + 1))
                    multiplied(dve, e, NP_ - 1)
                    dve.wait_ge(gate_ready, e + 1)
                    dve.wait_ge(ye_free, 1 + e)
                    dve.scalar_tensor_tensor(out=ye[:, :], in0=ps[:, 5:7, :].rearrange("p b c -> p (b c)"),
                                             scalar=gate[:, 0:1], in1=m["gate2"][:, :], op0=ALU.mult,
                                             op1=ALU.mult).then_inc(ye_done, 1)

                loop(dve, body)


def phase_finish(nc, a, m, x2_dram, y):
    with ExitStack() as ctx:
        def sb(name, shape, dt=F32):
            return ctx.enter_context(nc.sbuf_tensor(name, shape, dt))

        def sem(name):
            return ctx.enter_context(nc.semaphore(name))

        x3 = sb("x3", [P, NT, D_MODEL])
        fg = sb("fg", [P, D_MODEL])
        junk = sb("junk_f", [P, D_MODEL])
        ssq = sb("ssq_f", [P, NT])
        ms = sb("ms_f", [P, NT])
        rinv = sb("rinv_f", [P, NT])
        fg_in = sem("fg_in")
        x3_in = [sem(f"x3_in{t}") for t in range(NT)]
        ssq_done = sem("ssq_done_f")
        ms_done = sem("ms_done_f")
        rinv_done = sem("rinv_done_f")
        y_done = sem("y_done")
        y_out = sem("y_out")
        with nc.Block() as block:

            @block.sync
            def _(sp):
                sp.dma_start(fg[:, :], bass.AP(a["final_g"].tensor, 0, [[0, P], [1, D_MODEL]])).then_inc(fg_in, 16)
                x_v = x2_dram.rearrange("(t p) c -> t p c", p=P)
                y_v = y.rearrange("(t p) c -> t p c", p=P)
                for t in range(NT):
                    sp.dma_start(x3[:, t, :], x_v[t]).then_inc(x3_in[t], 16)
                for t in range(NT):
                    sp.wait_ge(y_done, t + 1)
                    sp.dma_start(y_v[t], x3[:, t, :]).then_inc(y_out, 16)
                sp.wait_ge(y_out, 16 * NT)

            @block.scalar
            def _(act):
                for t in range(NT):
                    act.wait_ge(x3_in[t], 16)
                    if t:
                        act.wait_ge(ssq_done, t)
                    act.activation(junk[:, :], x3[:, t, :], ACT.Square, accum_out=ssq[:, t:t + 1]).then_inc(ssq_done, 1)

            @block.gpsimd
            def _(pool):
                for t in range(NT):
                    pool.wait_ge(ms_done, t + 1)
                    pool.tensor_tensor(rinv[:, t:t + 1], ms[:, t:t + 1], m["neghalf"][:, 0:1], ALU.pow).then_inc(rinv_done, 1)

            @block.vector
            def _(dve):
                dve.wait_ge(fg_in, 16)
                for t in range(NT + 1):
                    if t < NT:
                        dve.wait_ge(ssq_done, t + 1)
                        dve.tensor_scalar(ms[:, t:t + 1], ssq[:, t:t + 1], 1.0 / D_MODEL, EPS, ALU.mult, ALU.add).then_inc(ms_done, 1)
                    if t >= 1:
                        v = t - 1
                        dve.wait_ge(rinv_done, v + 1)
                        dve.scalar_tensor_tensor(out=x3[:, v, :], in0=x3[:, v, :], scalar=rinv[:, v:v + 1], in1=fg[:, :],
                                                 op0=ALU.mult, op1=ALU.mult).then_inc(y_done, 1)


def build(nc, a, y):
    x2_dram = nc.dram_tensor("x2_dram", (TOK, D_MODEL), F32).ap()
    h2_dram = nc.dram_tensor("h2_dram", (TOK, D_MODEL), F32).ap()
    mod_dram = nc.dram_tensor("mod_dram", (GROUPS, 6 * D_MODEL), F32).ap()
    early_dram = nc.dram_tensor("early_dram", (EARLY_TILES * P, TOK), F32).ap()
    with ExitStack() as outer:
        ps = outer.enter_context(nc.psum_tensor("ps", [P, 8, 512], F32))
        m = {}
        for name, shape, dt in (("ident", [P, P], F32), ("neghalf", [P, 16], F32), ("gate2", [P, D_MODEL], F32),
                                ("gates", [P, NE], F32), ("token", [P, NE], U32)):
            m[name] = outer.enter_context(nc.sbuf_tensor(name, shape, dt))
        raw_in = [outer.enter_context(nc.semaphore(f"raw_in_e{i}")) for i in range(RAW_SLOTS)]
        x_in = outer.enter_context(nc.semaphore("x_in_r"))
        with ExitStack() as front:
            m.update(shared_buffers(nc, front, outer))
            raw = [m["oaT"][:, :, :].rearrange("p h t -> p (h t)"), m["obT"][:, :, :].rearrange("p h t -> p (h t)")]
            raw += [m["hT"][:, i * KD // 2:(i + 1) * KD // 2, :].rearrange("p k t -> p (k t)") for i in range(2)]
            with ExitStack() as ctx:
                first = first_buffers(nc, ctx)
                phase_prepare(nc, a, m, ps, first)
                phase_deltanet(nc, a, m, ps, early_dram, mod_dram, first)
            phase_attention(nc, a, m, ps, early_dram, x_in)
            with ExitStack() as ctx:
                late = late_buffers(nc, ctx)
                phase_merge(nc, a, m, ps, late, early_dram, mod_dram)
                phase_route(nc, a, m, ps, late, x2_dram, h2_dram, raw, raw_in, x_in)
        phase_experts(nc, a, m, ps, x2_dram, h2_dram, raw, raw_in)
        phase_finish(nc, a, m, x2_dram, y)


def kernel(**inputs):
    import numpy as np
    import concourse.bacc as bacc
    from concourse.bass_utils import run_bass_kernel_spmd as run

    nc = bacc.Bacc("TRN2", target_bir_lowering=False, num_devices=1)
    arrays = {n: np.ascontiguousarray(v) for n, v in inputs.items()
              if n not in ("x_prompt", "x_sample", "c_prompt", "c_sample", "rpb")}
    arrays["x"] = np.concatenate([inputs["x_prompt"][0], inputs["x_sample"][0]], axis=0)
    arrays["c"] = np.concatenate([inputs["c_prompt"], inputs["c_sample"]], axis=0)
    arrays["final_g"] = np.ascontiguousarray(inputs["final_g"]).reshape(1, D_MODEL)
    table = np.transpose(np.asarray(inputs["rpb"])[0], (0, 2, 1)).reshape(HB, RPB_C * RPB_R)
    arrays["rpb"] = np.stack([np.pad(table, ((0, 0), (RPB_FRONT + r, RPB_LEN + ROWS - RPB_FRONT - RPB_C * RPB_R - r)))
                              [:, :RPB_LEN] for r in range(ROWS)])
    a = {n: nc.dram_tensor(f"in_{n}", v.shape, mybir.dt.from_np(v.dtype), kind="ExternalInput").ap()
         for n, v in arrays.items()}
    y = nc.dram_tensor("out_y", (TOK, D_MODEL), F32, kind="ExternalOutput").ap()
    build(nc, a, y)
    r = run(nc, [{f"in_{n}": v for n, v in arrays.items()}], core_ids=[0])
    got = r.results[0]["out_y"]
    return got[None, :SEQ], got[None, SEQ:]
```
